# Optimizing a Trainium2 kernel written in Bass

```python
import math
import jax, jax.numpy as jnp
from jax import lax
import numpy as np

D_MODEL = 1024
BATCH = 1
SEQ = 2048
DEPTH = 1

ATTN_HEADS = 8
ATTN_KV_HEADS = 2
ATTN_HEAD_DIM = 64
Q_PER_KV = ATTN_HEADS // ATTN_KV_HEADS
WINDOW = 128
ATTN_BLOCK = WINDOW
ATTN_WIDTH = ATTN_HEADS * ATTN_HEAD_DIM
KV_WIDTH = ATTN_KV_HEADS * ATTN_HEAD_DIM
HGRN_HEADS = 4
HGRN_KEY_DIM = 128
HGRN_VAL_DIM = 128
HGRN_WIDTH = HGRN_HEADS * HGRN_VAL_DIM
HGRN_KEY_WIDTH = HGRN_HEADS * HGRN_KEY_DIM
HGRN_CHUNK = 32
MIX_WIDTH = ATTN_WIDTH + HGRN_WIDTH
IN_SPLITS = [ATTN_WIDTH, KV_WIDTH, KV_WIDTH, HGRN_KEY_WIDTH, HGRN_KEY_WIDTH, HGRN_WIDTH, HGRN_WIDTH]
IN_WIDTH = sum(IN_SPLITS)
N_GROUPS = 4
EXPERTS_PER_GROUP = 8
N_EXPERTS = N_GROUPS * EXPERTS_PER_GROUP
TOP_K = 2
EXPERT_FF = D_MODEL // 4

NORM_EPS = 1e-6
NEG_INF = -1e30


def rmsnorm(x, g):
    xf = x.astype(jnp.float32)
    y = xf * lax.rsqrt(jnp.mean(xf * xf, axis=-1, keepdims=True) + NORM_EPS)
    return (y * g.astype(jnp.float32)).astype(x.dtype)

def swa_sink_alibi(q, k, v, sinks):
    B, T, _ = q.shape
    NB = T // ATTN_BLOCK
    qb = q.reshape(B, NB, ATTN_BLOCK, ATTN_KV_HEADS, Q_PER_KV, ATTN_HEAD_DIM)
    pad = ((0, 0), (ATTN_BLOCK, 0), (0, 0))
    kp = jnp.pad(k, pad).reshape(B, NB + 1, ATTN_BLOCK, ATTN_KV_HEADS, ATTN_HEAD_DIM)
    vp = jnp.pad(v, pad).reshape(B, NB + 1, ATTN_BLOCK, ATTN_KV_HEADS, ATTN_HEAD_DIM)
    kb = jnp.concatenate([kp[:, :-1], kp[:, 1:]], axis=2)
    vb = jnp.concatenate([vp[:, :-1], vp[:, 1:]], axis=2)
    scale = 1.0 / math.sqrt(ATTN_HEAD_DIM)
    s = jnp.einsum('bnqgrd,bnkgd->bngrqk', qb, kb, preferred_element_type=jnp.float32) * scale
    qi = jnp.arange(ATTN_BLOCK)[:, None]
    kj = jnp.arange(2 * ATTN_BLOCK)[None, :]
    dist = qi + ATTN_BLOCK - kj
    in_win = (dist >= 0) & (dist < WINDOW)
    not_pad = (jnp.arange(NB)[:, None, None] > 0) | (kj >= ATTN_BLOCK)[None]
    valid = in_win[None] & not_pad
    slopes = jnp.exp2(-8.0 * (jnp.arange(ATTN_HEADS, dtype=jnp.float32) + 1.0) / ATTN_HEADS)
    slopes = slopes.reshape(ATTN_KV_HEADS, Q_PER_KV)[:, :, None, None]
    s = s - slopes * dist.astype(jnp.float32)
    s = jnp.where(valid[None, :, None, None], s, NEG_INF)
    sink = sinks.astype(jnp.float32).reshape(ATTN_KV_HEADS, Q_PER_KV)[:, :, None, None]
    m = jnp.maximum(jnp.max(s, axis=-1, keepdims=True), sink)
    p = jnp.exp(s - m)
    p = p / (jnp.sum(p, axis=-1, keepdims=True) + jnp.exp(sink - m))
    o = jnp.einsum('bngrqk,bnkgd->bnqgrd', p.astype(v.dtype), vb)
    return o.reshape(B, T, ATTN_WIDTH)

def hgrn2(q_raw, f_raw, i_raw, lb):
    B, T, _ = q_raw.shape
    NC = T // HGRN_CHUNK
    shp_k = (B, NC, HGRN_CHUNK, HGRN_HEADS, HGRN_KEY_DIM)
    q = jax.nn.silu(q_raw.astype(jnp.float32)).reshape(shp_k)
    lbf = lb.astype(jnp.float32)
    f = lbf + (1.0 - lbf) * jax.nn.sigmoid(f_raw.astype(jnp.float32))
    k = (1.0 - f).reshape(shp_k)
    logf = jnp.log(f).reshape(shp_k)
    v = i_raw.astype(jnp.float32).reshape(B, NC, HGRN_CHUNK, HGRN_HEADS, HGRN_VAL_DIM)
    b = jnp.cumsum(logf, axis=2)
    b_last = b[:, :, -1:]
    q_dec = q * jnp.exp(b)
    k_dec = k * jnp.exp(-b)
    k_end = k * jnp.exp(b_last - b)
    causal = jnp.tril(jnp.ones((HGRN_CHUNK, HGRN_CHUNK), dtype=bool))
    a = jnp.einsum('bnchk,bnshk->bnhcs', q_dec, k_dec)
    a = jnp.where(causal, a, 0.0)
    o_intra = jnp.einsum('bnhcs,bnshv->bnchv', a, v)

    def step(S, inp):
        qd, ke, vv, decay = inp
        o = jnp.einsum('bchk,bhkv->bchv', qd, S)
        S = S * decay[..., None] + jnp.einsum('bchk,bchv->bhkv', ke, vv)
        return S, o

    S0 = jnp.zeros((B, HGRN_HEADS, HGRN_KEY_DIM, HGRN_VAL_DIM), jnp.float32)
    xs = (jnp.moveaxis(q_dec, 1, 0), jnp.moveaxis(k_end, 1, 0), jnp.moveaxis(v, 1, 0),
          jnp.moveaxis(jnp.exp(b_last[:, :, 0]), 1, 0))
    _, o_inter = lax.scan(step, S0, xs)
    o = o_intra + jnp.moveaxis(o_inter, 0, 1)
    return o.reshape(B, T, HGRN_HEADS, HGRN_VAL_DIM).astype(q_raw.dtype)

def hierarchical_moe(h, w_rg, b_rg, w_re, b_re, w_gate, w_up, w_down):
    B, T, D = h.shape
    tok = h.reshape(-1, D)
    N = tok.shape[0]
    g_prob = jax.nn.softmax((tok @ w_rg + b_rg).astype(jnp.float32), axis=-1)
    g_w, g_idx = lax.top_k(g_prob, 1)
    e_logits = (tok @ w_re + b_re).astype(jnp.float32).reshape(N, N_GROUPS, EXPERTS_PER_GROUP)
    e_sel = e_logits[jnp.arange(N), g_idx[:, 0]]
    e_w, e_idx = lax.top_k(jax.nn.softmax(e_sel, axis=-1), TOP_K)
    e_w = e_w / jnp.sum(e_w, axis=-1, keepdims=True)
    weights = (g_w * e_w).astype(h.dtype)
    expert = (g_idx * EXPERTS_PER_GROUP + e_idx).reshape(-1)
    order = jnp.argsort(expert)
    inv = jnp.argsort(order)
    xs = tok[order // TOP_K]
    sizes = jnp.bincount(expert, length=N_EXPERTS).astype(jnp.int32)
    hg = lax.ragged_dot(xs, w_gate, sizes)
    hu = lax.ragged_dot(xs, w_up, sizes)
    ys = lax.ragged_dot(jax.nn.silu(hg) * hu, w_down, sizes)
    ys = ys[inv].reshape(N, TOP_K, D)
    out = jnp.einsum('nkd,nk->nd', ys, weights)
    return out.reshape(B, T, D)

def first_inputs(seed: int = 0) -> dict:
    key = jax.random.key(seed)
    ks = jax.random.split(key, 24)
    f32 = jnp.float32
    L, D = DEPTH, D_MODEL

    def nrm(k, shape, scale):
        return jax.random.normal(k, shape, f32) * scale

    return {
        "x": nrm(ks[0], (BATCH, SEQ, D), 1.0),
        "c": nrm(ks[1], (BATCH, D), 1.0),
        "ln1_pre": 1.0 + nrm(ks[2], (L, D), 0.02),
        "ln1_post": 1.0 + nrm(ks[3], (L, D), 0.02),
        "ln2_pre": 1.0 + nrm(ks[4], (L, D), 0.02),
        "ln2_post": 1.0 + nrm(ks[5], (L, D), 0.02),
        "w_ada": nrm(ks[6], (L, D, 6 * D), 0.25 * D ** -0.5),
        "b_ada": nrm(ks[7], (L, 6 * D), 0.01),
        "w_in": nrm(ks[8], (L, D, IN_WIDTH), D ** -0.5),
        "attn_sinks": nrm(ks[9], (L, ATTN_HEADS), 0.5),
        "attn_out_norm": 1.0 + nrm(ks[10], (L, ATTN_WIDTH), 0.02),
        "hgrn_lb": nrm(ks[11], (L + 1, HGRN_KEY_WIDTH), 0.1),
        "hgrn_out_norm": 1.0 + nrm(ks[12], (L, HGRN_WIDTH), 0.02),
        "w_out": nrm(ks[13], (L, MIX_WIDTH, D), MIX_WIDTH ** -0.5),
        "w_router_group": nrm(ks[14], (L, D, N_GROUPS), D ** -0.5),
        "b_router_group": nrm(ks[15], (L, N_GROUPS), 0.01),
        "w_router_expert": nrm(ks[16], (L, D, N_EXPERTS), D ** -0.5),
        "b_router_expert": nrm(ks[17], (L, N_EXPERTS), 0.01),
        "w_exp_gate": nrm(ks[18], (L, N_EXPERTS, D, EXPERT_FF), D ** -0.5),
        "w_exp_up": nrm(ks[19], (L, N_EXPERTS, D, EXPERT_FF), D ** -0.5),
        "w_exp_down": nrm(ks[20], (L, N_EXPERTS, EXPERT_FF, D), EXPERT_FF ** -0.5),
    }

def first_block(x, c, ln1_pre, ln1_post, ln2_pre, ln2_post, w_ada, b_ada, w_in, attn_sinks,
              attn_out_norm, hgrn_lb, hgrn_out_norm, w_out, w_router_group, b_router_group,
              w_router_expert, b_router_expert, w_exp_gate, w_exp_up, w_exp_down):
    B, T, D = x.shape
    lb_all = jnp.cumsum(jax.nn.softmax(hgrn_lb.astype(jnp.float32), axis=0), axis=0)
    offsets = list(np.cumsum(IN_SPLITS)[:-1])
    c_act = jax.nn.silu(c)
    for l in range(DEPTH):
        mod = (c_act @ w_ada[l] + b_ada[l])[:, None, :]
        sh1, sc1, ga1, sh2, sc2, ga2 = jnp.split(mod, 6, axis=-1)
        h = rmsnorm(x, ln1_pre[l]) * (1.0 + sc1) + sh1
        proj = h @ w_in[l]
        q_a, k_a, v_a, q_h, f_h, i_h, g_h = jnp.split(proj, offsets, axis=-1)
        attn = rmsnorm(swa_sink_alibi(q_a, k_a, v_a, attn_sinks[l]), attn_out_norm[l])
        hg = hgrn2(q_h, f_h, i_h, lb_all[l])
        hg = rmsnorm(hg, hgrn_out_norm[l].reshape(HGRN_HEADS, HGRN_VAL_DIM)).reshape(B, T, HGRN_WIDTH)
        hg = hg * jax.nn.silu(g_h)
        mix = jnp.concatenate([attn, hg], axis=-1) @ w_out[l]
        x = x + ga1 * rmsnorm(mix, ln1_post[l])
        h = rmsnorm(x, ln2_pre[l]) * (1.0 + sc2) + sh2
        y = hierarchical_moe(h, w_router_group[l], b_router_group[l], w_router_expert[l],
                             b_router_expert[l], w_exp_gate[l], w_exp_up[l], w_exp_down[l])
        x = x + ga2 * rmsnorm(y, ln2_post[l])
    return x


CHUNK = 64
N_LEFT_CHUNKS = 8
BAND = (N_LEFT_CHUNKS + 1) * CHUNK
A_HEADS = 8
A_HEAD_DIM = 64
A_WIDTH = A_HEADS * A_HEAD_DIM
REL_CLIP = 256
B_HEADS = 8
B_HEAD_DIM = 64
B_WIDTH = B_HEADS * B_HEAD_DIM
IDX_HEADS = 8
IDX_DIM = 32
TOPK_MAX = 256
Q_BLOCK = 128
ROPE_THETA = 500000.0
ROT_DIM_B = B_HEAD_DIM // 4
ROT_DIM_IDX = IDX_DIM // 4
EPS = 1e-6
NEG = -1e30

SPLIT_SIZES = (
    A_WIDTH, A_WIDTH, A_WIDTH, A_WIDTH,
    B_WIDTH, B_HEAD_DIM, B_HEAD_DIM, B_WIDTH,
    IDX_HEADS * IDX_DIM, IDX_DIM, IDX_HEADS,
    D_MODEL, D_MODEL,
)
IN_WIDTH_2 = sum(SPLIT_SIZES)


def rms_norm(x, g):
    xf = x.astype(jnp.float32)
    y = xf * lax.rsqrt(jnp.mean(xf * xf, axis=-1, keepdims=True) + EPS)
    return (y * g.astype(jnp.float32)).astype(x.dtype)

def partial_rope(x, rot_dim):
    S = x.shape[1]
    half = rot_dim // 2
    inv = ROPE_THETA ** (-jnp.arange(half, dtype=jnp.float32) / half)
    ang = jnp.arange(S, dtype=jnp.float32)[:, None] * inv[None, :]
    cos = jnp.cos(ang)[None, :, None, :].astype(x.dtype)
    sin = jnp.sin(ang)[None, :, None, :].astype(x.dtype)
    x1, x2, xp = x[..., :half], x[..., half:rot_dim], x[..., rot_dim:]
    return jnp.concatenate([x1 * cos - x2 * sin, x2 * cos + x1 * sin, xp], axis=-1)

def chunked_relpos_attention(q, k, v, rel_bias):
    B, S, H, d = q.shape
    n_chunks = S // CHUNK
    pad = N_LEFT_CHUNKS * CHUNK
    k_pad = jnp.pad(k, ((0, 0), (pad, 0), (0, 0), (0, 0)))
    v_pad = jnp.pad(v, ((0, 0), (pad, 0), (0, 0), (0, 0)))
    i = jnp.arange(CHUNK)[:, None]
    j = jnp.arange(BAND)[None, :]
    dist = pad + i - j
    bias = rel_bias.astype(jnp.float32)[:, jnp.clip(dist, -REL_CLIP, REL_CLIP) + REL_CLIP]
    scale = d ** -0.5

    def one_chunk(c):
        start = c * CHUNK
        qc = lax.dynamic_slice_in_dim(q, start, CHUNK, axis=1)
        kc = lax.dynamic_slice_in_dim(k_pad, start, BAND, axis=1)
        vc = lax.dynamic_slice_in_dim(v_pad, start, BAND, axis=1)
        s = jnp.einsum('bqhd,bkhd->bhqk', qc, kc).astype(jnp.float32) * scale + bias[None]
        valid = (start - pad + j) >= 0
        s = jnp.where(valid[None, None], s, NEG)
        p = jax.nn.softmax(s, axis=-1).astype(v.dtype)
        return jnp.einsum('bhqk,bkhd->bqhd', p, vc)

    out = lax.map(one_chunk, jnp.arange(n_chunks))
    return out.transpose(1, 0, 2, 3, 4).reshape(B, S, H * d)

def dsa_sparse_attention(q, k, v, iq, ik, iw):
    B, S, H, d = q.shape
    top_k = min(TOPK_MAX, S // 4)
    n_blocks = S // Q_BLOCK
    key_chunk = jnp.arange(S) // CHUNK
    scale = d ** -0.5
    gather = jax.vmap(lambda a, idx: a[idx])

    def one_block(blk):
        start = blk * Q_BLOCK
        qb = lax.dynamic_slice_in_dim(q, start, Q_BLOCK, axis=1)
        iqb = lax.dynamic_slice_in_dim(iq, start, Q_BLOCK, axis=1)
        iwb = lax.dynamic_slice_in_dim(iw, start, Q_BLOCK, axis=1)
        q_chunk = (start + jnp.arange(Q_BLOCK)) // CHUNK
        logits = jax.nn.relu(jnp.einsum('bqhd,bsd->bqhs', iqb, ik))
        score = jnp.einsum('bqhs,bqh->bqs', logits, iwb).astype(jnp.float32)
        adm = key_chunk[None, :] <= q_chunk[:, None]
        score = jnp.where(adm[None], score, -jnp.inf)
        _, idx = lax.top_k(score, top_k)
        sel_valid = (idx // CHUNK) <= q_chunk[None, :, None]
        ks = gather(k, idx)
        vs = gather(v, idx)
        s = jnp.einsum('bqhd,bqkd->bqhk', qb, ks).astype(jnp.float32) * scale
        s = jnp.where(sel_valid[:, :, None, :], s, NEG)
        p = jax.nn.softmax(s, axis=-1).astype(v.dtype)
        return jnp.einsum('bqhk,bqkd->bqhd', p, vs)

    out = lax.map(one_block, jnp.arange(n_blocks))
    return out.transpose(1, 0, 2, 3, 4).reshape(B, S, H * d)

def second_inputs(seed: int = 0) -> dict:
    key = jax.random.key(seed)
    ks = jax.random.split(key, 10)
    nrm = jax.random.normal
    return {
        "x": nrm(ks[0], (BATCH, SEQ, D_MODEL), jnp.float32),
        "norm_gain": 1.0 + 0.05 * nrm(ks[1], (DEPTH, D_MODEL), jnp.float32),
        "w_in": nrm(ks[2], (DEPTH, D_MODEL, IN_WIDTH_2), jnp.float32) * D_MODEL ** -0.5,
        "b_merge": 0.05 * nrm(ks[3], (DEPTH, 2, D_MODEL), jnp.float32),
        "rel_bias": 0.2 * nrm(ks[4], (DEPTH, A_HEADS, 2 * REL_CLIP + 1), jnp.float32),
        "w_branch_a": nrm(ks[5], (DEPTH, A_WIDTH, D_MODEL), jnp.float32) * A_WIDTH ** -0.5,
        "w_branch_b": nrm(ks[6], (DEPTH, B_WIDTH, D_MODEL), jnp.float32) * B_WIDTH ** -0.5,
        "w_out": nrm(ks[7], (DEPTH, D_MODEL, D_MODEL), jnp.float32) * D_MODEL ** -0.5,
        "final_norm_gain": 1.0 + 0.05 * nrm(ks[8], (D_MODEL,), jnp.float32),
    }

def second_block(x, norm_gain, w_in, b_merge, rel_bias, w_branch_a, w_branch_b, w_out, final_norm_gain):
    B, S, _ = x.shape
    offsets = [int(o) for o in np.cumsum(SPLIT_SIZES)[:-1]]
    h = x
    for layer in range(DEPTH):
        xn = rms_norm(h, norm_gain[layer])
        proj = xn @ w_in[layer]
        qa, ka, va, ga, qb, kb, vb, gb, iq, ik, iw, za, zb = jnp.split(proj, offsets, axis=-1)
        qa = qa.reshape(B, S, A_HEADS, A_HEAD_DIM)
        ka = ka.reshape(B, S, A_HEADS, A_HEAD_DIM)
        va = va.reshape(B, S, A_HEADS, A_HEAD_DIM)
        ya = chunked_relpos_attention(qa, ka, va, rel_bias[layer]) * jax.nn.silu(ga)
        qb = partial_rope(qb.reshape(B, S, B_HEADS, B_HEAD_DIM), ROT_DIM_B)
        kb = partial_rope(kb[:, :, None, :], ROT_DIM_B)[:, :, 0]
        iq = partial_rope(iq.reshape(B, S, IDX_HEADS, IDX_DIM), ROT_DIM_IDX)
        ik = partial_rope(ik[:, :, None, :], ROT_DIM_IDX)[:, :, 0]
        iw = iw * (IDX_HEADS ** -0.5 * IDX_DIM ** -0.5)
        yb = dsa_sparse_attention(qb, kb, vb, iq, ik, iw) * jax.nn.silu(gb)
        gate_a = jax.nn.sigmoid(za + b_merge[layer, 0])
        gate_b = jax.nn.sigmoid(zb + b_merge[layer, 1])
        merged = gate_a * (ya @ w_branch_a[layer]) + gate_b * (yb @ w_branch_b[layer])
        h = h + merged @ w_out[layer]
    return rms_norm(h, final_norm_gain)


def setup_inputs(seed=0):
    out = dict(first_inputs(seed))
    for name, value in second_inputs(seed + 1).items():
        if name != "x":
            out[name + "_2"] = value
    return out


def reference(
    x, c, ln1_pre, ln1_post, ln2_pre, ln2_post, w_ada, b_ada, w_in, attn_sinks, attn_out_norm,
    hgrn_lb, hgrn_out_norm, w_out, w_router_group, b_router_group, w_router_expert,
    b_router_expert, w_exp_gate, w_exp_up, w_exp_down, norm_gain_2, w_in_2, b_merge_2,
    rel_bias_2, w_branch_a_2, w_branch_b_2, w_out_2, final_norm_gain_2,
):
    x = first_block(
        x, c, ln1_pre, ln1_post, ln2_pre, ln2_post, w_ada, b_ada, w_in, attn_sinks,
        attn_out_norm, hgrn_lb, hgrn_out_norm, w_out, w_router_group, b_router_group,
        w_router_expert, b_router_expert, w_exp_gate, w_exp_up, w_exp_down,
    )
    return second_block(
        x, norm_gain_2, w_in_2, b_merge_2, rel_bias_2, w_branch_a_2, w_branch_b_2, w_out_2,
        final_norm_gain_2,
    )


_drawn_inputs = setup_inputs


def setup_inputs(seed=0):
    import zlib

    import numpy as np

    out = dict(_drawn_inputs(seed))
    spreads = {}
    factors = {'ln1_pre': 4.233,
     'ln1_post': 4.482,
     'ln2_post': 8.0,
     'attn_sinks': 3.5,
     'attn_out_norm': 5.726,
     'hgrn_lb': 8.0,
     'hgrn_out_norm': 7.426,
     'b_router_group': 8.0,
     'b_router_expert': 5.827,
     'norm_gain_2': 5.774,
     'b_merge_2': 8.0,
     'rel_bias_2': 8.0}
    for name, (base, spread) in spreads.items():
        noise = np.random.default_rng([zlib.crc32(name.encode()), seed]).standard_normal(out[name].shape)
        drawn = base * np.exp(spread * noise) if base else spread * noise
        out[name] = __import__('jax').numpy.asarray(drawn.astype(out[name].dtype))
    for name, factor in factors.items():
        out[name] = (out[name] * factor).astype(out[name].dtype)
    return out
```

```python
import math
from contextlib import ExitStack, contextmanager

import numpy as np

import concourse.bass as bass
from concourse import mybir

F32 = mybir.dt.float32
I32 = mybir.dt.int32
U32 = mybir.dt.uint32
ALU = mybir.AluOpType
ACT = mybir.ActivationFunctionType
AX = mybir.AxisListType

P = 128
T = 2048
D = 1024
KD = D // P
NB = T // P
EPS = 1e-6
NEG = -1e30
GONE = -3e38

AH, AKV, HD = 8, 2, 64
AW, KVW = AH * HD, AKV * HD
HH, HK = 4, 128
HW_ = HH * HK
CH = 32
NCH = P // CH
IN1 = AW + 2 * KVW + 4 * HW_
NG, EPG, NE, FF = 4, 8, 32, 256
NT = 2 * NE
CW, LEFT = 64, 8
BAND = LEFT * CW + P
CLIP = 256
BH = 8
IH, ID = 8, 32
TOPK = 256
ROPE = 24
W2 = dict(qa=0, ka=512, va=1024, ga=1536, qb=2048, kb=2560, vb=2624, gb=2688, iq=3200, ik=3456, iw=3488, za=3496, zb=4520)
IN2 = 5544

C_ID, C_TRI, C_AFTER, C_BEFORE, C_ONES, C_CHUNK = range(6)


def shape_constants():
    r = np.arange(P)
    same = (r[:, None] // CH) == (r[None, :] // CH)
    sq = np.zeros((P, 6, P), np.float32)
    sq[:, C_ID] = np.eye(P)
    sq[:, C_TRI] = same & (r[:, None] <= r[None, :])
    sq[:, C_AFTER] = same & (r[:, None] > r[None, :])
    sq[:, C_BEFORE] = r[:, None] < r[None, :]
    sq[:, C_ONES] = 1.0
    sq[:, C_CHUNK, 0:NCH] = (r[:, None] // CH) == np.arange(NCH)[None, :]
    dist = r[:, None] + P - np.arange(2 * P)[None, :]
    slopes = np.exp2(-8.0 * (np.arange(AH) + 1.0) / AH)
    alibi = np.where(((dist >= 0) & (dist < P))[:, None, :], -slopes[None, :, None] * dist[:, None, :], NEG).astype(np.float32)
    padflag = np.zeros((1, LEFT * CW + T), np.float32)
    padflag[:, 0:LEFT * CW] = 1.0
    pos = np.arange(T, dtype=np.float32)[:, None]

    def angles(half):
        inv = np.float32(500000.0) ** (-np.arange(half, dtype=np.float32) / np.float32(half))
        a = pos * inv.astype(np.float32)[None, :]
        return [np.cos(a), np.sin(a)]

    rope = np.concatenate(angles(8) + angles(4), axis=1).astype(np.float32)
    j = np.arange(BAND)[None, :]
    lo = r[:, None] < CW
    band = np.where((lo & (j >= BAND - CW)) | (~lo & (j < CW)), NEG, 0.0).astype(np.float32)
    j = np.arange(4 * P)
    causal = np.stack([np.where(j[None, :] < P * m + np.where(r < CW, CW, P)[:, None], 0.0, NEG) for m in range(4)], axis=0).astype(np.float32)
    ecol = np.zeros((P, NE * 4 + 64), np.float32)
    ecol[:, 0:NE] = np.arange(NE)
    ecol[:, NE:2 * NE] = np.arange(NE) * P
    ecol[:, 2 * NE:2 * NE + 15] = P * np.arange(1, 16)
    ecol[:, 3 * NE:3 * NE + NE] = np.arange(NE)
    ecol[:, 4 * NE:4 * NE + NG] = np.arange(NG)
    return dict(c_square=sq, c_alibi=alibi, c_padflag=padflag, c_rope=rope, c_band=band, c_causal=causal, c_expert=ecol)


@contextmanager
def semaphores(nc, stage):
    held = []

    def sem(name):
        held.append(nc.alloc_semaphore(f"{stage}_{name}"))
        return held[-1]
    yield sem
    nc.clear_and_free_semaphores(held)
    nc.all_engine_barrier()


def pairs(eng, n, body):
    with eng.Fori(0, n // 2 - 1) as j:
        for u in range(2):
            body(2 * j + u, u, j + 1, False)
    body(n - 2, 0, n // 2, False)
    body(n - 1, 1, n // 2, True)


def settle(g, eng):
    eng.sem_inc(g.tick, 1)


class Net:
    pass


def stage_modulation(nc, g):
    with ExitStack() as x:
        sb = lambda n, s, d=F32: x.enter_context(nc.sbuf_tensor(n, s, d))
        sem = x.enter_context(semaphores(nc, "modulation"))
        wa = sb("ada_w", [P, 2, KD, 512])
        mod = sb("ada_mod", [P, 48])
        bada = sb("ada_b", [P, 48])
        ccol = sb("ada_c", [P, 3, KD])
        lns = sb("ada_lns", [P, 4, KD])
        gcol = sb("ada_gcol", [P, 2, KD])
        diag = sb("ada_diag", [P, 2, KD, P])
        pm = x.enter_context(nc.psum_tensor("ada_pm", [P, 2, 512], F32))
        pg = x.enter_context(nc.psum_tensor("ada_pg", [P, 4, 512], F32))
        small, wload, sig, cact, mm, used, modded, diags, grows, done = map(
            sem, "small_loaded ada_w_loaded c_sigmoid c_silu mod_product mod_added mod_done diag_ready gate_rows ada_done".split())
        wload = [wload, sem("ada_w_loaded_odd")]
        NCOL = 6 * D // 512

        with nc.Block() as block:
            @block.sync
            def _(sp):
                sp.dma_start(ccol[:, 0, :], g.c[0, :].rearrange("(k p) -> p k", p=P), allow_slow_non_contiguous=True).then_inc(small, 16)
                for n, v in enumerate((g.ln1_pre, g.ln2_pre, g.ln1_post, g.ln2_post)):
                    sp.dma_start(lns[:, n, :], v[0, :].rearrange("(k p) -> p k", p=P), allow_slow_non_contiguous=True).then_inc(small, 16)
                sp.dma_start(bada[:], g.b_ada[0, :].rearrange("(k p) -> p k", p=P), allow_slow_non_contiguous=True).then_inc(small, 16)
                sp.dma_start(g.square[:], g.c_square[:, :, :]).then_inc(small, 16)
                with sp.Fori(0, NCOL // 2) as j:
                    for u in range(2):
                        i = 2 * j + u
                        sp.wait_ge(used, i + 1)
                        sp.dma_start(wa[:, u, :, :], g.w_ada[0].rearrange("(k p) n -> p k n", p=P)[:, :, bass.ds(i * 512, 512)]).then_inc(wload[u], 16)

            @block.scalar
            def _(act):
                act.dma_start(g.win1[:], g.w_in[0].rearrange("(k p) n -> p k n", p=P)).then_inc(g.win1_loaded, 16)
                act.wait_ge(small, 16 * 7)
                nc.scalar.activation(ccol[:, 1, :], ccol[:, 0, :], ACT.Sigmoid).then_inc(sig, 1)

            @block.tensor
            def _(pe):
                pe.wait_ge(cact, 1)
                with pe.Fori(0, NCOL // 2) as j:
                    for u in range(2):
                        i = 2 * j + u
                        pe.wait_ge(wload[u], 16 * (j + 1))
                        pe.wait_ge(used, i + 1)
                        for n in range(4):
                            for k in range(KD):
                                last = nc.tensor.matmul(pm[:, u, n:n + 1], wa[:, u, k, n * P:(n + 1) * P], ccol[:, 2, k:k + 1],
                                                        start=(k == 0), stop=(k == KD - 1))
                        last.then_inc(mm, 1)
                pe.wait_ge(diags, 1)
                for h in range(2):
                    for k in range(KD):
                        last = nc.tensor.matmul(pg[:, 2 * h + k // 4, (k % 4) * P:(k % 4 + 1) * P], g.square[:, C_ONES, :], diag[:, h, k, :],
                                                start=True, stop=True)
                last.then_inc(grows, 1)

            @block.vector
            def _(v):
                v.sem_inc(used, 2)
                v.wait_ge(small, 16 * 7)
                v.wait_ge(sig, 1)
                nc.vector.tensor_tensor(ccol[:, 2, :], ccol[:, 0, :], ccol[:, 1, :], ALU.mult).then_inc(cact, 1)
                with v.Fori(0, NCOL // 2) as j:
                    for u in range(2):
                        i = 2 * j + u
                        v.wait_ge(mm, i + 1)
                        nc.vector.tensor_tensor(mod[:, bass.ds(4 * i, 4)], pm[:, u, 0:4], bada[:, bass.ds(4 * i, 4)], ALU.add).then_inc(used, 1)
                v.drain()
                for n in range(2):
                    nc.vector.scalar_tensor_tensor(out=g.scale[:, n, :], in0=mod[:, 24 * n + 8:24 * n + 16], scalar=1.0, in1=lns[:, n, :],
                                                   op0=ALU.add, op1=ALU.mult)
                    nc.vector.tensor_copy(g.shift[:, n, :], mod[:, 24 * n:24 * n + 8])
                    nc.vector.tensor_tensor(gcol[:, n, :], mod[:, 24 * n + 16:24 * n + 24], lns[:, 2 + n, :], ALU.mult)
                v.drain()
                for n in range(2):
                    for k in range(KD):
                        last = nc.vector.tensor_scalar(diag[:, n, k, :], g.square[:, C_ID, :], gcol[:, n, k:k + 1], None, ALU.mult)
                last.then_inc(diags, 1)
                v.wait_ge(grows, 1)
                for n in range(2):
                    nc.vector.tensor_copy(g.gate[:, n, :].rearrange("p (a b) -> p a b", a=2), pg[:, 2 * n:2 * n + 2, :])


def stage_project1(nc, g):
    with ExitStack() as x:
        sb = lambda n, s, d=F32: x.enter_context(nc.sbuf_tensor(n, s, d))
        sem = x.enter_context(semaphores(nc, "project1"))
        xb = sb("p1_x", [P, 2, D])
        junk = sb("p1_junk", [P, D])
        xn = sb("p1_xn", [P, D])
        hT = sb("p1_hT", [P, 2, KD, P])
        st = sb("p1_stat", [P, 2, 4])
        qkT = sb("p1_qkT", [P, 2, 5, P])
        va = sb("p1_va", [P, 2, P])
        hx = sb("p1_hgrn", [P, 2, 5, HW_])
        sg = sb("p1_sig", [P, 3, HW_])
        fb = sb("p1_f", [P, HW_])
        lbr = sb("p1_lbrows", [P, 2, HW_])
        lb = sb("p1_lb", [P, 3, HW_])
        zero = sb("p1_zero", [P, 2 * P])
        half = sb("p1_half", [P, 1])
        pt = x.enter_context(nc.psum_tensor("p1_pt", [P, 2, 512], F32))
        pg = x.enter_context(nc.psum_tensor("p1_pg", [P, 6, 512], F32))
        (x_loaded, x_free, sumsq, msd, rs, xn_ready, xn_free, t_done, hT_ready, hT_free, g_done, act_evac, dve_evac, sf_ready, sfree,
         f_ready, st_act, st_dve, stored, padded, lb_loaded, lb_exp, lb_ready, logs) = map(sem, (
             "x_loaded x_free sumsq mean_square rs_ready xn_ready xn_free x_transposed hT_ready hT_free group_done act_evac dve_evac "
             "sig_ready sig_free f_ready staged_act staged_dve stored padded lb_loaded lb_exp lb_ready logs_done").split())

        x_loaded = [x_loaded, sem("x_loaded_odd")]
        with nc.Block() as block:
            @block.sync
            def _(sp):
                for r in range(2):
                    sp.dma_start(lbr[:, r, :], g.hgrn_lb[r:r + 1, :].to_broadcast([P, HW_])).then_inc(lb_loaded, 16)

                def load(i, u, uses, last):
                    sp.wait_ge(x_free, i + 1)
                    sp.dma_start(xb[:, u, :], g.x[0, bass.ds(i * P, P), :]).then_inc(x_loaded[u], 16)
                pairs(sp, NB, load)

            @block.gpsimd
            def _(pool):
                nc.gpsimd.memset(half[:], -0.5).then_inc(padded, 1)
                nc.gpsimd.memset(zero[:], 0.0).then_inc(padded, 1)
                pool.wait_ge(padded, 2)
                pool.dma_start(g.kaT[:, 0:P], zero[:, 0:P]).then_inc(stored, 16)
                pool.dma_start(g.va[0:P, :], zero[:, 0:P]).then_inc(stored, 16)

                def rsqrt(i, u):
                    pool.wait_ge(msd, i + 1)
                    nc.gpsimd.tensor_tensor(st[:, u, 2:3], st[:, u, 1:2], half[:], ALU.pow).then_inc(rs, 1)

                def step(i, u, uses, last):
                    if not last:
                        rsqrt(i + 1, 1 - u)
                    pool.wait_ge(stored, 16 * (2 + 4 * i))
                    pool.sem_inc(sfree, 1)
                    pool.wait_ge(st_act, i + 1)
                    pool.wait_ge(st_dve, i + 1)
                    settle(g, pool)
                    pool.dma_start(g.qaT.rearrange("(c p) t -> p c t", p=P)[:, :, bass.ds(i * P, P)], qkT[:, u, 0:4, :]).then_inc(stored, 16)
                    pool.dma_start(g.kaT[:, bass.ds((i + 1) * P, P)], qkT[:, u, 4, :]).then_inc(stored, 16)
                    pool.dma_start(g.va[bass.ds((i + 1) * P, P), :], va[:, u, :]).then_inc(stored, 16)
                    pool.dma_start(g.hg5[bass.ds(i * P, P), :, :], hx[:, u, :, :]).then_inc(stored, 16)
                rsqrt(0, 0)
                pairs(pool, NB, step)
                pool.wait_ge(stored, 16 * (2 + 4 * NB))

            @block.scalar
            def _(act):
                act.sem_inc(act_evac, 5)
                act.wait_ge(lb_loaded, 32)
                act.wait_ge(lb_ready, 1)
                for r in range(2):
                    last = nc.scalar.activation(lb[:, r, :], lb[:, r, :], ACT.Exp)
                last.then_inc(lb_exp, 1)

                def norm(i, u, uses):
                    act.wait_ge(x_loaded[u], 16 * uses)
                    nc.scalar.activation(junk[:], xb[:, u, :], ACT.Square, accum_out=st[:, u, 0:1]).then_inc(sumsq, 1)
                    act.wait_ge(rs, i + 1)
                    act.wait_ge(xn_free, i + 1)
                    nc.scalar.activation(xn[:], xb[:, u, :], ACT.Copy, scale=st[:, u, 2:3]).then_inc(xn_ready, 1)

                def step(i, u, uses, last):
                    if not last:
                        norm(i + 1, 1 - u, uses + u)
                    act.wait_ge(g_done, 6 * i + 1)
                    act.wait_ge(sfree, i + 1)
                    nc.scalar.activation(qkT[:, u, 0:4, :], pg[:, 0, :].rearrange("p (c t) -> p c t", c=4), ACT.Copy, scale=HD ** -0.5).then_inc(act_evac, 1)
                    act.wait_ge(g_done, 6 * i + 2)
                    nc.scalar.activation(qkT[:, u, 4, :], pg[:, 1, 0:P], ACT.Copy)
                    nc.scalar.activation(va[:, u, :], pg[:, 1, P:2 * P], ACT.Copy).then_inc(act_evac, 1)
                    for n, q in enumerate((2, 3, 5)):
                        act.wait_ge(g_done, 6 * i + q + 1)
                        nc.scalar.activation(sg[:, n, :], pg[:, q, :], ACT.Sigmoid).then_inc(act_evac, 1)
                    act.wait_ge(f_ready, i + 1)
                    nc.scalar.activation(hx[:, u, 2, :], fb[:], ACT.Ln).then_inc(st_act, 1)
                norm(0, 0, 1)
                pairs(act, NB, step)

            @block.tensor
            def _(pe):
                pe.wait_ge(g.win1_loaded, 16)

                def turn(i, u):
                    pe.wait_ge(xn_ready, i + 1)
                    pe.wait_ge(hT_ready, i + 1)
                    for k in range(KD):
                        last = nc.tensor.transpose(pt[:, k // 4, (k % 4) * P:(k % 4 + 1) * P], xn[:, k * P:(k + 1) * P], g.square[:, C_ID, :])
                    last.then_inc(t_done, 1)

                def step(i, u, uses, last):
                    pe.wait_ge(hT_ready, i + 2)
                    for q in range(6):
                        pe.wait_ge(act_evac, 5 * i + (1, 2, 3, 4, 4, 5)[q])
                        if q in (2, 4, 5):
                            pe.wait_ge(dve_evac, 3 * i + {2: 1, 4: 2, 5: 3}[q])
                        if q == 0:
                            for c in range(4):
                                for k in range(KD):
                                    mm = nc.tensor.matmul(pg[:, 0, c * P:(c + 1) * P], g.win1[:, k, c * P:(c + 1) * P], hT[:, u, k, :],
                                                          start=(k == 0), stop=(k == KD - 1))
                        elif q == 1:
                            for k in range(KD):
                                nc.tensor.matmul(pg[:, 1, 0:P], g.win1[:, k, AW:AW + P], hT[:, u, k, :], start=(k == 0), stop=(k == KD - 1))
                            for k in range(KD):
                                mm = nc.tensor.matmul(pg[:, 1, P:2 * P], hT[:, u, k, :], g.win1[:, k, AW + P:AW + 2 * P],
                                                      start=(k == 0), stop=(k == KD - 1))
                        else:
                            at = AW + 2 * KVW + (q - 2) * HW_
                            for k in range(KD):
                                mm = nc.tensor.matmul(pg[:, q, :], hT[:, u, k, :], g.win1[:, k, at:at + HW_], start=(k == 0), stop=(k == KD - 1))
                        mm.then_inc(g_done, 1)
                        if q == 2 and not last:
                            turn(i + 1, 1 - u)
                turn(0, 0)
                pairs(pe, NB, step)

            @block.vector
            def _(v):
                v.sem_inc(x_free, 2)
                v.sem_inc(xn_free, 1)
                v.sem_inc(hT_ready, 1)
                v.sem_inc(dve_evac, 3)
                v.sem_inc(sfree, 1)
                v.wait_ge(lb_loaded, 32)
                nc.vector.tensor_tensor(lb[:, 2, :], lbr[:, 0, :], lbr[:, 1, :], ALU.max)
                v.drain()
                nc.vector.tensor_tensor(lb[:, 0, :], lbr[:, 0, :], lb[:, 2, :], ALU.subtract)
                nc.vector.tensor_tensor(lb[:, 1, :], lbr[:, 1, :], lb[:, 2, :], ALU.subtract).then_inc(lb_ready, 1)
                v.wait_ge(lb_exp, 1)
                nc.vector.tensor_tensor(lb[:, 1, :], lb[:, 0, :], lb[:, 1, :], ALU.add)
                v.drain()
                nc.vector.reciprocal(lb[:, 2, :], lb[:, 1, :])
                v.drain()
                nc.vector.tensor_tensor(lb[:, 0, :], lb[:, 0, :], lb[:, 2, :], ALU.mult)
                v.drain()
                nc.vector.tensor_scalar(lb[:, 1, :], lb[:, 0, :], -1.0, 1.0, ALU.mult, ALU.add)

                def norm(i, u):
                    v.wait_ge(sumsq, i + 1)
                    nc.vector.tensor_scalar(st[:, u, 1:2], st[:, u, 0:1], 1.0 / D, EPS, ALU.mult, ALU.add).then_inc(msd, 1)
                    v.wait_ge(xn_ready, i + 1)
                    v.sem_inc(x_free, 1)
                    v.wait_ge(t_done, i + 1)
                    v.sem_inc(xn_free, 1)
                    for k in range(KD):
                        last = nc.vector.tensor_scalar(hT[:, u, k, :], pt[:, k // 4, (k % 4) * P:(k % 4 + 1) * P],
                                                       g.scale[:, 0, k:k + 1], g.shift[:, 0, k:k + 1], ALU.mult, ALU.add)
                    last.then_inc(hT_ready, 1)

                def step(i, u, uses, last):
                    if not last:
                        norm(i + 1, 1 - u)
                    v.wait_ge(sfree, i + 1)
                    v.wait_ge(act_evac, 5 * i + 5 + 3)
                    nc.vector.tensor_tensor(hx[:, u, 0, :], pg[:, 2, :], sg[:, 0, :], ALU.mult).then_inc(dve_evac, 1)
                    v.wait_ge(act_evac, 5 * i + 5 + 4)
                    nc.vector.tensor_tensor(fb[:], sg[:, 1, :], lb[:, 1, :], ALU.mult)
                    v.wait_ge(g_done, 6 * i + 5)
                    nc.vector.tensor_copy(hx[:, u, 3, :], pg[:, 4, :]).then_inc(dve_evac, 1)
                    v.drain()
                    nc.vector.tensor_tensor(fb[:], fb[:], lb[:, 0, :], ALU.add).then_inc(f_ready, 1)
                    v.drain()
                    nc.vector.tensor_scalar(hx[:, u, 1, :], fb[:], -1.0, 1.0, ALU.mult, ALU.add)
                    v.wait_ge(act_evac, 5 * i + 5 + 5)
                    nc.vector.tensor_tensor(hx[:, u, 4, :], pg[:, 5, :], sg[:, 2, :], ALU.mult).then_inc(dve_evac, 1)
                    v.drain().then_inc(st_dve, 1)
                norm(0, 0)
                pairs(v, NB, step)


def overlapped(eng, n, step):
    step((0, 0, 1), None)
    with eng.Fori(0, n // 2 - 1) as j:
        step((2 * j + 1, 1, j + 1), (2 * j, 0, j + 1))
        step((2 * j + 2, 0, j + 2), (2 * j + 1, 1, j + 1))
    step((n - 1, 1, n // 2), (n - 2, 0, n // 2))
    step(None, (n - 1, 1, n // 2))


def stage_mix(nc, g):
    with ExitStack() as x:
        sb = lambda n, s, d=F32: x.enter_context(nc.sbuf_tensor(n, s, d))
        sem = x.enter_context(semaphores(nc, "mix"))
        wout = sb("m_wout", [P, KD, D])
        wr = sb("m_wr", [P, KD, NG + NE])
        br = sb("m_br", [P, NG + NE])
        alibi = sb("m_alibi", [P, AH, 2 * P])
        sinks = sb("m_sinks", [P, AH])
        aon = sb("m_aon", [P, AW])
        hon = sb("m_hon", [P, HW_])
        qT = sb("m_qT", [HD + 1, 2, AH, P])
        kT = sb("m_kT", [HD + 1, 2, AKV, 2 * P])
        vw = sb("m_vw", [P, 2, 2, KVW])
        hx = sb("m_hx", [P, 2, 5, HW_])
        xb = sb("m_xb", [P, 2, D])
        S = sb("m_scores", [P, 2, 2 * P])
        Pb = sb("m_probs", [P, 2, 2 * P])
        PT = sb("m_probsT", [P, 2, 2 * P])
        E = sb("m_exps", [P, 3, HW_])
        dec = sb("m_decay", [P, HH * NCH])
        Q = sb("m_decayed", [P, 3, HW_])
        QT = sb("m_decayedT", [P, 2, HW_])
        A = sb("m_aT", [P, HW_])
        St = sb("m_state", [P, 2, NCH, HW_])
        at = sb("m_att", [P, AW])
        junk = sb("m_junk", [P, D])
        mixin = sb("m_mixin", [P, D])
        mixT = sb("m_mixT", [P, KD, P])
        mo = sb("m_mo", [P, D])
        x1 = sb("m_x1", [P, 2, D])
        xn = sb("m_xn", [P, 2, D])
        h2T = sb("m_h2T", [P, KD, P])
        sm = sb("m_small", [P, 16, AH])
        half = sb("m_half", [P, AH])
        bank = [x.enter_context(nc.psum_tensor(f"m_bank{b}", [P, 512], F32)) for b in range(8)]
        B0, B1, BS0, BS1, BPT, BO, X0, W0 = bank
        MX, NM, L, ES, RL, SSA, MSA, RSA, SSH, MSH, RSH, SST, MST, RST, SSX, RSX = range(16)
        names = ("w_loaded cum_done exps_done exps_read decayed qk_done s_read nm_ready p_ready tp_done pt_read pv_done "
                 "dT_done dT_read a_done a_read kv_done kv_read oh_done oh_read sink_arg sink_exp at_ready ssa_ready msa_ready rsa_ready "
                 "ssh_ready msh_ready rsh_ready mixin_ready mixT_done mixT_read wo_done wo_read sst_ready mst_ready rst_ready x1_ready "
                 "ssx_ready msx_ready rsx_ready xn_ready h2_done h2_read logit_done logit_read stored half_ready loads_free neg_ready").split()
        s = {n: sem(n) for n in names}
        loaded = [sem("block_loaded_even"), sem("block_loaded_odd")]
        gelem = lambda ap, n: ap.rearrange("p (h d) -> p h d", h=n)

        with nc.Block() as block:
            @block.sync
            def _(sp):
                sp.dma_start(wout[:], g.w_out[0].rearrange("(k p) n -> p k n", p=P)).then_inc(s["w_loaded"], 16)
                sp.dma_start(wr[:, :, 0:NG], g.w_router_group[0].rearrange("(k p) n -> p k n", p=P)).then_inc(s["w_loaded"], 16)
                sp.dma_start(wr[:, :, NG:], g.w_router_expert[0].rearrange("(k p) n -> p k n", p=P)).then_inc(s["w_loaded"], 16)
                for dst, src in ((br[:, 0:NG], g.b_router_group[0:1, :]), (br[:, NG:], g.b_router_expert[0:1, :]), (sinks[:], g.attn_sinks[0:1, :]),
                                 (aon[:], g.attn_out_norm[0:1, :]), (hon[:], g.hgrn_out_norm[0:1, :])):
                    sp.dma_start(dst, src.to_broadcast(list(dst.shape))).then_inc(s["w_loaded"], 16)
                sp.dma_start(alibi[:], g.c_alibi[:, :, :]).then_inc(s["w_loaded"], 16)

                def load(i, u, uses, last):
                    sp.wait_ge(s["loads_free"], i + 1)
                    sp.dma_start(qT[0:HD, u, :, :], g.qaT.rearrange("(h d) t -> d h t", d=HD)[:, :, bass.ds(i * P, P)]).then_inc(loaded[u], 16)
                    sp.dma_start(kT[0:HD, u, :, :], g.kaT.rearrange("(h d) t -> d h t", d=HD)[:, :, bass.ds(i * P, 2 * P)]).then_inc(loaded[u], 16)
                    for n in range(AKV):
                        sp.dma_start(kT[HD:HD + 1, u, n, :], g.c_padflag[:, bass.ds(i * P + LEFT * CW - P, 2 * P)]).then_inc(loaded[u], 16)
                    sp.dma_start(vw[:, u, :, :], g.va[bass.ds(i * P, 2 * P), :].rearrange("(c p) n -> p c n", p=P)).then_inc(loaded[u], 16)
                    sp.dma_start(hx[:, u, :, :], g.hg5[bass.ds(i * P, P), :, :]).then_inc(loaded[u], 16)
                    sp.dma_start(xb[:, u, :], g.x[0, bass.ds(i * P, P), :]).then_inc(loaded[u], 16)
                pairs(sp, NB, load)

            @block.gpsimd
            def _(pool):
                nc.gpsimd.memset(half[:], -0.5).then_inc(s["half_ready"], 1)
                nc.gpsimd.memset(St[:, 0, 0, :], 0.0).then_inc(s["neg_ready"], 1)
                nc.gpsimd.memset(A[:], 0.0).then_inc(s["neg_ready"], 1)
                pool.wait_ge(s["neg_ready"], 2)
                nc.gpsimd.memset(qT[HD:HD + 1, :, :, :], NEG).then_inc(s["neg_ready"], 1)
                pool.wait_ge(s["half_ready"], 1)

                def power(wait, i, src, dst, n, done):
                    pool.wait_ge(s[wait], i + 1)
                    nc.gpsimd.tensor_tensor(sm[:, dst, 0:n], sm[:, src, 0:n], half[:, 0:n], ALU.pow).then_inc(s[done], 1)

                def step(f, t):
                    if f:
                        i, u, uses = f
                        pool.wait_ge(loaded[u], 112 * uses)
                        pool.wait_ge(s["exps_done"], i + 1)
                        pool.wait_ge(s["kv_done"], NCH * i + 1)
                        for n, src in enumerate((0, 1, 1)):
                            last = nc.gpsimd.tensor_tensor(Q[:, n, :], hx[:, u, src, :], E[:, n, :], ALU.mult)
                        last.then_inc(s["decayed"], 1)
                    if t:
                        i, u, uses = t
                        power("mst_ready", i, MST, RST, 1, "rst_ready")
                        power("msx_ready", i, SSX, RSX, 1, "rsx_ready")
                        pool.wait_ge(s["xn_ready"], i + 1)
                        settle(g, pool)
                        pool.dma_start(g.x1[bass.ds(i * P, P), :], x1[:, u, :]).then_inc(s["stored"], 16)
                        pool.dma_start(g.xn2[bass.ds(i * P, P), :], xn[:, u, :]).then_inc(s["stored"], 16)
                    if f:
                        i, u, uses = f
                        power("msa_ready", i, MSA, RSA, 1, "rsa_ready")
                        power("msh_ready", i, MSH, RSH, HH, "rsh_ready")
                overlapped(pool, NB, step)
                pool.wait_ge(s["stored"], 32 * NB)

            @block.tensor
            def _(pe):
                pe.wait_ge(s["w_loaded"], 16 * 9)
                pe.wait_ge(s["neg_ready"], 3)

                def cum(i, u, uses):
                    pe.wait_ge(loaded[u], 112 * uses)
                    pe.wait_ge(s["oh_read"], i + 1)
                    pe.wait_ge(s["kv_read"], NCH * i + 1)
                    lf = hx[:, u, 2, :]
                    nc.tensor.matmul(B0[:, :], g.square[:, C_TRI, :], lf, start=True, stop=True)
                    nc.tensor.matmul(B1[:, :], g.square[:, C_AFTER, :], lf, start=True, stop=True)
                    pe.wait_ge(s["pt_read"], AH * i + 1)
                    for h in range(HH):
                        mm = nc.tensor.matmul(BPT[:, NCH * h:NCH * h + NCH], hx[:, u, 2, h * HK:(h + 1) * HK], g.square[:, C_CHUNK, 0:NCH],
                                              start=True, stop=True)
                    mm.then_inc(s["cum_done"], 1)

                def qk(i, u, h):
                    pe.wait_ge(s["s_read"], AH * i + h + 1)
                    nc.tensor.matmul((BS0, BS1)[h % 2][:, 0:2 * P], qT[:, u, h, :], kT[:, u, h // (AH // AKV), :],
                                     start=True, stop=True).then_inc(s["qk_done"], 1)

                def turn_p(i, u, h):
                    pe.wait_ge(s["p_ready"], AH * i + h + 3)
                    if h == 0:
                        pe.wait_ge(s["exps_done"], i + 1)
                    pe.wait_ge(s["pt_read"], AH * i + h + 1)
                    for c in range(2):
                        mm = nc.tensor.transpose(BPT[:, c * P:(c + 1) * P], Pb[:, h % 2, c * P:(c + 1) * P], g.square[:, C_ID, :])
                    mm.then_inc(s["tp_done"], 1)

                def pv(i, u, h):
                    if h == 0:
                        pe.wait_ge(s["at_ready"], i + 1)
                    pe.wait_ge(s["pt_read"], AH * i + h + 2)
                    n = h // (AH // AKV)
                    for c in range(2):
                        mm = nc.tensor.matmul(BO[:, h * HD:(h + 1) * HD], PT[:, h % 2, c * P:(c + 1) * P], vw[:, u, c, n * HD:(n + 1) * HD],
                                              start=(c == 0), stop=(c == 1))
                    mm.then_inc(s["pv_done"], 1)

                def turn_d(i, u):
                    pe.wait_ge(s["decayed"], i + 1)
                    for n, b in enumerate((B0, B1)):
                        for h in range(HH):
                            mm = nc.tensor.transpose(b[:, h * HK:(h + 1) * HK], Q[:, n, h * HK:(h + 1) * HK], g.square[:, C_ID, :])
                    mm.then_inc(s["dT_done"], 1)

                def intra(i, u):
                    pe.wait_ge(s["dT_read"], i + 1)
                    for h in range(HH):
                        mm = nc.tensor.matmul(B0[:, h * P:(h + 1) * P], QT[:, 1, h * HK:(h + 1) * HK], QT[:, 0, h * HK:(h + 1) * HK], start=True, stop=True)
                    mm.then_inc(s["a_done"], 1)

                def kv(i, u, j):
                    if j == 1:
                        pe.wait_ge(s["a_read"], i + 1)
                    if j > 1:
                        pe.wait_ge(s["kv_read"], NCH * i + j)
                    r = slice(CH * j, CH * j + CH)
                    for h in range(HH):
                        c = slice(h * HK, (h + 1) * HK)
                        mm = nc.tensor.matmul((B1, B0)[j % 2][:, c], Q[r, 2, c], hx[r, u, 3, c], start=True, stop=True, tile_position=(CH * j, 0))
                    mm.then_inc(s["kv_done"], 1)

                def hgrn_out(i, u):
                    pe.wait_ge(s["a_read"], i + 1)
                    pe.wait_ge(s["kv_read"], NCH * i + NCH)
                    for h in range(HH):
                        c = slice(h * HK, (h + 1) * HK)
                        nc.tensor.matmul(B1[:, c], A[:, c], hx[:, u, 3, c], start=True, stop=True)
                        for j in range(NCH):
                            mm = nc.tensor.matmul(B1[CH * j:CH * j + CH, c], QT[:, 0, h * HK + CH * j:h * HK + CH * j + CH], St[:, u, j, c],
                                                  start=False, stop=True, skip_group_check=True, tile_position=(0, CH * j))
                    mm.then_inc(s["oh_done"], 1)

                def turn_mix(i, u):
                    pe.wait_ge(s["mixin_ready"], i + 1)
                    pe.wait_ge(s["logit_read"], i + 1)
                    for k in range(KD):
                        mm = nc.tensor.transpose((X0, W0)[k // 4][:, (k % 4) * P:(k % 4 + 1) * P], mixin[:, k * P:(k + 1) * P], g.square[:, C_ID, :])
                    mm.then_inc(s["mixT_done"], 1)

                def out_product(i, u, n):
                    pe.wait_ge(s["mixT_read"], i + 1)
                    for k in range(KD):
                        mm = nc.tensor.matmul((W0, X0)[n][:, :], mixT[:, k, :], wout[:, k, n * 512:(n + 1) * 512], start=(k == 0), stop=(k == KD - 1))
                    mm.then_inc(s["wo_done"], 1)

                def turn_h2(i, u):
                    pe.wait_ge(s["xn_ready"], i + 1)
                    for k in range(KD):
                        mm = nc.tensor.transpose((X0, W0)[k // 4][:, (k % 4) * P:(k % 4 + 1) * P], xn[:, u, k * P:(k + 1) * P], g.square[:, C_ID, :])
                    mm.then_inc(s["h2_done"], 1)

                def router(i, u):
                    pe.wait_ge(s["h2_read"], i + 1)
                    for k in range(KD):
                        mm = nc.tensor.matmul(X0[:, 0:NG + NE], h2T[:, k, :], wr[:, k, :], start=(k == 0), stop=(k == KD - 1))
                    mm.then_inc(s["logit_done"], 1)

                def step(f, t):
                    if f:
                        cum(*f)
                        qk(*f[:2], 0)
                        qk(*f[:2], 1)
                    for h in range(AH):
                        if f:
                            turn_p(*f[:2], h)
                            if h + 2 < AH:
                                qk(*f[:2], h + 2)
                            if h:
                                pv(*f[:2], h - 1)
                        if t and h == 0:
                            turn_mix(*t[:2])
                        if f and h == 1:
                            turn_d(*f[:2])
                        if f and h == 2:
                            intra(*f[:2])
                        if t and h == 2:
                            out_product(*t[:2], 0)
                        if f and 3 <= h < 7:
                            kv(*f[:2], h - 3)
                        if t and h == 4:
                            out_product(*t[:2], 1)
                    if f:
                        pv(*f[:2], AH - 1)
                        hgrn_out(*f[:2])
                    if t:
                        turn_h2(*t[:2])
                        router(*t[:2])
                overlapped(pe, NB, step)

            @block.scalar
            def _(act):
                act.sem_inc(s["pt_read"], 1)
                act.sem_inc(s["p_ready"], 2)

                def exps(i, u):
                    act.wait_ge(s["cum_done"], i + 1)
                    act.wait_ge(s["exps_read"], i + 1)
                    nc.scalar.activation(E[:, 0, :], B0[:, :], ACT.Exp)
                    nc.scalar.activation(E[:, 1, :], B0[:, :], ACT.Exp, scale=-1.0)
                    nc.scalar.activation(E[:, 2, :], B1[:, :], ACT.Exp)
                    nc.scalar.activation(dec[:], BPT[:, 0:HH * NCH], ACT.Exp).then_inc(s["exps_done"], 1)

                def prob(i, u, h):
                    act.wait_ge(s["nm_ready"], AH * i + h + 1)
                    act.wait_ge(s["tp_done"], AH * i + h + 1)
                    nc.scalar.activation(Pb[:, h % 2, :], S[:, h % 2, :], ACT.Exp, bias=sm[:, NM, h:h + 1], accum_out=sm[:, L, h:h + 1]).then_inc(s["p_ready"], 1)

                def probT(i, u, h):
                    act.wait_ge(s["tp_done"], AH * i + h + 3)
                    act.wait_ge(s["pv_done"], AH * i + h + 1)
                    nc.scalar.activation(PT[:, h % 2, :], BPT[:, 0:2 * P], ACT.Copy).then_inc(s["pt_read"], 1)

                def step(f, t):
                    if f:
                        exps(*f[:2])
                        prob(*f[:2], 0)
                    for h in range(AH):
                        if f:
                            if h + 1 < AH:
                                prob(*f[:2], h + 1)
                            probT(*f[:2], h)
                        if t and h == 3:
                            i, u, _ = t
                            act.wait_ge(s["wo_done"], 2 * i + 1)
                            nc.scalar.activation(mo[:, 0:512], W0[:, :], ACT.Copy).then_inc(s["wo_read"], 1)
                        if t and h == 5:
                            i, u, _ = t
                            act.wait_ge(s["wo_done"], 2 * i + 2)
                            nc.scalar.activation(mo[:, 512:D], X0[:, :], ACT.Copy).then_inc(s["wo_read"], 1)
                            act.wait_ge(s["wo_read"], 2 * i + 2)
                            nc.scalar.activation(junk[:], mo[:], ACT.Square, accum_out=sm[:, SST, 0:1]).then_inc(s["sst_ready"], 1)
                        if t and h == 7:
                            i, u, _ = t
                            act.wait_ge(s["x1_ready"], i + 1)
                            nc.scalar.activation(junk[:], x1[:, u, :], ACT.Square, accum_out=sm[:, SSX, 0:1]).then_inc(s["ssx_ready"], 1)
                            act.wait_ge(s["rsx_ready"], i + 1)
                            nc.scalar.activation(xn[:, u, :], x1[:, u, :], ACT.Copy, scale=sm[:, RSX, 0:1]).then_inc(s["xn_ready"], 1)
                    if f:
                        i, u, _ = f
                        act.wait_ge(s["sink_arg"], i + 1)
                        nc.scalar.activation(sm[:, ES, :], sm[:, ES, :], ACT.Exp).then_inc(s["sink_exp"], 1)
                        act.wait_ge(s["at_ready"], i + 2)
                        nc.scalar.activation(junk[:, 0:AW], at[:], ACT.Square, accum_out=sm[:, SSA, 0:1]).then_inc(s["ssa_ready"], 1)
                        act.drain()
                        act.wait_ge(s["oh_done"], i + 1)
                        for h in range(HH):
                            last = nc.scalar.activation(junk[:, h * HK:(h + 1) * HK], B1[:, h * HK:(h + 1) * HK], ACT.Square, accum_out=sm[:, SSH, h:h + 1])
                        last.then_inc(s["ssh_ready"], 1)
                overlapped(act, NB, step)

            @block.vector
            def _(v):
                v.sem_inc(s["loads_free"], 2)
                for n in "exps_read at_ready oh_read logit_read".split():
                    v.sem_inc(s[n], 1)
                v.sem_inc(s["kv_read"], 1)
                v.sem_inc(s["kv_done"], 1)
                v.sem_inc(s["s_read"], 2)
                v.sem_inc(s["tp_done"], 2)
                v.sem_inc(s["pv_done"], 2)
                v.wait_ge(s["w_loaded"], 16 * 9)
                v.wait_ge(s["neg_ready"], 3)

                def rowmax(i, u, h):
                    v.wait_ge(s["qk_done"], AH * i + h + 1)
                    v.wait_ge(s["p_ready"], AH * i + h + 1)
                    settle(g, v)
                    nc.vector.tensor_tensor_reduce(S[:, h % 2, :], (BS0, BS1)[h % 2][:, 0:2 * P], alibi[:, h, :], 1.0, sinks[:, h:h + 1],
                                                   ALU.add, ALU.max, sm[:, MX, h:h + 1]).then_inc(s["s_read"], 1)
                    v.drain()
                    nc.vector.tensor_scalar(sm[:, NM, h:h + 1], sm[:, MX, h:h + 1], -1.0, None, ALU.mult).then_inc(s["nm_ready"], 1)

                def update(i, u, j):
                    v.drain()
                    v.wait_ge(s["kv_done"], NCH * i + j + 2)
                    nxt = St[:, u, j + 1, :] if j + 1 < NCH else St[:, 1 - u, 0, :]
                    for h in range(HH):
                        c = slice(h * HK, (h + 1) * HK)
                        last = nc.vector.scalar_tensor_tensor(out=nxt[:, c], in0=St[:, u, j, c], scalar=dec[:, NCH * h + j:NCH * h + j + 1],
                                                              in1=(B1, B0)[j % 2][:, c], op0=ALU.mult, op1=ALU.add)
                    last.then_inc(s["kv_read"], 1)

                def step(f, t):
                    if f:
                        rowmax(*f[:2], 0)
                        rowmax(*f[:2], 1)
                    for h in range(AH):
                        if f and h + 2 < AH:
                            rowmax(*f[:2], h + 2)
                        if t and h == 0:
                            i = t[0]
                            v.wait_ge(s["mixT_done"], i + 1)
                            nc.vector.tensor_copy(mixT[:, 0:4, :], X0[:, :].rearrange("p (k t) -> p k t", k=4))
                            nc.vector.tensor_copy(mixT[:, 4:8, :], W0[:, :].rearrange("p (k t) -> p k t", k=4)).then_inc(s["mixT_read"], 1)
                        if f and h == 1:
                            i = f[0]
                            v.wait_ge(s["decayed"], i + 1)
                            v.sem_inc(s["exps_read"], 1)
                            v.wait_ge(s["dT_done"], i + 1)
                            nc.vector.tensor_copy(QT[:, 0, :], B0[:, :])
                            nc.vector.tensor_copy(QT[:, 1, :], B1[:, :]).then_inc(s["dT_read"], 1)
                        if f and h == 2:
                            i = f[0]
                            v.wait_ge(s["a_done"], i + 1)
                            settle(g, v)
                            nc.vector.copy_predicated(A[:].rearrange("p (h t) -> p h t", h=HH),
                                                      g.square[:, C_TRI:C_TRI + 1, :].bitcast(I32).to_broadcast([P, HH, P]),
                                                      B0[:, :].rearrange("p (h t) -> p h t", h=HH)).then_inc(s["a_read"], 1)
                        if f and 3 <= h < 7:
                            update(*f[:2], h - 3)
                        if t and h == 6:
                            i, u, _ = t
                            v.wait_ge(s["sst_ready"], i + 1)
                            nc.vector.tensor_scalar(sm[:, MST, 0:1], sm[:, SST, 0:1], 1.0 / D, EPS, ALU.mult, ALU.add).then_inc(s["mst_ready"], 1)
                            v.wait_ge(s["rst_ready"], i + 1)
                            v.wait_ge(s["stored"], 32 * i) if not isinstance(i, int) or i > 0 else None
                            nc.vector.scalar_tensor_tensor(out=x1[:, u, :], in0=mo[:], scalar=sm[:, RST, 0:1], in1=g.gate[:, 0, :], op0=ALU.mult, op1=ALU.mult)
                            v.drain()
                            nc.vector.tensor_tensor(x1[:, u, :], x1[:, u, :], xb[:, u, :], ALU.add).then_inc(s["x1_ready"], 1)
                            v.wait_ge(s["ssx_ready"], i + 1)
                            nc.vector.tensor_scalar(sm[:, SSX, 0:1], sm[:, SSX, 0:1], 1.0 / D, EPS, ALU.mult, ALU.add).then_inc(s["msx_ready"], 1)
                    if f:
                        i, u, _ = f
                        v.wait_ge(s["nm_ready"], AH * i + AH)
                        nc.vector.tensor_tensor(sm[:, ES, :], sinks[:], sm[:, NM, :], ALU.add).then_inc(s["sink_arg"], 1)
                        v.wait_ge(s["sink_exp"], i + 1)
                        nc.vector.tensor_tensor(sm[:, ES, :], sm[:, L, :], sm[:, ES, :], ALU.add)
                        v.drain()
                        nc.vector.reciprocal(sm[:, RL, :], sm[:, ES, :])
                        v.drain()
                        v.wait_ge(s["pv_done"], AH * i + AH + 2)
                        nc.vector.tensor_tensor(gelem(at[:], AH), gelem(BO[:, :], AH), sm[:, RL, :].unsqueeze(2).to_broadcast([P, AH, HD]), ALU.mult).then_inc(s["at_ready"], 1)
                        v.wait_ge(s["ssa_ready"], i + 1)
                        nc.vector.tensor_scalar(sm[:, MSA, 0:1], sm[:, SSA, 0:1], 1.0 / AW, EPS, ALU.mult, ALU.add).then_inc(s["msa_ready"], 1)
                        v.wait_ge(s["ssh_ready"], i + 1)
                        nc.vector.tensor_scalar(sm[:, MSH, 0:HH], sm[:, SSH, 0:HH], 1.0 / HK, EPS, ALU.mult, ALU.add).then_inc(s["msh_ready"], 1)
                        v.wait_ge(s["rsa_ready"], i + 1)
                        nc.vector.scalar_tensor_tensor(out=mixin[:, 0:AW], in0=at[:], scalar=sm[:, RSA, 0:1], in1=aon[:], op0=ALU.mult, op1=ALU.mult)
                        v.wait_ge(s["rsh_ready"], i + 1)
                        for h in range(HH):
                            c = slice(h * HK, (h + 1) * HK)
                            last = nc.vector.scalar_tensor_tensor(out=mixin[:, AW + h * HK:AW + (h + 1) * HK], in0=B1[:, c], scalar=sm[:, RSH, h:h + 1],
                                                                  in1=hon[:, c], op0=ALU.mult, op1=ALU.mult)
                        last.then_inc(s["oh_read"], 1)
                        v.drain()
                        nc.vector.tensor_tensor(mixin[:, AW:], mixin[:, AW:], hx[:, u, 4, :], ALU.mult).then_inc(s["mixin_ready"], 1)
                    if t:
                        i, u, _ = t
                        v.sem_inc(s["loads_free"], 1)
                        v.wait_ge(s["h2_done"], i + 1)
                        for k in range(KD):
                            last = nc.vector.tensor_scalar(h2T[:, k, :], (X0, W0)[k // 4][:, (k % 4) * P:(k % 4 + 1) * P],
                                                           g.scale[:, 1, k:k + 1], g.shift[:, 1, k:k + 1], ALU.mult, ALU.add)
                        last.then_inc(s["h2_read"], 1)
                        v.wait_ge(s["logit_done"], i + 1)
                        nc.vector.tensor_tensor(g.logits[:, bass.ds(i, 1), :].rearrange("p a n -> p (a n)"), X0[:, 0:NG + NE], br[:], ALU.add).then_inc(s["logit_read"], 1)
                overlapped(v, NB, step)



def stage_route(nc, g):
    with ExitStack() as x:
        sb = lambda n, s, d=F32: x.enter_context(nc.sbuf_tensor(n, s, d))
        sem = x.enter_context(semaphores(nc, "route"))
        ec = sb("r_consts", [P, NE * 4 + 64])
        mg = sb("r_maxg", [P, NB])
        gt = sb("r_group", [P, NB, NG])
        go = sb("r_onegroup", [P, NB, NG])
        lm = sb("r_masked", [P, NB, NE])
        t32 = sb("r_tmp", [P, NB, NE])
        oh = sb("r_onehot", [P, 2, NB, NE])
        both = sb("r_both", [P, NB, NE])
        mx = sb("r_max", [P, 2, NB])
        first = sb("r_first", [P, NB])
        gw = sb("r_gw", [P, 4, NB])
        base = sb("r_base", [P, NB + 1, NE])
        cmp_ = sb("r_cmp", [P, NE, NE])
        ov = sb("r_over", [P, 4, NE])
        rk = sb("r_rank", [P, 4, NB])
        tok = sb("r_token", [P, NB], I32)
        zero = sb("r_zero", [NT, P], I32)
        pc = x.enter_context(nc.psum_tensor("r_before", [P, NB, NE], F32))
        pt = x.enter_context(nc.psum_tensor("r_total", [P, NB, NE], F32))
        consts, arg, expd, arg2, exp2, onehots, counted, routed, zeroed, scattered, tokens = map(
            sem, "consts group_arg group_exp pair_arg pair_exp onehots counted routed ids_zeroed ids_scattered token_ids".split())
        with nc.Block() as block:
            @block.sync
            def _(sp):
                sp.dma_start(ec[:], g.c_expert[:, :]).then_inc(consts, 16)

            @block.scalar
            def _(act):
                act.wait_ge(arg, 1)
                nc.scalar.activation(gt[:], gt[:], ACT.Exp).then_inc(expd, 1)
                act.wait_ge(arg2, 1)
                nc.scalar.activation(gw[:, 1, :], gw[:, 1, :], ACT.Exp).then_inc(exp2, 1)

            @block.tensor
            def _(pe):
                pe.wait_ge(onehots, 1)
                nc.tensor.matmul(pc[:], g.square[:, C_BEFORE, :], both[:], start=True, stop=True)
                nc.tensor.matmul(pt[:], g.square[:, C_ONES, :], both[:], start=True, stop=True).then_inc(counted, 1)

            @block.gpsimd
            def _(pool):
                nc.gpsimd.iota(tok[:], pattern=[[P, NB]], base=0, channel_multiplier=1).then_inc(tokens, 1)
                nc.gpsimd.memset(zero[:], 0).then_inc(tokens, 1)
                pool.wait_ge(tokens, 2)
                pool.dma_start(g.ids.rearrange("(t p) o -> t (p o)", p=P), zero[:]).then_inc(zeroed, 16)
                pool.wait_ge(zeroed, 16)
                pool.wait_ge(routed, 1)
                for n in range(2):
                    for b in range(NB):
                        pool.indirect_dma_start(out=g.ids[:, :], out_offset=bass.IndirectOffsetOnAxis(ap=g.route[:, b, n:n + 1].bitcast(U32), axis=0),
                                                in_=tok[:, b:b + 1], in_offset=None).then_inc(scattered, 16)
                pool.wait_ge(scattered, 16 * 2 * NB)

            @block.vector
            def _(v):
                V = nc.vector
                bc = lambda ap, n: ap.unsqueeze(2).to_broadcast([P, NB, n])
                row = lambda at, n: ec[:, at:at + n].unsqueeze(1).to_broadcast([P, NB, n])
                v.wait_ge(consts, 16)
                lg, le = g.logits[:, :, 0:NG], g.logits[:, :, NG:]
                V.tensor_reduce(mg[:], lg, AX.X, ALU.max)
                v.drain()
                V.tensor_tensor(gt[:], lg, bc(mg[:], NG), ALU.subtract)
                V.tensor_tensor(go[:], lg, bc(mg[:], NG), ALU.is_equal)
                V.tensor_scalar(ec[:, 0:NE], ec[:, 0:NE], -1.0, float(NE), ALU.mult, ALU.add)
                V.tensor_scalar(ec[:, 4 * NE:4 * NE + NG], ec[:, 4 * NE:4 * NE + NG], -1.0, float(NG), ALU.mult, ALU.add)
                v.drain().then_inc(arg, 1)
                V.tensor_tensor(go[:], go[:], row(4 * NE, NG), ALU.mult)
                v.drain()
                V.tensor_reduce(first[:], go[:], AX.X, ALU.max)
                v.drain()
                V.tensor_tensor(go[:], bc(first[:], NG), row(4 * NE, NG), ALU.is_equal)
                v.drain()
                V.tensor_scalar(go[:], go[:], -1.0, 1e30, ALU.add, ALU.mult)
                v.drain()
                V.tensor_tensor(lm[:].rearrange("p b (a e) -> p b a e", a=NG), le.rearrange("p b (a e) -> p b a e", a=NG),
                                go[:].unsqueeze(3).to_broadcast([P, NB, NG, EPG]), ALU.add)
                v.drain()
                for n in range(2):
                    V.tensor_reduce(mx[:, n, :], lm[:], AX.X, ALU.max)
                    v.drain()
                    V.tensor_tensor(t32[:], lm[:], bc(mx[:, n, :], NE), ALU.is_equal)
                    v.drain()
                    V.tensor_tensor(t32[:], t32[:], row(0, NE), ALU.mult)
                    v.drain()
                    V.tensor_reduce(first[:], t32[:], AX.X, ALU.max)
                    v.drain()
                    V.tensor_tensor(oh[:, n, :, :], bc(first[:], NE), row(0, NE), ALU.is_equal)
                    v.drain()
                    if n == 0:
                        V.tensor_scalar(t32[:], oh[:, 0, :, :], -2e30, None, ALU.mult)
                        v.drain()
                        V.tensor_tensor(lm[:], lm[:], t32[:], ALU.add)
                        v.drain()
                V.tensor_tensor(both[:], oh[:, 0, :, :], oh[:, 1, :, :], ALU.add).then_inc(onehots, 1)
                v.wait_ge(expd, 1)
                V.tensor_reduce(gw[:, 0, :], gt[:], AX.X, ALU.add)
                V.tensor_tensor(gw[:, 1, :], mx[:, 1, :], mx[:, 0, :], ALU.subtract).then_inc(arg2, 1)
                v.wait_ge(exp2, 1)
                V.tensor_scalar(gw[:, 2, :], gw[:, 1, :], 1.0, None, ALU.add)
                v.drain()
                V.tensor_tensor(gw[:, 2, :], gw[:, 2, :], gw[:, 0, :], ALU.mult)
                v.drain()
                V.reciprocal(gw[:, 3, :], gw[:, 2, :])
                v.drain()
                V.tensor_copy(g.route[:, :, 2].bitcast(F32), gw[:, 3, :])
                V.tensor_tensor(g.route[:, :, 3].bitcast(F32), gw[:, 3, :], gw[:, 1, :], ALU.mult)
                V.memset(base[:, 0, :], 0.0)
                v.drain()
                v.wait_ge(counted, 1)
                for b in range(NB):
                    V.tensor_tensor(base[:, b + 1, :], base[:, b, :], pt[:, b, :], ALU.add)
                    v.drain()
                V.tensor_tensor(t32[:], base[:, 0:NB, :], pc[:], ALU.add)
                V.tensor_tensor(cmp_[:, :, 0:15], base[:, NB, :].unsqueeze(2).to_broadcast([P, NE, 15]),
                                ec[:, 2 * NE:2 * NE + 15].unsqueeze(1).to_broadcast([P, NE, 15]), ALU.is_gt)
                V.memset(ov[:, 3, :], 1.0)
                v.drain()
                V.tensor_reduce(ov[:, 0, :], cmp_[:, :, 0:15], AX.X, ALU.add)
                v.drain()
                V.tensor_tensor_scan(ov[:, 1, :], ov[:, 3, :], ov[:, 0, :], 0.0, ALU.mult, ALU.add)
                v.drain()
                V.tensor_tensor(ov[:, 2, :], ov[:, 1, :], ov[:, 0, :], ALU.subtract)
                V.tensor_tensor(cmp_[:], ov[:, 1, :].unsqueeze(1).to_broadcast([P, NE, NE]),
                                ec[:, 3 * NE:4 * NE].unsqueeze(2).to_broadcast([P, NE, NE]), ALU.is_le)
                v.drain()
                V.tensor_scalar(ov[:, 2, :], ov[:, 2, :], float(P), float((NE - 1) * P), ALU.mult, ALU.add)
                V.tensor_reduce(ov[:, 3, :], cmp_[:], AX.X, ALU.add)
                v.drain()
                V.tensor_scalar(ov[:, 3, :], ov[:, 3, :], float(NE - 1), None, ALU.min)
                V.tensor_tensor(ec[:, 0:NE], ec[:, 3 * NE:4 * NE], ec[:, 3 * NE:4 * NE], ALU.max)
                v.drain()
                V.tensor_copy(g.tile_expert[:, 0:NE], ec[:, 0:NE])
                V.tensor_copy(g.tile_expert[:, NE:NT], ov[:, 3, :])
                for n in range(2):
                    for q, other in enumerate((t32[:], row(NE, NE), ov[:, 2, :].unsqueeze(1).to_broadcast([P, NB, NE]))):
                        V.tensor_tensor(both[:], oh[:, n, :, :], other, ALU.mult)
                        v.drain()
                        V.tensor_reduce(rk[:, q, :], both[:], AX.X, ALU.add)
                        v.drain()
                    V.tensor_scalar(rk[:, 3, :], rk[:, 0, :], float(P), None, ALU.is_lt)
                    V.tensor_tensor(rk[:, 1, :], rk[:, 1, :], rk[:, 2, :], ALU.subtract)
                    v.drain()
                    V.tensor_tensor(rk[:, 1, :], rk[:, 1, :], rk[:, 3, :], ALU.mult)
                    V.tensor_tensor(rk[:, 0, :], rk[:, 0, :], rk[:, 2, :], ALU.add)
                    v.drain()
                    last = V.tensor_tensor(g.route[:, :, n], rk[:, 0, :], rk[:, 1, :], ALU.add)
                    v.drain()
                v.drain().then_inc(routed, 1)


def stage_experts(nc, g):
    with ExitStack() as x:
        sb = lambda n, s, d=F32: x.enter_context(nc.sbuf_tensor(n, s, d))
        sem = x.enter_context(semaphores(nc, "experts"))
        wgu = sb("e_gateup", [P, 2, KD, 2 * FF])
        wd = sb("e_down", [P, 2, 2, D])
        ids = sb("e_ids", [P, 2], U32)
        xg = sb("e_rows", [P, 2, D])
        xT = sb("e_rowsT", [P, KD, P])
        sg = sb("e_sig", [P, FF])
        ac = sb("e_act", [P, FF])
        aT = sb("e_actT", [P, 2, P])
        ys = sb("e_out", [P, 2, D])
        px = x.enter_context(nc.psum_tensor("e_px", [P, 2, 512], F32))
        ph = x.enter_context(nc.psum_tensor("e_ph", [P, 2, 512], F32))
        pa = x.enter_context(nc.psum_tensor("e_pa", [P, 512], F32))
        py = x.enter_context(nc.psum_tensor("e_py", [P, 2, 512], F32))
        names = "w_free xT_done xT_read up_done sig_done act_ready aT_done aT_read down_done y_read".split()
        s = {n: sem(n) for n in names}
        w_loaded, ids_loaded, gathered, stored = ([sem(f"{n}_{u}") for u in range(2)] for n in ("tile_w_loaded", "ids_loaded", "gathered", "tile_stored"))
        with nc.Block() as block:
            @block.sync
            def _(sp):
                def load(i, u, uses, last):
                    e = sp.value_load(g.tile_expert[0:1, bass.ds(i, 1)] if not isinstance(i, int) else g.tile_expert[0:1, i:i + 1], min_val=0, max_val=NE - 1)
                    sp.wait_ge(s["w_free"], i + 1)
                    for n, w in enumerate((g.w_exp_gate, g.w_exp_up)):
                        sp.dma_start(wgu[:, u, :, n * FF:(n + 1) * FF], w[0, bass.ds(e, 1)].rearrange("o (k p) f -> p (o k) f", p=P)).then_inc(w_loaded[u], 16)
                    sp.dma_start(wd[:, u, :, :], g.w_exp_down[0, bass.ds(e, 1)].rearrange("o (k p) n -> p (o k) n", p=P)).then_inc(w_loaded[u], 16)
                pairs(sp, NT, load)

            @block.gpsimd
            def _(pool):
                def gather(i, u, uses, last):
                    pool.wait_ge(s["xT_done"], i + 1)
                    settle(g, pool)
                    pool.dma_start(ids[:, u:u + 1], g.ids[bass.ds(i * P, P), :].bitcast(U32)).then_inc(ids_loaded[u], 16)
                    pool.wait_ge(ids_loaded[u], 16 * uses)
                    settle(g, pool)
                    pool.indirect_dma_start(out=xg[:, u, :], out_offset=None, in_=g.xn2[:, :],
                                            in_offset=bass.IndirectOffsetOnAxis(ap=ids[:, u:u + 1], axis=0)).then_inc(gathered[u], 16)
                pairs(pool, NT, gather)

            @block.tensor
            def _(pe):
                pe.sem_inc(s["xT_done"], 2)

                def turn_rows(i, u, uses):
                    pe.wait_ge(gathered[u], 16 * uses)
                    pe.wait_ge(s["xT_read"], i + 1)
                    for k in range(KD):
                        mm = nc.tensor.transpose(px[:, k // 4, (k % 4) * P:(k % 4 + 1) * P], xg[:, u, k * P:(k + 1) * P], g.square[:, C_ID, :])
                    mm.then_inc(s["xT_done"], 1)

                def step(f, t):
                    if t:
                        i, u, uses = t
                        pe.wait_ge(s["act_ready"], i + 1)
                        pe.wait_ge(s["aT_read"], i + 1)
                        for k in range(2):
                            mm = nc.tensor.transpose(pa[:, k * P:(k + 1) * P], ac[:, k * P:(k + 1) * P], g.square[:, C_ID, :])
                        mm.then_inc(s["aT_done"], 1)
                    if f:
                        i, u, uses = f
                        pe.wait_ge(w_loaded[u], 48 * uses)
                        pe.wait_ge(s["xT_read"], i + 2)
                        for k in range(KD):
                            mm = nc.tensor.matmul(ph[:, u, :], xT[:, k, :], wgu[:, u, k, :], start=(k == 0), stop=(k == KD - 1))
                        mm.then_inc(s["up_done"], 1)
                        if not isinstance(i, int) or i < NT - 1:
                            turn_rows(i + 1, 1 - u, uses + u)
                    if t:
                        i, u, uses = t
                        pe.wait_ge(s["aT_read"], i + 2)
                        pe.wait_ge(s["y_read"], 2 * i + 2)
                        for n in range(2):
                            for k in range(2):
                                mm = nc.tensor.matmul(py[:, n, :], aT[:, k, :], wd[:, u, k, n * 512:(n + 1) * 512], start=(k == 0), stop=(k == 1))
                            mm.then_inc(s["down_done"], 1)
                turn_rows(0, 0, 1)
                overlapped(pe, NT, step)

            @block.scalar
            def _(act):
                def step(f, t):
                    if t:
                        i, u, uses = t
                        act.wait_ge(s["down_done"], 2 * i + 1)
                        act.wait_ge(stored[u], 16 * uses)
                        nc.scalar.activation(ys[:, u, 0:512], py[:, 0, :], ACT.Copy).then_inc(s["y_read"], 1)
                        act.wait_ge(s["down_done"], 2 * i + 2)
                        nc.scalar.activation(ys[:, u, 512:D], py[:, 1, :], ACT.Copy).then_inc(s["y_read"], 1)
                        act.wait_ge(s["y_read"], 2 * i + 4)
                        act.dma_start(g.ys[bass.ds(i * P, P), :], ys[:, u, :]).then_inc(stored[u], 16)
                    if f:
                        i, u, uses = f
                        act.wait_ge(s["up_done"], i + 1)
                        nc.scalar.activation(sg[:], ph[:, u, 0:FF], ACT.Sigmoid).then_inc(s["sig_done"], 1)
                overlapped(act, NT, step)
                for u in range(2):
                    act.wait_ge(stored[u], 16 * (NT // 2 + 1))

            @block.vector
            def _(v):
                v.sem_inc(s["w_free"], 2)
                v.sem_inc(s["xT_read"], 1)
                v.sem_inc(s["aT_read"], 1)
                v.sem_inc(s["y_read"], 2)
                for u in range(2):
                    v.sem_inc(stored[u], 16)

                def evac_rows(i):
                    v.wait_ge(s["xT_done"], i + 3)
                    for k in range(KD):
                        last = nc.vector.tensor_scalar(xT[:, k, :], px[:, k // 4, (k % 4) * P:(k % 4 + 1) * P],
                                                       g.scale[:, 1, k:k + 1], g.shift[:, 1, k:k + 1], ALU.mult, ALU.add)
                    last.then_inc(s["xT_read"], 1)

                def step(f, t):
                    if t:
                        i, u, uses = t
                        v.wait_ge(s["aT_done"], i + 1)
                        nc.vector.tensor_copy(aT[:], pa[:, 0:2 * P].rearrange("p (k t) -> p k t", k=2)).then_inc(s["aT_read"], 1)
                    if f:
                        i, u, uses = f
                        v.wait_ge(s["sig_done"], i + 1)
                        nc.vector.tensor_tensor(ac[:], ph[:, u, 0:FF], sg[:], ALU.mult)
                        v.drain()
                        nc.vector.tensor_tensor(ac[:], ph[:, u, FF:], ac[:], ALU.mult).then_inc(s["act_ready"], 1)
                        if not isinstance(i, int) or i < NT - 1:
                            evac_rows(i + 1)
                    if t:
                        i, u, uses = t
                        v.wait_ge(s["down_done"], 2 * i + 2)
                        v.sem_inc(s["w_free"], 1)
                evac_rows(0)
                overlapped(v, NT, step)



def stage_combine(nc, g):
    NW = BH * HD + 2 * HD + IH * ID + ID + IH
    CB = BH * HD + 2 * HD
    with ExitStack() as x:
        sb = lambda n, s, d=F32: x.enter_context(nc.sbuf_tensor(n, s, d))
        sem = x.enter_context(semaphores(nc, "combine"))
        w = sb("b_w", [P, KD, NW])
        ng = sb("b_gain", [P, KD])
        rt = sb("b_route", [P, 2, 4], I32)
        y1 = sb("b_y1", [P, 2, D])
        y2 = sb("b_y2", [P, 2, D])
        xb = sb("b_x", [P, 2, D])
        rope = sb("b_rope", [P, 2, ROPE])
        junk = sb("b_junk", [P, D])
        x2 = sb("b_x2", [P, 2, D])
        xn = sb("b_xn", [P, 2, D])
        xT = sb("b_xT", [P, 2, KD, P])
        nat = sb("b_nat", [P, 2, NW])
        rot = sb("b_rot", [P, 4, 9, 8])
        qT = sb("b_qT", [P, 2, 4, P])
        kT = sb("b_kT", [P, 2, 4, P])
        sm = sb("b_small", [P, 8])
        half = sb("b_half", [P, 1])
        px = x.enter_context(nc.psum_tensor("b_px", [P, 2, 512], F32))
        pp = x.enter_context(nc.psum_tensor("b_pp", [P, 2, 512], F32))
        pq = x.enter_context(nc.psum_tensor("b_pq", [P, 2, 512], F32))
        names = ("w_loaded half_ready route_ready gather_free y_ready ssy_ready msy_ready rsy_ready x2_ready ssx_ready msx_ready rsx_ready xn_ready xn_free "
                 "xT_done xT_ready proj_done nat_ready rotated heads_done heads_read out_free").split()
        s = {n: sem(n) for n in names}
        loaded, gathered, stored_f, stored_t = ([sem(f"{n}_{u}") for u in range(2)] for n in ("block_loaded", "block_gathered", "front_stored", "tail_stored"))
        with nc.Block() as block:
            @block.sync
            def _(sp):
                sp.dma_start(ng[:], g.norm_gain_2[0, :].rearrange("(k p) -> p k", p=P), allow_slow_non_contiguous=True).then_inc(s["w_loaded"], 16)
                wi = g.w_in_2[0].rearrange("(k p) n -> p k n", p=P)
                sp.dma_start(w[:, :, 0:CB], wi[:, :, W2["qb"]:W2["qb"] + CB]).then_inc(s["w_loaded"], 16)
                sp.dma_start(w[:, :, CB:], wi[:, :, W2["iq"]:W2["iq"] + NW - CB]).then_inc(s["w_loaded"], 16)

                def load(i, u, uses, last):
                    sp.wait_ge(s["gather_free"], i + 1)
                    sp.dma_start(xb[:, u, :], g.x1[bass.ds(i * P, P), :]).then_inc(loaded[u], 16)
                    sp.dma_start(rope[:, u, :], g.c_rope[bass.ds(i * P, P), :]).then_inc(loaded[u], 16)
                pairs(sp, NB, load)

            @block.gpsimd
            def _(pool):
                nc.gpsimd.memset(half[:], -0.5).then_inc(s["half_ready"], 1)
                pool.wait_ge(s["half_ready"], 1)

                def gather(i, u):
                    pool.wait_ge(s["route_ready"], i + 1)
                    settle(g, pool)
                    for n, y in enumerate((y1, y2)):
                        pool.indirect_dma_start(out=y[:, u, :], out_offset=None, in_=g.ys[:, :],
                                                in_offset=bass.IndirectOffsetOnAxis(ap=rt[:, u, n:n + 1].bitcast(U32), axis=0)).then_inc(gathered[u], 16)

                def step(f, t):
                    if f:
                        i, u, uses = f
                        if not isinstance(i, int) or i < NB - 1:
                            gather(i + 1, 1 - u)
                        pool.wait_ge(s["msy_ready"], i + 1)
                        nc.gpsimd.tensor_tensor(sm[:, 1:2], sm[:, 0:1], half[:], ALU.pow).then_inc(s["rsy_ready"], 1)
                        pool.wait_ge(s["msx_ready"], i + 1)
                        nc.gpsimd.tensor_tensor(sm[:, 3:4], sm[:, 2:3], half[:], ALU.pow).then_inc(s["rsx_ready"], 1)
                gather(0, 0)
                overlapped(pool, NB, step)

            @block.tensor
            def _(pe):
                pe.wait_ge(s["w_loaded"], 48)

                def step(f, t):
                    if t:
                        i, u, uses = t
                        pe.wait_ge(s["xn_ready"], i + 1)
                        for k in range(KD):
                            mm = nc.tensor.transpose(px[:, k // 4, (k % 4) * P:(k % 4 + 1) * P], xn[:, u, k * P:(k + 1) * P], g.square[:, C_ID, :])
                        mm.then_inc(s["xT_done"], 1)
                        pe.wait_ge(s["xT_ready"], i + 1)
                        for n, (c0, c1) in enumerate(((0, 512), (512, NW))):
                            for k in range(KD):
                                mm = nc.tensor.matmul(pp[:, n, 0:c1 - c0], xT[:, u, k, :], w[:, k, c0:c1], start=(k == 0), stop=(k == KD - 1))
                            mm.then_inc(s["proj_done"], 1)
                        pe.wait_ge(s["rotated"], i + 1)
                        pe.wait_ge(s["heads_read"], i + 1)
                        for c in range(4):
                            nc.tensor.transpose(pq[:, 0, c * P:(c + 1) * P], nat[:, u, c * P:(c + 1) * P], g.square[:, C_ID, :])
                        nc.tensor.transpose(pq[0:HD, 1, 0:P], nat[:, u, BH * HD:BH * HD + HD], g.square[:, C_ID, :])
                        for c in range(2):
                            nc.tensor.transpose(pq[:, 1, (c + 1) * P:(c + 2) * P], nat[:, u, CB + c * P:CB + (c + 1) * P], g.square[:, C_ID, :])
                        nc.tensor.transpose(pq[0:ID, 1, 3 * P:4 * P], nat[:, u, CB + 2 * P:CB + 2 * P + ID], g.square[:, C_ID, :]).then_inc(s["heads_done"], 1)
                overlapped(pe, NB, step)

            @block.scalar
            def _(act):
                def step(f, t):
                    if f:
                        i, u, uses = f
                        act.wait_ge(s["y_ready"], i + 1)
                        nc.scalar.activation(junk[:], y1[:, u, :], ACT.Square, accum_out=sm[:, 0:1]).then_inc(s["ssy_ready"], 1)
                        act.wait_ge(s["x2_ready"], i + 1)
                        nc.scalar.activation(junk[:], x2[:, u, :], ACT.Square, accum_out=sm[:, 2:3]).then_inc(s["ssx_ready"], 1)
                        act.wait_ge(s["rsx_ready"], i + 1)
                        act.wait_ge(s["xT_done"], i + 1)
                        nc.scalar.activation(xn[:, u, :], x2[:, u, :], ACT.Copy, scale=sm[:, 3:4]).then_inc(s["xn_ready"], 1)
                        act.dma_start(g.x2[bass.ds(i * P, P), :], x2[:, u, :]).then_inc(stored_f[u], 16)
                    if t:
                        i, u, uses = t
                        act.wait_ge(stored_t[u], 112 * uses)
                        act.wait_ge(s["proj_done"], 2 * i + 1)
                        nc.scalar.activation(nat[:, u, 0:512], pp[:, 0, :], ACT.Copy)
                        act.wait_ge(s["proj_done"], 2 * i + 2)
                        nc.scalar.activation(nat[:, u, 512:NW - IH], pp[:, 1, 0:NW - 512 - IH], ACT.Copy)
                        nc.scalar.activation(nat[:, u, NW - IH:NW], pp[:, 1, NW - 512 - IH:NW - 512], ACT.Copy, scale=IH ** -0.5 * ID ** -0.5).then_inc(s["nat_ready"], 1)
                        act.wait_ge(s["heads_done"], i + 1)
                        nc.scalar.activation(qT[:, u, :, :], pq[:, 0, :].rearrange("p (c t) -> p c t", c=4), ACT.Copy, scale=HD ** -0.5)
                        nc.scalar.activation(kT[:, u, 1:3, :], pq[:, 1, P:3 * P].rearrange("p (c t) -> p c t", c=2), ACT.Copy)
                        nc.scalar.activation(kT[0:HD, u, 0, :], pq[0:HD, 1, 0:P], ACT.Copy)
                        nc.scalar.activation(kT[0:ID, u, 3, :], pq[0:ID, 1, 3 * P:4 * P], ACT.Copy).then_inc(s["heads_read"], 1)
                        act.wait_ge(s["heads_read"], i + 2)
                        cols = bass.ds(i * P, P)
                        for dst, src in ((g.xn3T.rearrange("(k p) t -> p k t", p=P)[:, :, cols], xT[:, u, :, :]),
                                         (g.qbT.rearrange("(k p) t -> p k t", p=P)[:, :, cols], qT[:, u, :, :]),
                                         (g.kbT[:, cols], kT[0:HD, u, 0, :]),
                                         (g.iqT.rearrange("(k p) t -> p k t", p=P)[:, :, cols], kT[:, u, 1:3, :]),
                                         (g.ikT[:, cols], kT[0:ID, u, 3, :]),
                                         (g.vb[cols, :], nat[:, u, BH * HD + HD:CB]),
                                         (g.iw[cols, :], nat[:, u, NW - IH:NW])):
                            act.dma_start(dst, src).then_inc(stored_t[u], 16)
                overlapped(act, NB, step)
                for u in range(2):
                    act.wait_ge(stored_f[u], 16 * (NB // 2 + 1))
                    act.wait_ge(stored_t[u], 16 * 7 * (NB // 2 + 1))

            @block.vector
            def _(v):
                V = nc.vector
                v.sem_inc(s["gather_free"], 2)
                v.sem_inc(s["heads_read"], 1)
                v.sem_inc(s["xT_done"], 2)
                for u in range(2):
                    v.sem_inc(stored_t[u], 112)
                    v.sem_inc(stored_f[u], 16)
                v.wait_ge(s["w_loaded"], 48)

                def fetch_route(i, u):
                    V.tensor_copy(rt[:, u, :], g.route[:, bass.ds(i, 1), :].rearrange("p o n -> p (o n)")).then_inc(s["route_ready"], 1)

                def step(f, t):
                    if f:
                        i, u, uses = f
                        if not isinstance(i, int) or i < NB - 1:
                            fetch_route(i + 1, 1 - u)
                        v.wait_ge(gathered[u], 32 * uses)
                        V.tensor_scalar(y1[:, u, :], y1[:, u, :], rt[:, u, 2:3].bitcast(F32), None, ALU.mult)
                        v.drain()
                        V.scalar_tensor_tensor(out=y1[:, u, :], in0=y2[:, u, :], scalar=rt[:, u, 3:4].bitcast(F32), in1=y1[:, u, :],
                                               op0=ALU.mult, op1=ALU.add).then_inc(s["y_ready"], 1)
                        v.wait_ge(s["ssy_ready"], i + 1)
                        V.tensor_scalar(sm[:, 0:1], sm[:, 0:1], 1.0 / D, EPS, ALU.mult, ALU.add).then_inc(s["msy_ready"], 1)
                        v.wait_ge(s["rsy_ready"], i + 1)
                        v.wait_ge(stored_f[u], 16 * uses)
                        V.scalar_tensor_tensor(out=x2[:, u, :], in0=y1[:, u, :], scalar=sm[:, 1:2], in1=g.gate[:, 1, :], op0=ALU.mult, op1=ALU.mult)
                        v.drain()
                        v.wait_ge(loaded[u], 32 * uses)
                        V.tensor_tensor(x2[:, u, :], x2[:, u, :], xb[:, u, :], ALU.add).then_inc(s["x2_ready"], 1)
                        v.wait_ge(s["ssx_ready"], i + 1)
                        V.tensor_scalar(sm[:, 2:3], sm[:, 2:3], 1.0 / D, EPS, ALU.mult, ALU.add).then_inc(s["msx_ready"], 1)
                    if t:
                        i, u, uses = t
                        v.wait_ge(s["xT_done"], i + 3)
                        v.wait_ge(stored_t[u], 112 * uses)
                        for k in range(KD):
                            last = V.tensor_scalar(xT[:, u, k, :], px[:, k // 4, (k % 4) * P:(k % 4 + 1) * P], ng[:, k:k + 1], None, ALU.mult)
                        last.then_inc(s["xT_ready"], 1)
                        v.wait_ge(s["nat_ready"], i + 1)
                        for at, dh, r, c in ((0, HD, 8, 0), (CB, ID, 4, 16)):
                            q = nat[:, u, at:at + 9 * dh].rearrange("p (h d) -> p h d", d=dh)
                            lo, hi = q[:, :, 0:r], q[:, :, r:2 * r]
                            cos, sin = (rope[:, u, c + k * r:c + k * r + r].unsqueeze(1).to_broadcast([P, 9, r]) for k in range(2))
                            for n, (a_, b_) in enumerate(((lo, cos), (hi, sin), (hi, cos), (lo, sin))):
                                V.tensor_tensor(rot[:, n, :, 0:r], a_, b_, ALU.mult)
                            v.drain()
                            V.tensor_tensor(lo, rot[:, 0, :, 0:r], rot[:, 1, :, 0:r], ALU.subtract)
                            V.tensor_tensor(hi, rot[:, 2, :, 0:r], rot[:, 3, :, 0:r], ALU.add)
                            v.drain()
                        v.drain().then_inc(s["rotated"], 1)
                        v.sem_inc(s["gather_free"], 1)
                fetch_route(0, 0)
                overlapped(v, NB, step)


def stage_index_scores(nc, g):
    with ExitStack() as x:
        sb = lambda n, s, d=F32: x.enter_context(nc.sbuf_tensor(n, s, d))
        sem = x.enter_context(semaphores(nc, "index_scores"))
        ik = sb("i_k", [ID, T])
        iq = sb("i_q", [ID, 2, IH, P])
        iw = sb("i_w", [P, 2, IH])
        caus = sb("i_causal", [P, 2, 4 * P])
        rel = sb("i_relu", [P, 4, 512])
        sc = sb("i_score", [P, 2, T])
        pl = [x.enter_context(nc.psum_tensor(f"i_logits{n}", [P, 512], F32)) for n in range(8)]
        k_loaded, dot, relu, acc, freed, sc_free = map(sem, "ik_loaded dots_done relu_done accumulated loads_free score_free".split())
        loaded, stored = ([sem(f"{n}_{u}") for u in range(2)] for n in ("iq_loaded", "score_stored"))
        GROUPS = T // 512
        STEPS = [IH * (q + 1) for q in range(GROUPS)]
        START = [4 * sum(STEPS[:q]) for q in range(GROUPS)]

        def groups(eng, body):
            for q in range(GROUPS):
                with eng.Fori(0, 2) as j:
                    for u in range(2):
                        body(4 * q + 2 * j + u, u, 2 * q + j + 1, START[q] + (2 * j + u) * STEPS[q], q)

        with nc.Block() as block:
            @block.sync
            def _(sp):
                sp.dma_start(ik[:], g.ikT[:, :]).then_inc(k_loaded, 16)

                def load(i, u, uses, at, q):
                    sp.wait_ge(freed, i + 1)
                    sp.dma_start(iq[:, u, :, :], g.iqT.rearrange("(h d) t -> d h t", d=ID)[:, :, bass.ds(i * P, P)]).then_inc(loaded[u], 16)
                    sp.dma_start(iw[:, u, :], g.iw[bass.ds(i * P, P), :]).then_inc(loaded[u], 16)
                    sp.dma_start(caus[:, u, :], g.c_causal[bass.ds(i - 4 * q, 1), :, :].rearrange("o p n -> p (o n)")).then_inc(loaded[u], 16)
                groups(sp, load)

            @block.tensor
            def _(pe):
                pe.wait_ge(k_loaded, 16)

                def body(i, u, uses, at, q):
                    pe.wait_ge(loaded[u], 48 * uses)
                    for c in range(q + 1):
                        for h in range(IH):
                            n = c * IH + h
                            pe.wait_ge(relu, at + n + 1)
                            nc.tensor.matmul(pl[n % 8][:, :], iq[:, u, h, :], ik[:, c * 512:(c + 1) * 512], start=True, stop=True).then_inc(dot, 1)
                groups(pe, body)

            @block.scalar
            def _(act):
                def body(i, u, uses, at, q):
                    for n in range(IH * (q + 1)):
                        act.wait_ge(dot, at + n + 1)
                        act.wait_ge(acc, at + n + 1)
                        nc.scalar.activation(rel[:, n % 4, :], pl[n % 8][:, :], ACT.Relu).then_inc(relu, 1)
                groups(act, body)

            @block.vector
            def _(v):
                v.sem_inc(freed, 2)
                v.sem_inc(relu, 8)
                v.sem_inc(acc, 4)
                v.sem_inc(sc_free, 2)

                def body(i, u, uses, at, q):
                    v.wait_ge(sc_free, i + 1)
                    for c in range(q + 1):
                        cols = sc[:, u, c * 512:(c + 1) * 512]
                        for h in range(IH):
                            n = c * IH + h
                            v.wait_ge(relu, at + n + 9)
                            if h:
                                nc.vector.scalar_tensor_tensor(out=cols, in0=rel[:, n % 4, :], scalar=iw[:, u, h:h + 1], in1=cols,
                                                               op0=ALU.mult, op1=ALU.add).then_inc(acc, 1)
                            else:
                                nc.vector.tensor_scalar(cols, rel[:, n % 4, :], iw[:, u, h:h + 1], None, ALU.mult).then_inc(acc, 1)
                            v.drain()
                    nc.vector.tensor_tensor(cols, cols, caus[:, u, :], ALU.add)
                    v.drain().then_inc(freed, 1)
                groups(v, body)

            @block.gpsimd
            def _(pool):
                def body(i, u, uses, at, q):
                    pool.wait_ge(freed, i + 3)
                    settle(g, pool)
                    n = 512 * (q + 1)
                    pool.dma_start(g.score[bass.ds(i * P, P), 0:n], sc[:, u, 0:n]).then_inc(stored[u], 16)
                    pool.wait_ge(stored[u], 16 * uses)
                    pool.sem_inc(sc_free, 1)
                groups(pool, body)



GROUPS = T // 512


def growing(eng, unit, body):
    for q in range(GROUPS):
        start = 4 * unit * (q * (q + 1) // 2)
        with eng.Fori(0, 2) as j:
            for u in range(2):
                body(4 * q + 2 * j + u, u, 2 * q + j + 1, start + (2 * j + u) * (unit * (q + 1)), q)


def stage_select(nc, g):
    NA = 5 * 512
    with ExitStack() as x:
        sb = lambda n, s, d=F32: x.enter_context(nc.sbuf_tensor(n, s, d))
        sem = x.enter_context(semaphores(nc, "select"))
        w = sb("s_w", [P, KD, NA])
        xT = sb("s_xT", [P, 2, KD, P])
        out = sb("s_out", [P, 2, NA])
        bm = sb("s_bmerge", [P, 2 * KD])
        sc = sb("s_score", [P, 2, T])
        wk = sb("s_work", [P, T])
        best = sb("s_best", [P, 8])
        pen = sb("s_pen", [P, T])
        bank = [x.enter_context(nc.psum_tensor(f"s_bank{n}", [P, 512], F32)) for n in range(8)]
        w1_loaded, w2_loaded, done, read, sc_free, pen_ready, pen_free, zeroed, zero_stored = map(
            sem, "w1_loaded w2_loaded group_done group_read score_free penalty_ready penalty_free zeroed zero_stored".split())
        sc_loaded, xT_loaded, stored = ([sem(f"{n}_{u}") for u in range(2)] for n in ("score_loaded", "xT_loaded", "stored"))
        pen_stored = sem("penalty_stored")
        wi = g.w_in_2[0].rearrange("(k p) n -> p k n", p=P)
        with nc.Block() as block:
            @block.sync
            def _(sp):
                sp.dma_start(w[:, :, 0:2048], wi[:, :, 0:2048]).then_inc(w1_loaded, 16)
                sp.dma_start(w[:, :, 2048:NA], wi[:, :, W2["gb"]:W2["gb"] + 512]).then_inc(w1_loaded, 16)
                sp.dma_start(bm[:], g.b_merge_2[0].rearrange("a (k p) -> p (a k)", p=P), allow_slow_non_contiguous=True).then_inc(w1_loaded, 16)

                def load(before, groups):
                    def body(i, u, uses, last):
                        sp.wait_ge(done, 10 + before + groups * (i - 1))
                        sp.dma_start(xT[:, u, :, :], g.xn3T.rearrange("(k p) t -> p k t", p=P)[:, :, bass.ds(i * P, P)]).then_inc(xT_loaded[u], 16)
                    return body
                pairs(sp, NB, load(0, 5))
                sp.wait_ge(done, 10 + 5 * NB)
                sp.dma_start(w[:, :, 0:2048], wi[:, :, W2["za"]:IN2]).then_inc(w2_loaded, 16)
                pairs(sp, NB, load(5 * NB, 4))

            @block.tensor
            def _(pe):
                pe.sem_inc(done, 10)
                pe.sem_inc(read, 5)
                pe.wait_ge(w1_loaded, 48)

                def body(i, u, uses, last):
                    pe.wait_ge(xT_loaded[u], 16 * uses)
                    for q in range(5):
                        pe.wait_ge(read, 5 * i + q + 1)
                        b = bank[q]
                        for c in range(4) if q < 2 else (None,):
                            for k in range(KD):
                                if c is not None:
                                    at = q * 512 + c * P
                                    mm = nc.tensor.matmul(b[:, c * P:(c + 1) * P], w[:, k, at:at + P], xT[:, u, k, :], start=(k == 0), stop=(k == KD - 1))
                                else:
                                    mm = nc.tensor.matmul(b[:, :], xT[:, u, k, :], w[:, k, q * 512:(q + 1) * 512], start=(k == 0), stop=(k == KD - 1))
                        mm.then_inc(done, 1)
                pairs(pe, NB, body)
                pe.wait_ge(w2_loaded, 16)
                pe.wait_ge(read, 5 * NB + 5)

                def body2(i, u, uses, last):
                    pe.wait_ge(xT_loaded[u], 16 * uses + 16 * NB // 2)
                    for q in range(4):
                        pe.wait_ge(read, 5 * NB + 4 * i + q + 2)
                        for c in range(4):
                            for k in range(KD):
                                at = (q * 4 + c) * P
                                mm = nc.tensor.matmul(bank[q][:, c * P:(c + 1) * P], w[:, k, at:at + P], xT[:, u, k, :], start=(k == 0), stop=(k == KD - 1))
                        mm.then_inc(done, 1)
                pairs(pe, NB, body2)

            @block.scalar
            def _(act):
                zero = out[:, 0, :]
                act.wait_ge(zeroed, 1)
                act.dma_start(g.ka2T.rearrange("(c p) t -> p c t", p=P)[:, :, 0:LEFT * CW], zero[:, 0:2048].rearrange("p (c t) -> p c t", c=4)).then_inc(zero_stored, 16)
                act.dma_start(g.va2[0:LEFT * CW, :].rearrange("(c p) n -> p c n", p=P), zero[:, 0:2048].rearrange("p (c t) -> p c t", c=4)).then_inc(zero_stored, 16)
                act.wait_ge(zero_stored, 32)
                for u in range(2):
                    act.sem_inc(stored[u], 80)

                def body(i, u, uses, last):
                    act.wait_ge(stored[u], 80 * uses)
                    for q, (f, scale) in enumerate(((ACT.Copy, HD ** -0.5), (ACT.Copy, 1.0), (ACT.Copy, 1.0), (ACT.Silu, 1.0), (ACT.Silu, 1.0))):
                        act.wait_ge(done, 10 + 5 * i + q + 1)
                        nc.scalar.activation(out[:, u, q * 512:(q + 1) * 512], bank[q][:, :], f, scale=scale).then_inc(read, 1)
                    act.wait_ge(read, 5 * i + 10)
                    cut = lambda q: out[:, u, q * 512:(q + 1) * 512].rearrange("p (c t) -> p c t", c=4)
                    act.dma_start(g.qa2T.rearrange("(c p) t -> p c t", p=P)[:, :, bass.ds(i * P, P)], cut(0)).then_inc(stored[u], 16)
                    act.dma_start(g.ka2T.rearrange("(c p) t -> p c t", p=P)[:, :, bass.ds(i * P + LEFT * CW, P)], cut(1)).then_inc(stored[u], 16)
                    act.dma_start(g.va2[bass.ds(i * P + LEFT * CW, P), :], out[:, u, 1024:1536]).then_inc(stored[u], 16)
                    act.dma_start(g.sga[bass.ds(i * P, P), :], out[:, u, 1536:2048]).then_inc(stored[u], 16)
                    act.dma_start(g.sgb[bass.ds(i * P, P), :], out[:, u, 2048:2560]).then_inc(stored[u], 16)
                pairs(act, NB, body)

                def body2(i, u, uses, last):
                    act.wait_ge(stored[u], 80 * (NB // 2 + 1) + 16 * (uses - 1))
                    for q in range(4):
                        act.wait_ge(done, 10 + 5 * NB + 4 * i + q + 1)
                        for c in range(4):
                            n = 4 * q + c
                            mm = nc.scalar.activation(out[:, u, n * P:(n + 1) * P], bank[q][:, c * P:(c + 1) * P], ACT.Sigmoid, bias=bm[:, n:n + 1])
                        mm.then_inc(read, 1)
                    act.wait_ge(read, 5 * NB + 5 + 4 * i + 4)
                    act.dma_start(g.gzT.rearrange("(c p) t -> p c t", p=P)[:, :, bass.ds(i * P, P)], out[:, u, 0:2048].rearrange("p (c t) -> p c t", c=16)).then_inc(stored[u], 16)
                pairs(act, NB, body2)
                for u in range(2):
                    act.wait_ge(stored[u], 80 * (NB // 2 + 1) + 16 * (NB // 2))

            @block.gpsimd
            def _(pool):
                for i in range(NB + 1):
                    if i < NB:
                        n = 512 * (i // 4 + 1)
                        pool.wait_ge(sc_free, i + 1)
                        pool.dma_start(sc[:, i % 2, 0:n], g.score[i * P:(i + 1) * P, 0:n]).then_inc(sc_loaded[i % 2], 16)
                    if i:
                        n = 512 * ((i - 1) // 4 + 1)
                        pool.wait_ge(pen_ready, i)
                        pool.dma_start(g.pen[(i - 1) * P:i * P, 0:n], pen[:, 0:n]).then_inc(pen_stored, 16)
                        pool.wait_ge(pen_stored, 16 * i)
                        pool.sem_inc(pen_free, 1)

            @block.vector
            def _(v):
                V = nc.vector
                V.memset(out[:, 0, :], 0.0).then_inc(zeroed, 1)
                v.sem_inc(sc_free, 2)
                v.sem_inc(pen_free, 1)

                def body(i, u, uses, at, q):
                    n = 512 * (q + 1)
                    s, k, p = sc[:, u, 0:n], wk[:, 0:n], pen[:, 0:n]
                    v.wait_ge(sc_loaded[u], 16 * uses)
                    settle(g, v)
                    V.max(best[:], s)
                    v.drain()
                    V.match_replace(k, best[:], s, GONE)
                    v.drain()
                    for r in range(TOPK // 8 - 1):
                        V.max(best[:], k)
                        v.drain()
                        V.match_replace(k, best[:], k, GONE)
                        v.drain()
                    v.wait_ge(pen_free, i + 1)
                    V.tensor_tensor(p, k, s, ALU.is_equal)
                    v.drain()
                    V.scalar_tensor_tensor(out=p, in0=s, scalar=0.9 * NEG, in1=p, op0=ALU.is_lt, op1=ALU.max)
                    v.drain()
                    V.tensor_scalar(p, p, NEG, None, ALU.mult).then_inc(pen_ready, 1)
                    v.drain().then_inc(sc_free, 1)
                growing(v, 1, body)



def stage_attend(nc, g, banded):
    name = "banded" if banded else "sparse"
    NH = 8
    KW = BAND if banded else T
    KK = HD + 1 if banded else HD
    with ExitStack() as x:
        sb = lambda n, s, d=F32: x.enter_context(nc.sbuf_tensor(f"{name}_{n}", s, d))
        sem = x.enter_context(semaphores(nc, name))
        q = sb("q", [KK, 2, NH, P])
        if banded:
            kk = sb("k", [KK, 2, NH, KW])
            vv = sb("v", [P, 2, KW // P, NH * HD])
            bias = sb("bias", [P, NH, KW])
            band = sb("band", [P, KW])
            ext = sb("ext", [NH, BAND + P])
            rev = sb("rev", [NH, 2 * CLIP + 1])
        else:
            kk = sb("k", [KK, T])
            vv = sb("v", [P, T // P, HD])
            bias = sb("pen", [P, 2, T])
        gate = sb("gate", [P, 2, NH * HD])
        S = sb("scores", [P, 2, KW])
        Pb = sb("probs", [P, 2, KW])
        PT = sb("probsT", [P, 2, 512])
        mx = sb("max", [P, 2, 8])
        L = sb("sums", [P, 2, NH])
        at_sb = sb("out", [P, NH * HD])
        aT = sb("outT", [P, 2, 4, P])
        bs = [x.enter_context(nc.psum_tensor(f"{name}_s{n}", [P, 512], F32)) for n in range(4)]
        bt = [x.enter_context(nc.psum_tensor(f"{name}_t{n}", [P, 512], F32)) for n in range(2)]
        bo = x.enter_context(nc.psum_tensor(f"{name}_o", [P, 512], F32))
        by = x.enter_context(nc.psum_tensor(f"{name}_y", [P, 512], F32))
        const, qk, s_read, m_ready, p_ready, tp, pt_read, pv, at_ready, aT_done, aT_read, freed, bias_ready, ext_stored, rows_stored, flag = map(
            sem, "consts_loaded qk_done scores_read max_ready probs_ready probsT_done probsT_read pv_done out_ready outT_done outT_read loads_free bias_ready table_stored rows_stored flag_ready".split())
        loaded, stored = ([sem(f"{n}_{u}") for u in range(2)] for n in ("loaded", "stored"))
        LOADS = 5 + NH if banded else 3
        yT = g.yaT if banded else g.ybT

        def blocks(eng, body):
            if banded:
                widths = [512, P]
                with eng.Fori(0, NB // 2) as j:
                    for u in range(2):
                        body(2 * j + u, u, j + 1, (2 * j + u) * NH * 2, widths)
            else:
                growing(eng, NH, lambda i, u, uses, at, grp: body(i, u, uses, at, [512] * (grp + 1)))

        with nc.Block() as block:
            @block.sync
            def _(sp):
                if banded:
                    sp.dma_start(rev[:], g.rel_rev[0]).then_inc(const, 16)
                    sp.dma_start(band[:], g.c_band[:, :]).then_inc(const, 16)
                    sp.wait_ge(bias_ready, 1)
                    sp.dma_start(g.rel_ext[:, :], ext[:]).then_inc(ext_stored, 16)
                    sp.wait_ge(ext_stored, 16)
                    every_query = bass.AP(tensor=g.rel_ext.tensor, offset=0, ap=[[0, P], [BAND + P, NH], [1, BAND + P]])
                    sp.dma_start(g.rel_rows[:, :, :], every_query).then_inc(rows_stored, 16)
                    sp.wait_ge(rows_stored, 16)
                    toeplitz = bass.AP(tensor=g.rel_rows.tensor, offset=P - 1, ap=[[NH * (BAND + P) - 1, P], [BAND + P, NH], [1, BAND]])
                    sp.dma_start(bias[:], toeplitz).then_inc(const, 16)
                else:
                    sp.dma_start(kk[:], g.kbT[:, :]).then_inc(const, 16)
                    sp.dma_start(vv[:], g.vb.rearrange("(c p) n -> p c n", p=P)).then_inc(const, 16)

                def load(i, u, uses, at, widths):
                    sp.wait_ge(freed, i + 1)
                    n = sum(widths)
                    src = g.qa2T if banded else g.qbT
                    sp.dma_start(q[0:HD, u, :, :], src.rearrange("(h d) t -> d h t", d=HD)[:, :, bass.ds(i * P, P)]).then_inc(loaded[u], 16)
                    sp.dma_start(gate[:, u, :], (g.sga if banded else g.sgb)[bass.ds(i * P, P), :]).then_inc(loaded[u], 16)
                    if banded:
                        sp.dma_start(kk[0:HD, u, :, :], g.ka2T.rearrange("(h d) t -> d h t", d=HD)[:, :, bass.ds(i * P, KW)]).then_inc(loaded[u], 16)
                        for h in range(NH):
                            sp.dma_start(kk[HD:KK, u, h, :], g.c_padflag[:, bass.ds(i * P, KW)]).then_inc(loaded[u], 16)
                        for c in range(2):
                            sp.dma_start(vv[:, u, 0:4, :] if c == 0 else vv[:, u, 4:5, :],
                                         g.va2[bass.ds(i * P + 512 * c, 512 if c == 0 else P), :].rearrange("(c p) n -> p c n", p=P)).then_inc(loaded[u], 16)
                    else:
                        sp.dma_start(bias[:, u, 0:n], g.pen[bass.ds(i * P, P), 0:n]).then_inc(loaded[u], 16)
                blocks(sp, load)

            @block.gpsimd
            def _(pool):
                if banded:
                    nc.gpsimd.memset(q[HD:KK, :, :, :], NEG).then_inc(flag, 1)

            @block.tensor
            def _(pe):
                pe.sem_inc(aT_read, 1)
                pe.wait_ge(const, 48 if banded else 32)
                if banded:
                    pe.wait_ge(flag, 1)

                def body(i, u, uses, at, widths):
                    nch = len(widths)
                    pe.wait_ge(loaded[u], 16 * LOADS * uses)

                    def scores(h):
                        for c, w in enumerate(widths):
                            pe.wait_ge(s_read, at + h * nch + 4)
                            keys = kk[:, u, h, c * 512:c * 512 + w] if banded else kk[:, c * 512:c * 512 + w]
                            nc.tensor.matmul(bs[c][:, 0:w], q[:, u, h, :], keys, start=True, stop=True).then_inc(qk, 1)

                    def turn(h, c):
                        n = h * nch + c
                        if c == 0:
                            pe.wait_ge(p_ready, NH * i + h + 3)
                        pe.wait_ge(pt_read, at + n + 1)
                        for k in range(widths[c] // P):
                            mm = nc.tensor.transpose(bt[n % 2][:, k * P:(k + 1) * P], Pb[:, h % 2, c * 512 + k * P:c * 512 + (k + 1) * P], g.square[:, C_ID, :])
                        mm.then_inc(tp, 1)

                    def values(h, c):
                        n = h * nch + c
                        pe.wait_ge(pt_read, at + n + 3)
                        if h == 0 and c == 0:
                            pe.wait_ge(at_ready, i + 1)
                        for k in range(widths[c] // P):
                            val = vv[:, u, 4 * c + k, h * HD:(h + 1) * HD] if banded else vv[:, 4 * c + k, :]
                            mm = nc.tensor.matmul(bo[:, h * HD:(h + 1) * HD], PT[:, n % 2, k * P:(k + 1) * P], val,
                                                  start=(c == 0 and k == 0), stop=(c == nch - 1 and k == widths[c] // P - 1))
                        mm.then_inc(pv, 1)
                    scores(0)
                    for h in range(NH):
                        if h + 1 < NH:
                            scores(h + 1)
                        turn(h, 0)
                        for c in range(1, nch):
                            turn(h, c)
                            values(h, c - 1)
                        values(h, nch - 1)
                    pe.wait_ge(at_ready, i + 2)
                    pe.wait_ge(aT_read, i + 1)
                    for c in range(4):
                        mm = nc.tensor.transpose(by[:, c * P:(c + 1) * P], at_sb[:, c * P:(c + 1) * P], g.square[:, C_ID, :])
                    mm.then_inc(aT_done, 1)
                blocks(pe, body)

            @block.scalar
            def _(act):
                act.sem_inc(pt_read, 2)
                act.sem_inc(p_ready, 2)
                act.sem_inc(s_read, 4)
                for u in range(2):
                    act.sem_inc(stored[u], 16)

                def body(i, u, uses, at, widths):
                    nch, n_keys = len(widths), sum(widths)

                    def probs(h):
                        act.wait_ge(m_ready, NH * i + h + 1)
                        act.wait_ge(tp, at + (h - 1) * nch + 8)
                        nc.scalar.activation(Pb[:, h % 2, 0:n_keys], S[:, h % 2, 0:n_keys], ACT.Exp, bias=mx[:, h % 2, 7:8],
                                             accum_out=L[:, u, h:h + 1]).then_inc(p_ready, 1)
                    probs(0)
                    for h in range(NH):
                        if h + 1 < NH:
                            probs(h + 1)
                        for c, w in enumerate(widths):
                            n = h * nch + c
                            act.wait_ge(tp, at + n + 9)
                            act.wait_ge(pv, at + n + 1)
                            nc.scalar.activation(PT[:, n % 2, 0:w], bt[n % 2][:, 0:w], ACT.Copy).then_inc(pt_read, 1)
                    act.wait_ge(aT_done, i + 1)
                    act.wait_ge(stored[u], 16 * uses)
                    nc.scalar.activation(aT[:, u, :, :], by[:, :].rearrange("p (c t) -> p c t", c=4), ACT.Copy).then_inc(aT_read, 1)
                    act.wait_ge(aT_read, i + 2)
                    act.dma_start(yT.rearrange("(c p) t -> p c t", p=P)[:, :, bass.ds(i * P, P)], aT[:, u, :, :]).then_inc(stored[u], 16)
                blocks(act, body)
                for u in range(2):
                    act.wait_ge(stored[u], 16 * (NB // 2 + 1))

            @block.vector
            def _(v):
                V = nc.vector
                v.sem_inc(freed, 2)
                v.sem_inc(at_ready, 1)
                v.sem_inc(tp, 8)
                v.sem_inc(pv, 2)
                if banded:
                    v.wait_ge(const, 32)
                    V.tensor_copy(ext[:, 0:BAND - CLIP], rev[:, 0:1].to_broadcast([NH, BAND - CLIP]))
                    V.tensor_copy(ext[:, BAND - CLIP:BAND - CLIP + CLIP + P - 1 + 1], rev[:, 1:CLIP + P + 1]).then_inc(bias_ready, 1)
                    v.wait_ge(const, 48)
                    V.tensor_tensor(bias[:], bias[:], band[:].unsqueeze(1).to_broadcast([P, NH, KW]), ALU.add)
                    v.drain()

                def body(i, u, uses, at, widths):
                    nch = len(widths)
                    v.wait_ge(loaded[u], 16 * LOADS * uses)
                    for h in range(NH):
                        v.wait_ge(p_ready, NH * i + h + 1)
                        for c, w in enumerate(widths):
                            v.wait_ge(qk, at + h * nch + c + 1)
                            settle(g, v)
                            add = bias[:, h, c * 512:c * 512 + w] if banded else bias[:, u, c * 512:c * 512 + w]
                            V.tensor_tensor_reduce(S[:, h % 2, c * 512:c * 512 + w], bs[c][:, 0:w], add, 1.0, GONE, ALU.add, ALU.max,
                                                   mx[:, h % 2, c:c + 1]).then_inc(s_read, 1)
                        v.drain()
                        V.tensor_reduce(mx[:, h % 2, 7:8], mx[:, h % 2, 0:nch], AX.X, ALU.max, negate=True).then_inc(m_ready, 1)
                    v.wait_ge(p_ready, NH * i + NH + 2)
                    V.reciprocal(L[:, u, :], L[:, u, :])
                    v.drain()
                    v.wait_ge(pv, at + NH * nch + 2)
                    V.tensor_tensor(at_sb[:].rearrange("p (h d) -> p h d", h=NH), bo[:, :].rearrange("p (h d) -> p h d", h=NH),
                                    L[:, u, :].unsqueeze(2).to_broadcast([P, NH, HD]), ALU.mult)
                    v.drain()
                    V.tensor_tensor(at_sb[:], at_sb[:], gate[:, u, :], ALU.mult).then_inc(at_ready, 1)
                    v.drain().then_inc(freed, 1)
                blocks(v, body)


def stage_output(nc, g):
    with ExitStack() as x:
        sb = lambda n, s, d=F32: x.enter_context(nc.sbuf_tensor(n, s, d))
        sem = x.enter_context(semaphores(nc, "output"))
        wab = sb("o_wab", [P, 2, 4, D])
        wo = sb("o_wo", [P, KD, D])
        fg = sb("o_gain", [P, D])
        y = sb("o_y", [P, 2, 2, 4, P])
        gz = sb("o_gates", [P, 2, 2 * KD, P])
        xb = sb("o_x", [P, 2, D])
        mer = sb("o_merged", [P, 2, 2, KD, P])
        r = sb("o_res", [P, 2, D])
        junk = sb("o_junk", [P, D])
        sm = sb("o_small", [P, 4])
        half = sb("o_half", [P, 1])
        pb = [x.enter_context(nc.psum_tensor(f"o_branch{n}", [P, 512], F32)) for n in range(4)]
        po = [x.enter_context(nc.psum_tensor(f"o_out{n}", [P, 512], F32)) for n in range(2)]
        w_loaded, half_ready, br, br_read, merged, out_done, out_read, res, ssq, msq, rs, freed = map(
            sem, "w_loaded half_ready branch_done branch_read merged out_done out_read residual sum_squares mean_square rs_ready loads_free".split())
        loaded, stored = ([sem(f"{n}_{u}") for u in range(2)] for n in ("loaded", "stored"))
        with nc.Block() as block:
            @block.sync
            def _(sp):
                for n, w in enumerate((g.w_branch_a_2, g.w_branch_b_2)):
                    sp.dma_start(wab[:, n, :, :], w[0].rearrange("(k p) n -> p k n", p=P)).then_inc(w_loaded, 16)
                sp.dma_start(wo[:], g.w_out_2[0].rearrange("(k p) n -> p k n", p=P)).then_inc(w_loaded, 16)
                sp.dma_start(fg[:], g.final_norm_gain_2.rearrange("(o n) -> o n", o=1).to_broadcast([P, D])).then_inc(w_loaded, 16)

                def load(i, u, uses, last):
                    sp.wait_ge(freed, i + 1)
                    cols = bass.ds(i * P, P)
                    for n, src in enumerate((g.yaT, g.ybT)):
                        sp.dma_start(y[:, u, n, :, :], src.rearrange("(k p) t -> p k t", p=P)[:, :, cols]).then_inc(loaded[u], 16)
                    sp.dma_start(gz[:, u, :, :], g.gzT.rearrange("(k p) t -> p k t", p=P)[:, :, cols]).then_inc(loaded[u], 16)
                    sp.dma_start(xb[:, u, :], g.x2[cols, :]).then_inc(loaded[u], 16)
                pairs(sp, NB, load)

            @block.gpsimd
            def _(pool):
                nc.gpsimd.memset(half[:], -0.5).then_inc(half_ready, 1)
                pool.wait_ge(half_ready, 1)

                def step(f, t):
                    if t:
                        i, u, uses = t
                        pool.wait_ge(msq, i + 1)
                        nc.gpsimd.tensor_tensor(sm[:, 2:3], sm[:, 1:2], half[:], ALU.pow).then_inc(rs, 1)
                    if f:
                        i, u, uses = f
                        pool.wait_ge(br_read, 4 * i + 8)
                        nc.gpsimd.tensor_tensor(mer[:, u, 0, :, :], mer[:, u, 0, :, :], mer[:, u, 1, :, :], ALU.add).then_inc(merged, 1)
                overlapped(pool, NB, step)

            @block.tensor
            def _(pe):
                pe.sem_inc(br_read, 4)
                pe.sem_inc(out_read, 2)
                pe.wait_ge(w_loaded, 64)

                def branches(i, u, uses):
                    pe.wait_ge(loaded[u], 64 * uses)
                    for n in range(2):
                        for m in range(2):
                            pe.wait_ge(br_read, 4 * i + 2 * n + m + 1)
                            for c in range(4):
                                for k in range(4):
                                    at = (4 * m + c) * P
                                    mm = nc.tensor.matmul(pb[2 * n + m][:, c * P:(c + 1) * P], wab[:, n, k, at:at + P], y[:, u, n, k, :], start=(k == 0), stop=(k == 3))
                            mm.then_inc(br, 1)

                def step(f, t):
                    if f:
                        branches(*f)
                    if t:
                        i, u, uses = t
                        pe.wait_ge(merged, i + 1)
                        for n in range(2):
                            pe.wait_ge(out_read, 2 * i + n + 1)
                            for k in range(KD):
                                mm = nc.tensor.matmul(po[n][:, :], mer[:, u, 0, k, :], wo[:, k, n * 512:(n + 1) * 512], start=(k == 0), stop=(k == KD - 1))
                            mm.then_inc(out_done, 1)
                overlapped(pe, NB, step)

            @block.scalar
            def _(act):
                for u in range(2):
                    act.sem_inc(stored[u], 16)

                def step(f, t):
                    if t:
                        i, u, uses = t
                        act.wait_ge(res, 3 * i + 2)
                        nc.scalar.activation(junk[:], r[:, u, :], ACT.Square, accum_out=sm[:, 0:1]).then_inc(ssq, 1)
                        act.wait_ge(res, 3 * i + 3)
                        act.dma_start(g.out[0, bass.ds(i * P, P), :], r[:, u, :]).then_inc(stored[u], 16)
                overlapped(act, NB, step)
                for u in range(2):
                    act.wait_ge(stored[u], 16 * (NB // 2 + 1))

            @block.vector
            def _(v):
                V = nc.vector
                v.sem_inc(freed, 2)
                v.wait_ge(w_loaded, 64)

                def step(f, t):
                    if f:
                        i, u, uses = f
                        if not isinstance(i, int) or i > 1:
                            v.wait_ge(out_done, 2 * i - 2)
                        for n in range(2):
                            for m in range(2):
                                v.wait_ge(br, 4 * i + 2 * n + m + 1)
                                ks = slice(4 * m, 4 * m + 4)
                                V.tensor_tensor(mer[:, u, n, ks, :], pb[2 * n + m][:, :].rearrange("p (k t) -> p k t", k=4),
                                                gz[:, u, KD * n + 4 * m:KD * n + 4 * m + 4, :], ALU.mult).then_inc(br_read, 1)
                    if t:
                        i, u, uses = t
                        v.wait_ge(stored[u], 16 * uses)
                        for n in range(2):
                            v.wait_ge(out_done, 2 * i + n + 1)
                            V.tensor_tensor(r[:, u, n * 512:(n + 1) * 512], po[n][:, :], xb[:, u, n * 512:(n + 1) * 512], ALU.add).then_inc(out_read, 1)
                        v.drain().then_inc(freed, 1)
                        v.sem_inc(res, 2)
                        v.wait_ge(ssq, i + 1)
                        V.tensor_scalar(sm[:, 1:2], sm[:, 0:1], 1.0 / D, EPS, ALU.mult, ALU.add).then_inc(msq, 1)
                        v.wait_ge(rs, i + 1)
                        V.scalar_tensor_tensor(out=r[:, u, :], in0=r[:, u, :], scalar=sm[:, 2:3], in1=fg[:], op0=ALU.mult, op1=ALU.mult).then_inc(res, 1)
                overlapped(v, NB, step)




_INS = ["x", "c", "ln1_pre", "ln1_post", "ln2_pre", "ln2_post", "w_ada", "b_ada", "w_in", "attn_sinks", "attn_out_norm",
        "hgrn_lb", "hgrn_out_norm", "w_out", "w_router_group", "b_router_group", "w_router_expert", "b_router_expert",
        "w_exp_gate", "w_exp_up", "w_exp_down", "norm_gain_2", "w_in_2", "b_merge_2", "rel_bias_2", "w_branch_a_2",
        "w_branch_b_2", "w_out_2", "final_norm_gain_2"]
_SCRATCH = dict(qaT=(AW, T), kaT=(KVW, P + T), va=(P + T, KVW), hg5=(T, 5, HW_), x1=(T, D), xn2=(T, D), ids=((NT * P, 1), I32), ys=(NT * P, D), x2=(T, D), xn3T=(D, T), qbT=(BH * HD, T), kbT=(HD, T),
                iqT=(IH * ID, T), ikT=(ID, T), vb=(T, HD), iw=(T, IH), score=(T, T), pen=(T, T),
                qa2T=(512, T), ka2T=(512, LEFT * CW + T), va2=(LEFT * CW + T, 512), sga=(T, 512), sgb=(T, 512), gzT=(2 * D, T), rel_ext=(8, BAND + P), rel_rows=(P, 8, BAND + P), yaT=(512, T), ybT=(512, T))



def build(nc, g):
    with ExitStack() as x:
        sb = lambda n, s, d=F32: x.enter_context(nc.sbuf_tensor(n, s, d))
        g.square = sb("square", [P, 6, P])
        g.scale = sb("norm_scale", [P, 2, KD])
        g.shift = sb("norm_shift", [P, 2, KD])
        g.gate = sb("gate_rows", [P, 2, D])
        g.tick = x.enter_context(nc.semaphore("tick"))
        g.win1_loaded = x.enter_context(nc.semaphore("win1_loaded"))
        with nc.sbuf_tensor("win1", [P, KD, IN1], F32) as g.win1:
            stage_modulation(nc, g)
            stage_project1(nc, g)
        g.logits = sb("logits", [P, NB, NG + NE])
        g.route = sb("route", [P, NB, 4], I32)
        g.tile_expert = sb("tile_expert", [P, NT], I32)
        stage_mix(nc, g)
        stage_route(nc, g)
        stage_experts(nc, g)
        stage_combine(nc, g)
        stage_index_scores(nc, g)
        stage_select(nc, g)
        stage_attend(nc, g, True)
        stage_attend(nc, g, False)
        stage_output(nc, g)


def kernel(**inputs):
    import concourse.bacc as _bacc
    from concourse.bass_utils import run_bass_kernel_spmd as _run

    nc = _bacc.Bacc("TRN2", target_bir_lowering=False, num_devices=1)
    g = Net()
    arrays = {}
    given = {name: inputs[name] for name in _INS if name != "rel_bias_2"}
    given["rel_rev"] = np.asarray(inputs["rel_bias_2"])[:, :, ::-1]
    given.update(shape_constants())
    for name, a in given.items():
        a = np.ascontiguousarray(a)
        arrays[f"in_{name}"] = a
        g.__dict__[name] = nc.dram_tensor(f"in_{name}", a.shape, mybir.dt.from_np(a.dtype), kind="ExternalInput").ap()
    for name, shape in _SCRATCH.items():
        shape, dtype = shape if isinstance(shape[0], tuple) else (shape, F32)
        g.__dict__[name] = nc.dram_tensor(f"mid_{name}", shape, dtype, kind="Internal").ap()
    g.out = nc.dram_tensor("out_0_dram", (1, T, D), F32, kind="ExternalOutput").ap()
    build(nc, g)
    r = _run(nc, [arrays], core_ids=[0])
    return r.results[0]["out_0_dram"]
```

```python
import math
from contextlib import ExitStack, contextmanager

import numpy as np

import concourse.bass as bass
from concourse import mybir

F32 = mybir.dt.float32
F32R = mybir.dt.float32r
I32 = mybir.dt.int32
U32 = mybir.dt.uint32
ALU = mybir.AluOpType
ACT = mybir.ActivationFunctionType
AX = mybir.AxisListType

P = 128
T = 2048
D = 1024
KD = D // P
NB = T // P
EPS = 1e-6
NEG = -1e30
GONE = -3e38

AH, AKV, HD = 8, 2, 64
AW, KVW = AH * HD, AKV * HD
HH, HK = 4, 128
HW_ = HH * HK
CH = 32
NCH = P // CH
IN1 = AW + 2 * KVW + 4 * HW_
NG, EPG, NE, FF = 4, 8, 32, 256
NT = 2 * NE
CW, LEFT = 64, 8
BAND = LEFT * CW + P
CLIP = 256
BH = 8
IH, ID = 8, 32
TOPK = 256
ROPE = 24
W2 = dict(qa=0, ka=512, va=1024, ga=1536, qb=2048, kb=2560, vb=2624, gb=2688, iq=3200, ik=3456, iw=3488, za=3496, zb=4520)
IN2 = 5544
NA = 5 * 512

C_ID, C_TRI, C_AFTER, C_BEFORE, C_ONES, C_CHUNK = range(6)


def shape_constants():
    r = np.arange(P)
    same = (r[:, None] // CH) == (r[None, :] // CH)
    sq = np.zeros((P, 6, P), np.float32)
    sq[:, C_ID] = np.eye(P)
    sq[:, C_TRI] = same & (r[:, None] <= r[None, :])
    sq[:, C_AFTER] = same & (r[:, None] > r[None, :])
    sq[:, C_BEFORE] = r[:, None] < r[None, :]
    sq[:, C_ONES] = 1.0
    sq[:, C_CHUNK, 0:NCH] = (r[:, None] // CH) == np.arange(NCH)[None, :]
    dist = r[:, None] + P - np.arange(2 * P)[None, :]
    slopes = np.exp2(-8.0 * (np.arange(AH) + 1.0) / AH)
    alibi = np.where(((dist >= 0) & (dist < P))[:, None, :], -slopes[None, :, None] * dist[:, None, :], NEG).astype(np.float32)
    padflag = np.zeros((1, LEFT * CW + T), np.float32)
    padflag[:, 0:LEFT * CW] = 1.0
    pos = np.arange(T, dtype=np.float32)[:, None]

    def angles(half):
        inv = np.float32(500000.0) ** (-np.arange(half, dtype=np.float32) / np.float32(half))
        a = pos * inv.astype(np.float32)[None, :]
        return [np.cos(a), np.sin(a)]

    rope = np.concatenate(angles(8) + angles(4), axis=1).astype(np.float32)
    j = np.arange(BAND)[None, :]
    lo = r[:, None] < CW
    band = np.where((lo & (j >= BAND - CW)) | (~lo & (j < CW)), NEG, 0.0).astype(np.float32)
    j = np.arange(4 * P)
    causal = np.stack([np.where(j[None, :] < P * m + np.where(r < CW, CW, P)[:, None], 0.0, NEG) for m in range(4)], axis=0).astype(np.float32)
    ecol = np.zeros((P, NE * 4 + 64), np.float32)
    ecol[:, 0:NE] = np.arange(NE)
    ecol[:, NE:2 * NE] = np.arange(NE) * P
    ecol[:, 2 * NE:2 * NE + 15] = P * np.arange(1, 16)
    ecol[:, 3 * NE:3 * NE + NE] = np.arange(NE)
    ecol[:, 4 * NE:4 * NE + NG] = np.arange(NG)
    return dict(c_square=sq, c_alibi=alibi, c_padflag=padflag, c_rope=rope, c_band=band, c_causal=causal, c_expert=ecol)


@contextmanager
def semaphores(nc, stage):
    held = []

    def sem(name):
        held.append(nc.alloc_semaphore(f"{stage}_{name}"))
        return held[-1]
    yield sem
    nc.clear_and_free_semaphores(held)
    nc.all_engine_barrier()


def pairs(eng, n, body):
    with eng.Fori(0, n // 2 - 1) as j:
        for u in range(2):
            body(2 * j + u, u, j + 1, False)
    body(n - 2, 0, n // 2, False)
    body(n - 1, 1, n // 2, True)


def settle(g, eng):
    eng.sem_inc(g.tick, 1)


def head(v, out, x):
    return v.tensor_copy(out.bitcast(F32R), x)


def rest(v, out, x, top):
    return v.tensor_tensor(out.bitcast(F32R), x, top, ALU.subtract)


def one_pass(nc, out, lhsT, rhs, **where):
    return nc.tensor.matmul(out, lhsT.bitcast(F32R), rhs.bitcast(F32R), **where)


class Net:
    pass


def stage_modulation(nc, g):
    with ExitStack() as x:
        sb = lambda n, s, d=F32: x.enter_context(nc.sbuf_tensor(n, s, d))
        sem = x.enter_context(semaphores(nc, "modulation"))
        wa = sb("ada_w", [P, 2, KD, 512])
        mod = sb("ada_mod", [P, 48])
        bada = sb("ada_b", [P, 48])
        ccol = sb("ada_c", [P, 3, KD])
        lns = sb("ada_lns", [P, 4, KD])
        gcol = sb("ada_gcol", [P, 2, KD])
        diag = sb("ada_diag", [P, 2, KD, P])
        crep = sb("ada_c_copies", [P, KD, P])
        own = sb("ada_own", [P, 4, P])
        pm = x.enter_context(nc.psum_tensor("ada_pm", [P, 2, 512], F32))
        pg = x.enter_context(nc.psum_tensor("ada_pg", [P, 4, 512], F32))
        small, wload, sig, cact, mm, used, diags, grows = map(
            sem, "small_loaded ada_w_loaded c_sigmoid c_silu mod_product mod_added diag_ready gate_rows".split())
        wload = [wload, sem("ada_w_loaded_odd")]
        CHUNKS = 6 * D // 512

        with nc.Block() as block:
            @block.sync
            def _(sp):
                sp.dma_start(ccol[:, 0, :], g.c[0, :].rearrange("(k p) -> p k", p=P), allow_slow_non_contiguous=True).then_inc(small, 16)
                for n, v in enumerate((g.ln1_pre, g.ln2_pre, g.ln1_post, g.ln2_post)):
                    sp.dma_start(lns[:, n, :], v[0, :].rearrange("(k p) -> p k", p=P), allow_slow_non_contiguous=True).then_inc(small, 16)
                sp.dma_start(bada[:], g.b_ada[0, :].rearrange("(k p) -> p k", p=P), allow_slow_non_contiguous=True).then_inc(small, 16)
                sp.dma_start(g.square[:], g.c_square[:, :, :]).then_inc(small, 16)
                with sp.Fori(0, CHUNKS // 2) as j:
                    for u in range(2):
                        i = 2 * j + u
                        sp.wait_ge(used, i + 1)
                        sp.dma_start(wa[:, u, :, :], g.w_ada[0].rearrange("(k p) n -> p k n", p=P)[:, :, bass.ds(i * 512, 512)]).then_inc(wload[u], 16)

            @block.scalar
            def _(act):
                act.dma_start(g.win1[:], g.w_in[0].rearrange("(k p) n -> p k n", p=P)).then_inc(g.win1_loaded, 16)
                act.wait_ge(small, 16 * 7)
                nc.scalar.activation(ccol[:, 1, :], ccol[:, 0, :], ACT.Sigmoid).then_inc(sig, 1)

            @block.tensor
            def _(pe):
                pe.wait_ge(cact, 1)
                with pe.Fori(0, CHUNKS // 2) as j:
                    for u in range(2):
                        i = 2 * j + u
                        pe.wait_ge(wload[u], 16 * (j + 1))
                        pe.wait_ge(used, i + 1)
                        for k in range(KD):
                            last = nc.tensor.matmul(pm[:, u, :], crep[:, k, :], wa[:, u, k, :], start=(k == 0), stop=(k == KD - 1))
                        last.then_inc(mm, 1)
                pe.wait_ge(diags, 1)
                for h in range(2):
                    for k in range(KD):
                        last = nc.tensor.matmul(pg[:, 2 * h + k // 4, (k % 4) * P:(k % 4 + 1) * P], g.square[:, C_ONES, :], diag[:, h, k, :],
                                                start=True, stop=True)
                last.then_inc(grows, 1)

            @block.vector
            def _(v):
                v.sem_inc(used, 2)
                v.wait_ge(small, 16 * 7)
                v.wait_ge(sig, 1)
                nc.vector.tensor_tensor(ccol[:, 2, :], ccol[:, 0, :], ccol[:, 1, :], ALU.mult)
                v.drain()
                nc.vector.tensor_copy(crep[:], ccol[:, 2, :].unsqueeze(2).to_broadcast([P, KD, P])).then_inc(cact, 1)
                with v.Fori(0, CHUNKS // 2) as j:
                    for u in range(2):
                        i = 2 * j + u
                        v.wait_ge(mm, i + 1)
                        nc.vector.tensor_tensor(own[:], pm[:, u, :].rearrange("p (n q) -> p n q", n=4),
                                                g.square[:, C_ID:C_ID + 1, :].to_broadcast([P, 4, P]), ALU.mult).then_inc(used, 1)
                        v.drain()
                        nc.vector.tensor_reduce(mod[:, bass.ds(4 * i, 4)], own[:], AX.X, ALU.add)
                        v.drain()
                v.drain()
                nc.vector.tensor_tensor(mod[:], mod[:], bada[:], ALU.add)
                v.drain()
                for n in range(2):
                    nc.vector.scalar_tensor_tensor(out=g.scale[:, n, :], in0=mod[:, 24 * n + 8:24 * n + 16], scalar=1.0, in1=lns[:, n, :],
                                                   op0=ALU.add, op1=ALU.mult)
                    nc.vector.tensor_copy(g.shift[:, n, :], mod[:, 24 * n:24 * n + 8])
                    nc.vector.tensor_tensor(gcol[:, n, :], mod[:, 24 * n + 16:24 * n + 24], lns[:, 2 + n, :], ALU.mult)
                v.drain()
                for n in range(2):
                    for k in range(KD):
                        last = nc.vector.tensor_scalar(diag[:, n, k, :], g.square[:, C_ID, :], gcol[:, n, k:k + 1], None, ALU.mult)
                last.then_inc(diags, 1)
                v.wait_ge(grows, 1)
                for n in range(2):
                    nc.vector.tensor_copy(g.gate[:, n, :].rearrange("p (a b) -> p a b", a=2), pg[:, 2 * n:2 * n + 2, :])


def stage_project1(nc, g):
    with ExitStack() as x:
        sb = lambda n, s, d=F32: x.enter_context(nc.sbuf_tensor(n, s, d))
        sem = x.enter_context(semaphores(nc, "project1"))
        xb = sb("p1_x", [P, 2, D])
        junk = sb("p1_junk", [P, D])
        xn = sb("p1_xn", [P, D])
        hT = sb("p1_hT", [P, 2, KD, P])
        st = sb("p1_stat", [P, 2, 4])
        qkT = sb("p1_qkT", [P, 2, 5, P])
        va = sb("p1_va", [P, 2, P])
        hx = sb("p1_hgrn", [P, 2, 5, HW_])
        sg = sb("p1_sig", [P, 3, HW_])
        fb = sb("p1_f", [P, HW_])
        lbr = sb("p1_lbrows", [P, 2, HW_])
        lb = sb("p1_lb", [P, 3, HW_])
        zero = sb("p1_zero", [P, 2 * P])
        half = sb("p1_half", [P, 1])
        pt = x.enter_context(nc.psum_tensor("p1_pt", [P, 2, 512], F32))
        pg = x.enter_context(nc.psum_tensor("p1_pg", [P, 6, 512], F32))
        (x_loaded, x_free, sumsq, msd, rs, xn_ready, xn_free, t_done, hT_ready, hT_free, g_done, act_evac, dve_evac, sf_ready, sfree,
         f_ready, st_act, st_dve, stored, padded, lb_loaded, lb_exp, lb_ready, logs) = map(sem, (
             "x_loaded x_free sumsq mean_square rs_ready xn_ready xn_free x_transposed hT_ready hT_free group_done act_evac dve_evac "
             "sig_ready sig_free f_ready staged_act staged_dve stored padded lb_loaded lb_exp lb_ready logs_done").split())

        x_loaded = [x_loaded, sem("x_loaded_odd")]
        with nc.Block() as block:
            @block.sync
            def _(sp):
                for r in range(2):
                    sp.dma_start(lbr[:, r, :], g.hgrn_lb[r:r + 1, :].to_broadcast([P, HW_])).then_inc(lb_loaded, 16)

                def load(i, u, uses, last):
                    sp.wait_ge(x_free, i + 1)
                    sp.dma_start(xb[:, u, :], g.x[0, bass.ds(i * P, P), :]).then_inc(x_loaded[u], 16)
                pairs(sp, NB, load)

            @block.gpsimd
            def _(pool):
                nc.gpsimd.memset(half[:], -0.5).then_inc(padded, 1)
                nc.gpsimd.memset(zero[:], 0.0).then_inc(padded, 1)
                pool.wait_ge(padded, 2)
                pool.dma_start(g.kaT[:, 0:P], zero[:, 0:P]).then_inc(stored, 16)
                pool.dma_start(g.va[0:P, :], zero[:, 0:P]).then_inc(stored, 16)

                def rsqrt(i, u):
                    pool.wait_ge(msd, i + 1)
                    nc.gpsimd.tensor_tensor(st[:, u, 2:3], st[:, u, 1:2], half[:], ALU.pow).then_inc(rs, 1)

                def step(i, u, uses, last):
                    if not last:
                        rsqrt(i + 1, 1 - u)
                    pool.wait_ge(stored, 16 * (2 + 4 * i))
                    pool.sem_inc(sfree, 1)
                    pool.wait_ge(st_act, i + 1)
                    pool.wait_ge(st_dve, i + 1)
                    settle(g, pool)
                    pool.dma_start(g.qaT.rearrange("(c p) t -> p c t", p=P)[:, :, bass.ds(i * P, P)], qkT[:, u, 0:4, :]).then_inc(stored, 16)
                    pool.dma_start(g.kaT[:, bass.ds((i + 1) * P, P)], qkT[:, u, 4, :]).then_inc(stored, 16)
                    pool.dma_start(g.va[bass.ds((i + 1) * P, P), :], va[:, u, :]).then_inc(stored, 16)
                    pool.dma_start(g.hg5[bass.ds(i * P, P), :, :], hx[:, u, :, :]).then_inc(stored, 16)
                rsqrt(0, 0)
                pairs(pool, NB, step)
                pool.wait_ge(stored, 16 * (2 + 4 * NB))

            @block.scalar
            def _(act):
                act.sem_inc(act_evac, 5)
                act.wait_ge(lb_loaded, 32)
                act.wait_ge(lb_ready, 1)
                for r in range(2):
                    last = nc.scalar.activation(lb[:, r, :], lb[:, r, :], ACT.Exp)
                last.then_inc(lb_exp, 1)

                def norm(i, u, uses):
                    act.wait_ge(x_loaded[u], 16 * uses)
                    nc.scalar.activation(junk[:], xb[:, u, :], ACT.Square, accum_out=st[:, u, 0:1]).then_inc(sumsq, 1)
                    act.wait_ge(rs, i + 1)
                    act.wait_ge(xn_free, i + 1)
                    nc.scalar.activation(xn[:], xb[:, u, :], ACT.Copy, scale=st[:, u, 2:3]).then_inc(xn_ready, 1)

                def step(i, u, uses, last):
                    if not last:
                        norm(i + 1, 1 - u, uses + u)
                    act.wait_ge(g_done, 6 * i + 1)
                    act.wait_ge(sfree, i + 1)
                    nc.scalar.activation(qkT[:, u, 0:4, :], pg[:, 0, :].rearrange("p (c t) -> p c t", c=4), ACT.Copy, scale=HD ** -0.5).then_inc(act_evac, 1)
                    act.wait_ge(g_done, 6 * i + 2)
                    nc.scalar.activation(qkT[:, u, 4, :], pg[:, 1, 0:P], ACT.Copy)
                    nc.scalar.activation(va[:, u, :], pg[:, 1, P:2 * P], ACT.Copy).then_inc(act_evac, 1)
                    for n, q in enumerate((2, 3, 5)):
                        act.wait_ge(g_done, 6 * i + q + 1)
                        nc.scalar.activation(sg[:, n, :], pg[:, q, :], ACT.Sigmoid).then_inc(act_evac, 1)
                    act.wait_ge(f_ready, i + 1)
                    nc.scalar.activation(hx[:, u, 2, :], fb[:], ACT.Ln).then_inc(st_act, 1)
                norm(0, 0, 1)
                pairs(act, NB, step)

            @block.tensor
            def _(pe):
                pe.wait_ge(g.win1_loaded, 16)

                def turn(i, u):
                    pe.wait_ge(xn_ready, i + 1)
                    pe.wait_ge(hT_ready, i + 1)
                    for k in range(KD):
                        last = nc.tensor.transpose(pt[:, k // 4, (k % 4) * P:(k % 4 + 1) * P], xn[:, k * P:(k + 1) * P], g.square[:, C_ID, :])
                    last.then_inc(t_done, 1)

                def step(i, u, uses, last):
                    pe.wait_ge(hT_ready, i + 2)
                    for q in range(6):
                        pe.wait_ge(act_evac, 5 * i + (1, 2, 3, 4, 4, 5)[q])
                        if q in (2, 4, 5):
                            pe.wait_ge(dve_evac, 3 * i + {2: 1, 4: 2, 5: 3}[q])
                        if q == 0:
                            for c in range(4):
                                for k in range(KD):
                                    mm = nc.tensor.matmul(pg[:, 0, c * P:(c + 1) * P], g.win1[:, k, c * P:(c + 1) * P], hT[:, u, k, :],
                                                          start=(k == 0), stop=(k == KD - 1))
                        elif q == 1:
                            for k in range(KD):
                                nc.tensor.matmul(pg[:, 1, 0:P], g.win1[:, k, AW:AW + P], hT[:, u, k, :], start=(k == 0), stop=(k == KD - 1))
                            for k in range(KD):
                                mm = nc.tensor.matmul(pg[:, 1, P:2 * P], hT[:, u, k, :], g.win1[:, k, AW + P:AW + 2 * P],
                                                      start=(k == 0), stop=(k == KD - 1))
                        else:
                            at = AW + 2 * KVW + (q - 2) * HW_
                            for k in range(KD):
                                mm = nc.tensor.matmul(pg[:, q, :], hT[:, u, k, :], g.win1[:, k, at:at + HW_], start=(k == 0), stop=(k == KD - 1))
                        mm.then_inc(g_done, 1)
                        if q == 2 and not last:
                            turn(i + 1, 1 - u)
                turn(0, 0)
                pairs(pe, NB, step)

            @block.vector
            def _(v):
                v.sem_inc(x_free, 2)
                v.sem_inc(xn_free, 1)
                v.sem_inc(hT_ready, 1)
                v.sem_inc(dve_evac, 3)
                v.sem_inc(sfree, 1)
                v.wait_ge(lb_loaded, 32)
                nc.vector.tensor_tensor(lb[:, 2, :], lbr[:, 0, :], lbr[:, 1, :], ALU.max)
                v.drain()
                nc.vector.tensor_tensor(lb[:, 0, :], lbr[:, 0, :], lb[:, 2, :], ALU.subtract)
                nc.vector.tensor_tensor(lb[:, 1, :], lbr[:, 1, :], lb[:, 2, :], ALU.subtract).then_inc(lb_ready, 1)
                v.wait_ge(lb_exp, 1)
                nc.vector.tensor_tensor(lb[:, 1, :], lb[:, 0, :], lb[:, 1, :], ALU.add)
                v.drain()
                nc.vector.reciprocal(lb[:, 2, :], lb[:, 1, :])
                v.drain()
                nc.vector.tensor_tensor(lb[:, 0, :], lb[:, 0, :], lb[:, 2, :], ALU.mult)
                v.drain()
                nc.vector.tensor_scalar(lb[:, 1, :], lb[:, 0, :], -1.0, 1.0, ALU.mult, ALU.add)

                def norm(i, u):
                    v.wait_ge(sumsq, i + 1)
                    nc.vector.tensor_scalar(st[:, u, 1:2], st[:, u, 0:1], 1.0 / D, EPS, ALU.mult, ALU.add).then_inc(msd, 1)
                    v.wait_ge(xn_ready, i + 1)
                    v.sem_inc(x_free, 1)
                    v.wait_ge(t_done, i + 1)
                    v.sem_inc(xn_free, 1)
                    for k in range(KD):
                        last = nc.vector.tensor_scalar(hT[:, u, k, :], pt[:, k // 4, (k % 4) * P:(k % 4 + 1) * P],
                                                       g.scale[:, 0, k:k + 1], g.shift[:, 0, k:k + 1], ALU.mult, ALU.add)
                    last.then_inc(hT_ready, 1)

                def step(i, u, uses, last):
                    if not last:
                        norm(i + 1, 1 - u)
                    v.wait_ge(sfree, i + 1)
                    v.wait_ge(act_evac, 5 * i + 5 + 3)
                    nc.vector.tensor_tensor(hx[:, u, 0, :], pg[:, 2, :], sg[:, 0, :], ALU.mult).then_inc(dve_evac, 1)
                    v.wait_ge(act_evac, 5 * i + 5 + 4)
                    nc.vector.tensor_tensor(fb[:], sg[:, 1, :], lb[:, 1, :], ALU.mult)
                    v.wait_ge(g_done, 6 * i + 5)
                    nc.vector.tensor_copy(hx[:, u, 3, :], pg[:, 4, :]).then_inc(dve_evac, 1)
                    v.drain()
                    nc.vector.tensor_tensor(fb[:], fb[:], lb[:, 0, :], ALU.add).then_inc(f_ready, 1)
                    v.drain()
                    nc.vector.tensor_scalar(hx[:, u, 1, :], fb[:], -1.0, 1.0, ALU.mult, ALU.add)
                    v.wait_ge(act_evac, 5 * i + 5 + 5)
                    nc.vector.tensor_tensor(hx[:, u, 4, :], pg[:, 5, :], sg[:, 2, :], ALU.mult).then_inc(dve_evac, 1)
                    v.drain().then_inc(st_dve, 1)
                norm(0, 0)
                pairs(v, NB, step)


def overlapped(eng, n, step, ring=2):
    step((0, 0, 1), None)
    with eng.Fori(0, n // ring - 1) as j:
        for m in range(1, ring + 1):
            step((ring * j + m, m % ring, j + 1 + m // ring), (ring * j + m - 1, m - 1, j + 1))
    for i in range(n - ring + 1, n):
        step((i, i % ring, i // ring + 1), (i - 1, (i - 1) % ring, (i - 1) // ring + 1))
    step(None, (n - 1, (n - 1) % ring, n // ring))


def staged(eng, n, step):
    step((0, 0, 1), None, None)
    step((1, 1, 1), (0, 0, 1), None)
    with eng.Fori(0, n // 2 - 1) as j:
        step((2 * j + 2, 0, j + 2), (2 * j + 1, 1, j + 1), (2 * j, 0, j + 1))
        step((2 * j + 3, 1, j + 2), (2 * j + 2, 0, j + 2), (2 * j + 1, 1, j + 1))
    step(None, (n - 1, 1, n // 2), (n - 2, 0, n // 2))
    step(None, None, (n - 1, 1, n // 2))


def stage_mix(nc, g):
    with ExitStack() as x:
        sb = lambda n, s, d=F32: x.enter_context(nc.sbuf_tensor(n, s, d))
        sem = x.enter_context(semaphores(nc, "mix"))
        wout = sb("m_wout", [P, KD, D])
        wr = sb("m_wr", [P, KD, NG + NE])
        br = sb("m_br", [P, NG + NE])
        alibi = sb("m_alibi", [P, AH, 2 * P])
        sinks = sb("m_sinks", [P, AH])
        aon = sb("m_aon", [P, AW])
        hon = sb("m_hon", [P, HW_])
        qT = sb("m_qT", [HD + 1, 2, AH, P])
        kT = sb("m_kT", [HD + 1, 2, AKV, 2 * P])
        vw = sb("m_vw", [P, 2, 2, KVW])
        hx = sb("m_hx", [P, 2, 5, HW_])
        xb = sb("m_xb", [P, 2, D])
        S = sb("m_scores", [P, 2, 2 * P])
        Pb = sb("m_probs", [P, 2, 2 * P])
        PT = sb("m_probsT", [P, 2, 2 * P])
        E = sb("m_exps", [P, 3, HW_])
        dec = sb("m_decay", [P, HH * NCH])
        Q = sb("m_decayed", [P, 3, HW_])
        QT = sb("m_decayedT", [P, 2, HW_])
        A = sb("m_aT", [P, HW_])
        St = sb("m_state", [P, 2, NCH, HW_])
        at = sb("m_att", [P, AW])
        junk = sb("m_junk", [P, D])
        mixin = sb("m_mixin", [P, D])
        mixT = sb("m_mixT", [P, KD, P])
        mo = sb("m_mo", [P, D])
        x1 = sb("m_x1", [P, 2, D])
        xn = sb("m_xn", [P, 2, D])
        h2T = sb("m_h2T", [P, KD, P])
        sm = sb("m_small", [P, 16, AH])
        half = sb("m_half", [P, AH])
        bank = [x.enter_context(nc.psum_tensor(f"m_bank{b}", [P, 512], F32)) for b in range(8)]
        B0, B1, BS0, BS1, BPT, BO, X0, W0 = bank
        MX, NM, L, ES, RL, SSA, MSA, RSA, SSH, MSH, RSH, SST, MST, RST, SSX, RSX = range(16)
        names = ("w_loaded cum_done exps_done exps_read decayed qk_done s_read nm_ready p_ready tp_done pt_read pv_done "
                 "dT_done dT_read a_done a_read kv_done kv_read oh_done oh_read sink_arg sink_exp at_ready ssa_ready msa_ready rsa_ready "
                 "ssh_ready msh_ready rsh_ready mixin_ready mixT_done mixT_read wo_done wo_read sst_ready mst_ready rst_ready x1_ready "
                 "ssx_ready msx_ready rsx_ready xn_ready h2_done h2_read logit_done logit_read stored half_ready loads_free front_free x1_free neg_ready").split()
        s = {n: sem(n) for n in names}
        loaded, x_loaded = ([sem(f"{n}_{u}") for u in range(2)] for n in ("block_loaded", "x_loaded"))
        gelem = lambda ap, n: ap.rearrange("p (h d) -> p h d", h=n)

        with nc.Block() as block:
            @block.sync
            def _(sp):
                sp.dma_start(wout[:], g.w_out[0].rearrange("(k p) n -> p k n", p=P)).then_inc(s["w_loaded"], 16)
                sp.dma_start(wr[:, :, 0:NG], g.w_router_group[0].rearrange("(k p) n -> p k n", p=P)).then_inc(s["w_loaded"], 16)
                sp.dma_start(wr[:, :, NG:], g.w_router_expert[0].rearrange("(k p) n -> p k n", p=P)).then_inc(s["w_loaded"], 16)
                for dst, src in ((br[:, 0:NG], g.b_router_group[0:1, :]), (br[:, NG:], g.b_router_expert[0:1, :]), (sinks[:], g.attn_sinks[0:1, :]),
                                 (aon[:], g.attn_out_norm[0:1, :]), (hon[:], g.hgrn_out_norm[0:1, :])):
                    sp.dma_start(dst, src.to_broadcast(list(dst.shape))).then_inc(s["w_loaded"], 16)
                sp.dma_start(alibi[:], g.c_alibi[:, :, :]).then_inc(s["w_loaded"], 16)

                def load(i, u, uses, last):
                    sp.wait_ge(s["front_free"], i + 1)
                    sp.dma_start(qT[0:HD, u, :, :], g.qaT.rearrange("(h d) t -> d h t", d=HD)[:, :, bass.ds(i * P, P)]).then_inc(loaded[u], 16)
                    sp.dma_start(kT[0:HD, u, :, :], g.kaT.rearrange("(h d) t -> d h t", d=HD)[:, :, bass.ds(i * P, 2 * P)]).then_inc(loaded[u], 16)
                    for n in range(AKV):
                        sp.dma_start(kT[HD:HD + 1, u, n, :], g.c_padflag[:, bass.ds(i * P + LEFT * CW - P, 2 * P)]).then_inc(loaded[u], 16)
                    sp.dma_start(vw[:, u, :, :], g.va[bass.ds(i * P, 2 * P), :].rearrange("(c p) n -> p c n", p=P)).then_inc(loaded[u], 16)
                    sp.dma_start(hx[:, u, :, :], g.hg5[bass.ds(i * P, P), :, :]).then_inc(loaded[u], 16)
                    sp.wait_ge(s["loads_free"], i + 1)
                    sp.dma_start(xb[:, u, :], g.x[0, bass.ds(i * P, P), :]).then_inc(x_loaded[u], 16)
                pairs(sp, NB, load)

            @block.gpsimd
            def _(pool):
                nc.gpsimd.memset(half[:], -0.5).then_inc(s["half_ready"], 1)
                nc.gpsimd.memset(St[:, 0, 0, :], 0.0).then_inc(s["neg_ready"], 1)
                nc.gpsimd.memset(A[:], 0.0).then_inc(s["neg_ready"], 1)
                pool.wait_ge(s["neg_ready"], 2)
                nc.gpsimd.memset(qT[HD:HD + 1, :, :, :], NEG).then_inc(s["neg_ready"], 1)
                pool.wait_ge(s["half_ready"], 1)

                def power(wait, i, src, dst, n, done):
                    pool.wait_ge(s[wait], i + 1)
                    nc.gpsimd.tensor_tensor(sm[:, dst, 0:n], sm[:, src, 0:n], half[:, 0:n], ALU.pow).then_inc(s[done], 1)

                def step(f, t, l):
                    if l:
                        power("mst_ready", l[0], MST, RST, 1, "rst_ready")
                    if f:
                        i, u, uses = f
                        pool.wait_ge(loaded[u], 96 * uses)
                        pool.wait_ge(s["exps_done"], i + 1)
                        pool.wait_ge(s["kv_done"], NCH * i + 1)
                        for n, src in enumerate((0, 1, 1)):
                            product = nc.gpsimd.tensor_tensor(Q[:, n, :], hx[:, u, src, :], E[:, n, :], ALU.mult)
                        product.then_inc(s["decayed"], 1)
                    if l:
                        i, u, uses = l
                        power("msx_ready", i, SSX, RSX, 1, "rsx_ready")
                        pool.wait_ge(s["xn_ready"], i + 1)
                        settle(g, pool)
                        pool.dma_start(g.x1[bass.ds(i * P, P), :], x1[:, u, :]).then_inc(s["stored"], 16)
                        pool.dma_start(g.xn2[bass.ds(i * P, P), :], xn[:, u, :]).then_inc(s["stored"], 16)
                    if f:
                        i, u, uses = f
                        power("msa_ready", i, MSA, RSA, 1, "rsa_ready")
                        power("msh_ready", i, MSH, RSH, HH, "rsh_ready")
                    if l:
                        pool.wait_ge(s["stored"], 32 * (l[0] + 1))
                        pool.sem_inc(s["x1_free"], 1)
                staged(pool, NB, step)

            @block.tensor
            def _(pe):
                pe.wait_ge(s["w_loaded"], 16 * 9)
                pe.wait_ge(s["neg_ready"], 3)

                def cum(i, u, uses):
                    pe.wait_ge(loaded[u], 96 * uses)
                    pe.wait_ge(s["oh_read"], i + 1)
                    pe.wait_ge(s["kv_read"], NCH * i + 1)
                    lf = hx[:, u, 2, :]
                    nc.tensor.matmul(B0[:, :], g.square[:, C_TRI, :], lf, start=True, stop=True)
                    nc.tensor.matmul(B1[:, :], g.square[:, C_AFTER, :], lf, start=True, stop=True)
                    pe.wait_ge(s["pt_read"], AH * i + 1)
                    for h in range(HH):
                        mm = nc.tensor.matmul(BPT[:, NCH * h:NCH * h + NCH], hx[:, u, 2, h * HK:(h + 1) * HK], g.square[:, C_CHUNK, 0:NCH],
                                              start=True, stop=True)
                    mm.then_inc(s["cum_done"], 1)

                def qk(i, u, h):
                    pe.wait_ge(s["s_read"], AH * i + h + 1)
                    nc.tensor.matmul((BS0, BS1)[h % 2][:, 0:2 * P], qT[:, u, h, :], kT[:, u, h // (AH // AKV), :],
                                     start=True, stop=True).then_inc(s["qk_done"], 1)

                def turn_p(i, u, h):
                    pe.wait_ge(s["p_ready"], AH * i + h + 3)
                    if h == 0:
                        pe.wait_ge(s["exps_done"], i + 1)
                    pe.wait_ge(s["pt_read"], AH * i + h + 1)
                    for c in range(2):
                        mm = nc.tensor.transpose(BPT[:, c * P:(c + 1) * P], Pb[:, h % 2, c * P:(c + 1) * P], g.square[:, C_ID, :])
                    mm.then_inc(s["tp_done"], 1)

                def pv(i, u, h):
                    if h == 0:
                        pe.wait_ge(s["at_ready"], i + 1)
                    pe.wait_ge(s["pt_read"], AH * i + h + 2)
                    n = h // (AH // AKV)
                    for c in range(2):
                        mm = nc.tensor.matmul(BO[:, h * HD:(h + 1) * HD], PT[:, h % 2, c * P:(c + 1) * P], vw[:, u, c, n * HD:(n + 1) * HD],
                                              start=(c == 0), stop=(c == 1))
                    mm.then_inc(s["pv_done"], 1)

                def turn_d(i, u):
                    pe.wait_ge(s["decayed"], i + 1)
                    for n, b in enumerate((B0, B1)):
                        for h in range(HH):
                            mm = nc.tensor.transpose(b[:, h * HK:(h + 1) * HK], Q[:, n, h * HK:(h + 1) * HK], g.square[:, C_ID, :])
                    mm.then_inc(s["dT_done"], 1)

                def intra(i, u):
                    pe.wait_ge(s["dT_read"], i + 1)
                    for h in range(HH):
                        mm = nc.tensor.matmul(B0[:, h * P:(h + 1) * P], QT[:, 1, h * HK:(h + 1) * HK], QT[:, 0, h * HK:(h + 1) * HK], start=True, stop=True)
                    mm.then_inc(s["a_done"], 1)

                def kv(i, u, j):
                    if j == 1:
                        pe.wait_ge(s["a_read"], i + 1)
                    if j > 1:
                        pe.wait_ge(s["kv_read"], NCH * i + j)
                    r = slice(CH * j, CH * j + CH)
                    for h in range(HH):
                        c = slice(h * HK, (h + 1) * HK)
                        mm = nc.tensor.matmul((B1, B0)[j % 2][:, c], Q[r, 2, c], hx[r, u, 3, c], start=True, stop=True, tile_position=(CH * j, 0))
                    mm.then_inc(s["kv_done"], 1)

                def hgrn_out(i, u):
                    pe.wait_ge(s["a_read"], i + 1)
                    pe.wait_ge(s["kv_read"], NCH * i + NCH)
                    for h in range(HH):
                        c = slice(h * HK, (h + 1) * HK)
                        nc.tensor.matmul(B1[:, c], A[:, c], hx[:, u, 3, c], start=True, stop=True)
                        for j in range(NCH):
                            mm = nc.tensor.matmul(B1[CH * j:CH * j + CH, c], QT[:, 0, h * HK + CH * j:h * HK + CH * j + CH], St[:, u, j, c],
                                                  start=False, stop=True, skip_group_check=True, tile_position=(0, CH * j))
                    mm.then_inc(s["oh_done"], 1)

                def turn_mix(i, u):
                    pe.wait_ge(s["mixin_ready"], i + 1)
                    pe.wait_ge(s["logit_read"], i + 1)
                    for k in range(KD):
                        mm = nc.tensor.transpose((X0, W0)[k // 4][:, (k % 4) * P:(k % 4 + 1) * P], mixin[:, k * P:(k + 1) * P], g.square[:, C_ID, :])
                    mm.then_inc(s["mixT_done"], 1)

                def out_product(i, u, n):
                    pe.wait_ge(s["mixT_read"], i + 1)
                    for k in range(KD):
                        mm = nc.tensor.matmul((W0, X0)[n][:, :], mixT[:, k, :], wout[:, k, n * 512:(n + 1) * 512], start=(k == 0), stop=(k == KD - 1))
                    mm.then_inc(s["wo_done"], 1)

                def turn_h2(i, u):
                    pe.wait_ge(s["xn_ready"], i + 1)
                    for k in range(KD):
                        mm = nc.tensor.transpose((X0, W0)[k // 4][:, (k % 4) * P:(k % 4 + 1) * P], xn[:, u, k * P:(k + 1) * P], g.square[:, C_ID, :])
                    mm.then_inc(s["h2_done"], 1)

                def router(i, u):
                    pe.wait_ge(s["h2_read"], i + 1)
                    for k in range(KD):
                        mm = nc.tensor.matmul(X0[:, 0:NG + NE], h2T[:, k, :], wr[:, k, :], start=(k == 0), stop=(k == KD - 1))
                    mm.then_inc(s["logit_done"], 1)

                def step(f, t, l):
                    if f:
                        cum(*f)
                        qk(*f[:2], 0)
                        qk(*f[:2], 1)
                    for h in range(AH):
                        if f:
                            turn_p(*f[:2], h)
                            if h + 2 < AH:
                                qk(*f[:2], h + 2)
                            if h:
                                pv(*f[:2], h - 1)
                        if f and h == 1:
                            turn_d(*f[:2])
                        if f and h == 2:
                            intra(*f[:2])
                        if f and 3 <= h < 7:
                            kv(*f[:2], h - 3)
                        if l and h == 4:
                            turn_h2(*l[:2])
                        if l and h == 6:
                            router(*l[:2])
                    if f:
                        pv(*f[:2], AH - 1)
                    if t:
                        turn_mix(*t[:2])
                    if f:
                        hgrn_out(*f[:2])
                    if t:
                        out_product(*t[:2], 0)
                        out_product(*t[:2], 1)
                staged(pe, NB, step)

            @block.scalar
            def _(act):
                act.sem_inc(s["pt_read"], 1)
                act.sem_inc(s["p_ready"], 2)

                def exps(i, u):
                    act.wait_ge(s["cum_done"], i + 1)
                    act.wait_ge(s["exps_read"], i + 1)
                    nc.scalar.activation(E[:, 0, :], B0[:, :], ACT.Exp)
                    nc.scalar.activation(E[:, 1, :], B0[:, :], ACT.Exp, scale=-1.0)
                    nc.scalar.activation(E[:, 2, :], B1[:, :], ACT.Exp)
                    nc.scalar.activation(dec[:], BPT[:, 0:HH * NCH], ACT.Exp).then_inc(s["exps_done"], 1)

                def prob(i, u, h):
                    act.wait_ge(s["nm_ready"], AH * i + h + 1)
                    act.wait_ge(s["tp_done"], AH * i + h + 1)
                    nc.scalar.activation(Pb[:, h % 2, :], S[:, h % 2, :], ACT.Exp, bias=sm[:, NM, h:h + 1], accum_out=sm[:, L, h:h + 1]).then_inc(s["p_ready"], 1)

                def probT(i, u, h):
                    act.wait_ge(s["tp_done"], AH * i + h + 3)
                    act.wait_ge(s["pv_done"], AH * i + h + 1)
                    nc.scalar.activation(PT[:, h % 2, :], BPT[:, 0:2 * P], ACT.Copy).then_inc(s["pt_read"], 1)

                def step(f, t, l):
                    if f:
                        exps(*f[:2])
                        prob(*f[:2], 0)
                    for h in range(AH):
                        if f:
                            if h + 1 < AH:
                                prob(*f[:2], h + 1)
                            probT(*f[:2], h)
                        if l and h == 1:
                            i, u, _ = l
                            act.wait_ge(s["x1_ready"], i + 1)
                            nc.scalar.activation(junk[:], x1[:, u, :], ACT.Square, accum_out=sm[:, SSX, 0:1]).then_inc(s["ssx_ready"], 1)
                        if l and h == 3:
                            i, u, _ = l
                            act.wait_ge(s["rsx_ready"], i + 1)
                            nc.scalar.activation(xn[:, u, :], x1[:, u, :], ACT.Copy, scale=sm[:, RSX, 0:1]).then_inc(s["xn_ready"], 1)
                    if f:
                        i, u, _ = f
                        act.wait_ge(s["sink_arg"], i + 1)
                        nc.scalar.activation(sm[:, ES, :], sm[:, ES, :], ACT.Exp).then_inc(s["sink_exp"], 1)
                        act.wait_ge(s["at_ready"], i + 2)
                        nc.scalar.activation(junk[:, 0:AW], at[:], ACT.Square, accum_out=sm[:, SSA, 0:1]).then_inc(s["ssa_ready"], 1)
                        act.drain()
                        act.wait_ge(s["oh_done"], i + 1)
                        for h in range(HH):
                            last = nc.scalar.activation(junk[:, h * HK:(h + 1) * HK], B1[:, h * HK:(h + 1) * HK], ACT.Square, accum_out=sm[:, SSH, h:h + 1])
                        last.then_inc(s["ssh_ready"], 1)
                    if t:
                        i = t[0]
                        act.wait_ge(s["wo_done"], 2 * i + 1)
                        nc.scalar.activation(mo[:, 0:512], W0[:, :], ACT.Copy).then_inc(s["wo_read"], 1)
                        act.wait_ge(s["wo_done"], 2 * i + 2)
                        nc.scalar.activation(mo[:, 512:D], X0[:, :], ACT.Copy).then_inc(s["wo_read"], 1)
                        act.wait_ge(s["wo_read"], 2 * i + 2)
                        nc.scalar.activation(junk[:], mo[:], ACT.Square, accum_out=sm[:, SST, 0:1]).then_inc(s["sst_ready"], 1)
                staged(act, NB, step)

            @block.vector
            def _(v):
                v.sem_inc(s["loads_free"], 2)
                v.sem_inc(s["front_free"], 2)
                v.sem_inc(s["x1_free"], 2)
                for n in "exps_read at_ready oh_read logit_read".split():
                    v.sem_inc(s[n], 1)
                v.sem_inc(s["kv_read"], 1)
                v.sem_inc(s["kv_done"], 1)
                v.sem_inc(s["s_read"], 2)
                v.sem_inc(s["tp_done"], 2)
                v.sem_inc(s["pv_done"], 2)
                v.wait_ge(s["w_loaded"], 16 * 9)
                v.wait_ge(s["neg_ready"], 3)

                def rowmax(i, u, h):
                    v.wait_ge(s["qk_done"], AH * i + h + 1)
                    v.wait_ge(s["p_ready"], AH * i + h + 1)
                    settle(g, v)
                    nc.vector.tensor_tensor_reduce(S[:, h % 2, :], (BS0, BS1)[h % 2][:, 0:2 * P], alibi[:, h, :], 1.0, sinks[:, h:h + 1],
                                                   ALU.add, ALU.max, sm[:, MX, h:h + 1]).then_inc(s["s_read"], 1)
                    v.drain()
                    nc.vector.tensor_scalar(sm[:, NM, h:h + 1], sm[:, MX, h:h + 1], -1.0, None, ALU.mult).then_inc(s["nm_ready"], 1)

                def update(i, u, j):
                    v.drain()
                    v.wait_ge(s["kv_done"], NCH * i + j + 2)
                    nxt = St[:, u, j + 1, :] if j + 1 < NCH else St[:, 1 - u, 0, :]
                    for h in range(HH):
                        c = slice(h * HK, (h + 1) * HK)
                        last = nc.vector.scalar_tensor_tensor(out=nxt[:, c], in0=St[:, u, j, c], scalar=dec[:, NCH * h + j:NCH * h + j + 1],
                                                              in1=(B1, B0)[j % 2][:, c], op0=ALU.mult, op1=ALU.add)
                    last.then_inc(s["kv_read"], 1)

                def step(f, t, l):
                    if f:
                        rowmax(*f[:2], 0)
                        rowmax(*f[:2], 1)
                    for h in range(AH):
                        if f and h + 2 < AH:
                            rowmax(*f[:2], h + 2)
                        if l and h == 0:
                            i = l[0]
                            v.wait_ge(s["sst_ready"], i + 1)
                            nc.vector.tensor_scalar(sm[:, MST, 0:1], sm[:, SST, 0:1], 1.0 / D, EPS, ALU.mult, ALU.add).then_inc(s["mst_ready"], 1)
                        if l and h == 1:
                            i, u, uses = l
                            v.wait_ge(s["rst_ready"], i + 1)
                            v.wait_ge(s["x1_free"], i + 1)
                            nc.vector.scalar_tensor_tensor(out=x1[:, u, :], in0=mo[:], scalar=sm[:, RST, 0:1], in1=g.gate[:, 0, :], op0=ALU.mult, op1=ALU.mult)
                            v.drain()
                            v.wait_ge(x_loaded[u], 16 * uses)
                            nc.vector.tensor_tensor(x1[:, u, :], x1[:, u, :], xb[:, u, :], ALU.add).then_inc(s["x1_ready"], 1)
                        if l and h == 2:
                            i = l[0]
                            v.wait_ge(s["ssx_ready"], i + 1)
                            nc.vector.tensor_scalar(sm[:, SSX, 0:1], sm[:, SSX, 0:1], 1.0 / D, EPS, ALU.mult, ALU.add).then_inc(s["msx_ready"], 1)
                        if f and h == 1:
                            i = f[0]
                            v.wait_ge(s["decayed"], i + 1)
                            v.sem_inc(s["exps_read"], 1)
                            v.wait_ge(s["dT_done"], i + 1)
                            nc.vector.tensor_copy(QT[:, 0, :], B0[:, :])
                            nc.vector.tensor_copy(QT[:, 1, :], B1[:, :]).then_inc(s["dT_read"], 1)
                        if f and h == 2:
                            i = f[0]
                            v.wait_ge(s["a_done"], i + 1)
                            settle(g, v)
                            nc.vector.copy_predicated(A[:].rearrange("p (h t) -> p h t", h=HH),
                                                      g.square[:, C_TRI:C_TRI + 1, :].bitcast(I32).to_broadcast([P, HH, P]),
                                                      B0[:, :].rearrange("p (h t) -> p h t", h=HH)).then_inc(s["a_read"], 1)
                        if f and 3 <= h < 7:
                            update(*f[:2], h - 3)
                        if l and h == 3:
                            v.sem_inc(s["loads_free"], 1)
                        if l and h == 4:
                            v.wait_ge(s["h2_done"], l[0] + 1)
                            for k in range(KD):
                                part = nc.vector.tensor_scalar(h2T[:, k, :], (X0, W0)[k // 4][:, (k % 4) * P:(k % 4 + 1) * P],
                                                               g.scale[:, 1, k:k + 1], g.shift[:, 1, k:k + 1], ALU.mult, ALU.add)
                            part.then_inc(s["h2_read"], 1)
                        if l and h == 6:
                            i = l[0]
                            v.wait_ge(s["logit_done"], i + 1)
                            nc.vector.tensor_tensor(g.logits[:, bass.ds(i, 1), :].rearrange("p a n -> p (a n)"), X0[:, 0:NG + NE], br[:], ALU.add).then_inc(s["logit_read"], 1)
                    if t:
                        i = t[0]
                        v.wait_ge(s["mixT_done"], i + 1)
                        nc.vector.tensor_copy(mixT[:, 0:4, :], X0[:, :].rearrange("p (k t) -> p k t", k=4))
                        nc.vector.tensor_copy(mixT[:, 4:8, :], W0[:, :].rearrange("p (k t) -> p k t", k=4)).then_inc(s["mixT_read"], 1)
                    if f:
                        i, u, _ = f
                        v.wait_ge(s["nm_ready"], AH * i + AH)
                        nc.vector.tensor_tensor(sm[:, ES, :], sinks[:], sm[:, NM, :], ALU.add).then_inc(s["sink_arg"], 1)
                        v.wait_ge(s["sink_exp"], i + 1)
                        nc.vector.tensor_tensor(sm[:, ES, :], sm[:, L, :], sm[:, ES, :], ALU.add)
                        v.drain()
                        nc.vector.reciprocal(sm[:, RL, :], sm[:, ES, :])
                        v.drain()
                        v.wait_ge(s["pv_done"], AH * i + AH + 2)
                        nc.vector.tensor_tensor(gelem(at[:], AH), gelem(BO[:, :], AH), sm[:, RL, :].unsqueeze(2).to_broadcast([P, AH, HD]), ALU.mult).then_inc(s["at_ready"], 1)
                        v.wait_ge(s["ssa_ready"], i + 1)
                        nc.vector.tensor_scalar(sm[:, MSA, 0:1], sm[:, SSA, 0:1], 1.0 / AW, EPS, ALU.mult, ALU.add).then_inc(s["msa_ready"], 1)
                        v.wait_ge(s["ssh_ready"], i + 1)
                        nc.vector.tensor_scalar(sm[:, MSH, 0:HH], sm[:, SSH, 0:HH], 1.0 / HK, EPS, ALU.mult, ALU.add).then_inc(s["msh_ready"], 1)
                        v.wait_ge(s["rsa_ready"], i + 1)
                        nc.vector.scalar_tensor_tensor(out=mixin[:, 0:AW], in0=at[:], scalar=sm[:, RSA, 0:1], in1=aon[:], op0=ALU.mult, op1=ALU.mult)
                        v.wait_ge(s["rsh_ready"], i + 1)
                        for h in range(HH):
                            c = slice(h * HK, (h + 1) * HK)
                            last = nc.vector.scalar_tensor_tensor(out=mixin[:, AW + h * HK:AW + (h + 1) * HK], in0=B1[:, c], scalar=sm[:, RSH, h:h + 1],
                                                                  in1=hon[:, c], op0=ALU.mult, op1=ALU.mult)
                        last.then_inc(s["oh_read"], 1)
                        v.drain()
                        nc.vector.tensor_tensor(mixin[:, AW:], mixin[:, AW:], hx[:, u, 4, :], ALU.mult).then_inc(s["mixin_ready"], 1)
                        v.drain().then_inc(s["front_free"], 1)
                staged(v, NB, step)



def stage_route(nc, g):
    with ExitStack() as x:
        sb = lambda n, s, d=F32: x.enter_context(nc.sbuf_tensor(n, s, d))
        sem = x.enter_context(semaphores(nc, "route"))
        ec = sb("r_consts", [P, NE * 4 + 64])
        mg = sb("r_maxg", [P, NB])
        gt = sb("r_group", [P, NB, NG])
        go = sb("r_onegroup", [P, NB, NG])
        lm = sb("r_masked", [P, NB, NE])
        t32 = sb("r_tmp", [P, NB, NE])
        oh = sb("r_onehot", [P, 2, NB, NE])
        both = sb("r_both", [P, NB, NE])
        mx = sb("r_max", [P, 2, NB])
        first = sb("r_first", [P, NB])
        gw = sb("r_gw", [P, 4, NB])
        base = sb("r_base", [P, NB + 1, NE])
        cmp_ = sb("r_cmp", [P, NE, NE])
        ov = sb("r_over", [P, 4, NE])
        rk = sb("r_rank", [P, 4, NB])
        tok = sb("r_token", [P, NB], I32)
        zero = sb("r_zero", [NT, P], I32)
        pc = x.enter_context(nc.psum_tensor("r_before", [P, NB, NE], F32))
        pt = x.enter_context(nc.psum_tensor("r_total", [P, NB, NE], F32))
        consts, arg, expd, arg2, exp2, onehots, counted, routed, zeroed, scattered, tokens = map(
            sem, "consts group_arg group_exp pair_arg pair_exp onehots counted routed ids_zeroed ids_scattered token_ids".split())
        with nc.Block() as block:
            @block.sync
            def _(sp):
                sp.dma_start(ec[:], g.c_expert[:, :]).then_inc(consts, 16)

            @block.scalar
            def _(act):
                act.wait_ge(arg, 1)
                nc.scalar.activation(gt[:], gt[:], ACT.Exp).then_inc(expd, 1)
                act.wait_ge(arg2, 1)
                nc.scalar.activation(gw[:, 1, :], gw[:, 1, :], ACT.Exp).then_inc(exp2, 1)

            @block.tensor
            def _(pe):
                pe.wait_ge(onehots, 1)
                nc.tensor.matmul(pc[:], g.square[:, C_BEFORE, :], both[:], start=True, stop=True)
                nc.tensor.matmul(pt[:], g.square[:, C_ONES, :], both[:], start=True, stop=True).then_inc(counted, 1)

            @block.gpsimd
            def _(pool):
                nc.gpsimd.iota(tok[:], pattern=[[P, NB]], base=0, channel_multiplier=1).then_inc(tokens, 1)
                nc.gpsimd.memset(zero[:], 0).then_inc(tokens, 1)
                pool.wait_ge(tokens, 2)
                pool.dma_start(g.ids.rearrange("(t p) o -> t (p o)", p=P), zero[:]).then_inc(zeroed, 16)
                pool.wait_ge(zeroed, 16)
                pool.wait_ge(routed, 1)
                for n in range(2):
                    for b in range(NB):
                        pool.indirect_dma_start(out=g.ids[:, :], out_offset=bass.IndirectOffsetOnAxis(ap=g.route[:, b, n:n + 1].bitcast(U32), axis=0),
                                                in_=tok[:, b:b + 1], in_offset=None).then_inc(scattered, 16)
                pool.wait_ge(scattered, 16 * 2 * NB)

            @block.vector
            def _(v):
                V = nc.vector
                bc = lambda ap, n: ap.unsqueeze(2).to_broadcast([P, NB, n])
                row = lambda at, n: ec[:, at:at + n].unsqueeze(1).to_broadcast([P, NB, n])
                v.wait_ge(consts, 16)
                lg, le = g.logits[:, :, 0:NG], g.logits[:, :, NG:]
                V.tensor_reduce(mg[:], lg, AX.X, ALU.max)
                v.drain()
                V.tensor_tensor(gt[:], lg, bc(mg[:], NG), ALU.subtract)
                V.tensor_tensor(go[:], lg, bc(mg[:], NG), ALU.is_equal)
                V.tensor_scalar(ec[:, 0:NE], ec[:, 0:NE], -1.0, float(NE), ALU.mult, ALU.add)
                V.tensor_scalar(ec[:, 4 * NE:4 * NE + NG], ec[:, 4 * NE:4 * NE + NG], -1.0, float(NG), ALU.mult, ALU.add)
                v.drain().then_inc(arg, 1)
                V.tensor_tensor(go[:], go[:], row(4 * NE, NG), ALU.mult)
                v.drain()
                V.tensor_reduce(first[:], go[:], AX.X, ALU.max)
                v.drain()
                V.tensor_tensor(go[:], bc(first[:], NG), row(4 * NE, NG), ALU.is_equal)
                v.drain()
                V.tensor_scalar(go[:], go[:], -1.0, 1e30, ALU.add, ALU.mult)
                v.drain()
                V.tensor_tensor(lm[:].rearrange("p b (a e) -> p b a e", a=NG), le.rearrange("p b (a e) -> p b a e", a=NG),
                                go[:].unsqueeze(3).to_broadcast([P, NB, NG, EPG]), ALU.add)
                v.drain()
                for n in range(2):
                    V.tensor_reduce(mx[:, n, :], lm[:], AX.X, ALU.max)
                    v.drain()
                    V.tensor_tensor(t32[:], lm[:], bc(mx[:, n, :], NE), ALU.is_equal)
                    v.drain()
                    V.tensor_tensor(t32[:], t32[:], row(0, NE), ALU.mult)
                    v.drain()
                    V.tensor_reduce(first[:], t32[:], AX.X, ALU.max)
                    v.drain()
                    V.tensor_tensor(oh[:, n, :, :], bc(first[:], NE), row(0, NE), ALU.is_equal)
                    v.drain()
                    if n == 0:
                        V.tensor_scalar(t32[:], oh[:, 0, :, :], -2e30, None, ALU.mult)
                        v.drain()
                        V.tensor_tensor(lm[:], lm[:], t32[:], ALU.add)
                        v.drain()
                V.tensor_tensor(both[:], oh[:, 0, :, :], oh[:, 1, :, :], ALU.add).then_inc(onehots, 1)
                v.wait_ge(expd, 1)
                V.tensor_reduce(gw[:, 0, :], gt[:], AX.X, ALU.add)
                V.tensor_tensor(gw[:, 1, :], mx[:, 1, :], mx[:, 0, :], ALU.subtract).then_inc(arg2, 1)
                v.wait_ge(exp2, 1)
                V.tensor_scalar(gw[:, 2, :], gw[:, 1, :], 1.0, None, ALU.add)
                v.drain()
                V.tensor_tensor(gw[:, 2, :], gw[:, 2, :], gw[:, 0, :], ALU.mult)
                v.drain()
                V.reciprocal(gw[:, 3, :], gw[:, 2, :])
                v.drain()
                V.tensor_copy(g.route[:, :, 2].bitcast(F32), gw[:, 3, :])
                V.tensor_tensor(g.route[:, :, 3].bitcast(F32), gw[:, 3, :], gw[:, 1, :], ALU.mult)
                V.memset(base[:, 0, :], 0.0)
                v.drain()
                v.wait_ge(counted, 1)
                for b in range(NB):
                    V.tensor_tensor(base[:, b + 1, :], base[:, b, :], pt[:, b, :], ALU.add)
                    v.drain()
                V.tensor_tensor(t32[:], base[:, 0:NB, :], pc[:], ALU.add)
                V.tensor_tensor(cmp_[:, :, 0:15], base[:, NB, :].unsqueeze(2).to_broadcast([P, NE, 15]),
                                ec[:, 2 * NE:2 * NE + 15].unsqueeze(1).to_broadcast([P, NE, 15]), ALU.is_gt)
                V.memset(ov[:, 3, :], 1.0)
                v.drain()
                V.tensor_reduce(ov[:, 0, :], cmp_[:, :, 0:15], AX.X, ALU.add)
                v.drain()
                V.tensor_tensor_scan(ov[:, 1, :], ov[:, 3, :], ov[:, 0, :], 0.0, ALU.mult, ALU.add)
                v.drain()
                V.tensor_tensor(ov[:, 2, :], ov[:, 1, :], ov[:, 0, :], ALU.subtract)
                V.tensor_tensor(cmp_[:], ov[:, 1, :].unsqueeze(1).to_broadcast([P, NE, NE]),
                                ec[:, 3 * NE:4 * NE].unsqueeze(2).to_broadcast([P, NE, NE]), ALU.is_le)
                v.drain()
                V.tensor_scalar(ov[:, 2, :], ov[:, 2, :], float(P), float((NE - 1) * P), ALU.mult, ALU.add)
                V.tensor_reduce(ov[:, 3, :], cmp_[:], AX.X, ALU.add)
                v.drain()
                V.tensor_scalar(ov[:, 3, :], ov[:, 3, :], float(NE - 1), None, ALU.min)
                V.tensor_tensor(ec[:, 0:NE], ec[:, 3 * NE:4 * NE], ec[:, 3 * NE:4 * NE], ALU.max)
                v.drain()
                V.tensor_copy(g.tile_expert[:, 0:NE], ec[:, 0:NE])
                V.tensor_copy(g.tile_expert[:, NE:NT], ov[:, 3, :])
                for n in range(2):
                    for q, other in enumerate((t32[:], row(NE, NE), ov[:, 2, :].unsqueeze(1).to_broadcast([P, NB, NE]))):
                        V.tensor_tensor(both[:], oh[:, n, :, :], other, ALU.mult)
                        v.drain()
                        V.tensor_reduce(rk[:, q, :], both[:], AX.X, ALU.add)
                        v.drain()
                    V.tensor_scalar(rk[:, 3, :], rk[:, 0, :], float(P), None, ALU.is_lt)
                    V.tensor_tensor(rk[:, 1, :], rk[:, 1, :], rk[:, 2, :], ALU.subtract)
                    v.drain()
                    V.tensor_tensor(rk[:, 1, :], rk[:, 1, :], rk[:, 3, :], ALU.mult)
                    V.tensor_tensor(rk[:, 0, :], rk[:, 0, :], rk[:, 2, :], ALU.add)
                    v.drain()
                    last = V.tensor_tensor(g.route[:, :, n], rk[:, 0, :], rk[:, 1, :], ALU.add)
                    v.drain()
                v.drain().then_inc(routed, 1)


def stage_experts(nc, g):
    RING = 4

    def rings(eng, body):
        with eng.Fori(0, NT // RING) as j:
            for u in range(RING):
                body(RING * j + u, u, j + 1)

    with ExitStack() as x:
        sb = lambda n, s, d=F32: x.enter_context(nc.sbuf_tensor(n, s, d))
        sem = x.enter_context(semaphores(nc, "experts"))
        wgu = sb("e_gateup", [P, RING, KD, 2 * FF])
        wd = sb("e_down", [P, RING, 2, D])
        ids = sb("e_ids", [P, NT], U32)
        tile_ids = sb("e_tile_ids", [P, RING], U32)
        xg = sb("e_rows", [P, RING, D])
        xT = sb("e_rowsT", [P, KD, P])
        sg = sb("e_sig", [P, FF])
        ac = sb("e_act", [P, FF])
        aT = sb("e_actT", [P, 2, P])
        ys = sb("e_out", [P, RING, D])
        px = x.enter_context(nc.psum_tensor("e_px", [P, 2, 512], F32))
        ph = x.enter_context(nc.psum_tensor("e_ph", [P, 2, 512], F32))
        pa = x.enter_context(nc.psum_tensor("e_pa", [P, 512], F32))
        py = x.enter_context(nc.psum_tensor("e_py", [P, 2, 512], F32))
        names = "w_free xT_done xT_read up_done sig_done act_ready aT_done aT_read down_done y_read".split()
        s = {n: sem(n) for n in names}
        ids_loaded = sem("ids_loaded")
        w_loaded, gathered, stored = ([sem(f"{n}_{u}") for u in range(RING)] for n in ("tile_w_loaded", "gathered", "tile_stored"))
        with nc.Block() as block:
            @block.sync
            def _(sp):
                def load(i, u, uses):
                    e = sp.value_load(g.tile_expert[0:1, bass.ds(i, 1)], min_val=0, max_val=NE - 1)
                    sp.wait_ge(s["w_free"], i + 1)
                    for n, w in enumerate((g.w_exp_gate, g.w_exp_up)):
                        sp.dma_start(wgu[:, u, :, n * FF:(n + 1) * FF], w[0, bass.ds(e, 1)].rearrange("o (k p) f -> p (o k) f", p=P)).then_inc(w_loaded[u], 16)
                    sp.dma_start(wd[:, u, :, :], g.w_exp_down[0, bass.ds(e, 1)].rearrange("o (k p) n -> p (o k) n", p=P)).then_inc(w_loaded[u], 16)
                rings(sp, load)

            @block.gpsimd
            def _(pool):
                pool.dma_start(ids[:], g.ids.rearrange("(t p) o -> p (t o)", p=P).bitcast(U32), allow_slow_non_contiguous=True).then_inc(ids_loaded, 16)
                pool.wait_ge(ids_loaded, 16)

                def gather(i, u, uses):
                    pool.wait_ge(s["xT_done"], i + 1)
                    settle(g, pool)
                    nc.gpsimd.tensor_copy(tile_ids[:, u:u + 1], ids[:, bass.ds(i, 1)])
                    pool.drain()
                    pool.indirect_dma_start(out=xg[:, u, :], out_offset=None, in_=g.xn2[:, :],
                                            in_offset=bass.IndirectOffsetOnAxis(ap=tile_ids[:, u:u + 1], axis=0)).then_inc(gathered[u], 16)
                rings(pool, gather)

            @block.tensor
            def _(pe):
                pe.sem_inc(s["xT_done"], RING)

                def turn_rows(i, u, uses):
                    pe.wait_ge(gathered[u], 16 * uses)
                    pe.wait_ge(s["xT_read"], i + 1)
                    for k in range(KD):
                        mm = nc.tensor.transpose(px[:, k // 4, (k % 4) * P:(k % 4 + 1) * P], xg[:, u, k * P:(k + 1) * P], g.square[:, C_ID, :])
                    mm.then_inc(s["xT_done"], 1)

                def step(f, t):
                    if t:
                        i, u, uses = t
                        pe.wait_ge(s["act_ready"], i + 1)
                        pe.wait_ge(s["aT_read"], i + 1)
                        for k in range(2):
                            mm = nc.tensor.transpose(pa[:, k * P:(k + 1) * P], ac[:, k * P:(k + 1) * P], g.square[:, C_ID, :])
                        mm.then_inc(s["aT_done"], 1)
                    if f:
                        i, u, uses = f
                        pe.wait_ge(w_loaded[u], 48 * uses)
                        pe.wait_ge(s["xT_read"], i + 2)
                        for k in range(KD):
                            mm = nc.tensor.matmul(ph[:, u % 2, :], xT[:, k, :], wgu[:, u, k, :], start=(k == 0), stop=(k == KD - 1))
                        mm.then_inc(s["up_done"], 1)
                        if not isinstance(i, int) or i < NT - 1:
                            turn_rows(i + 1, (u + 1) % RING, uses + (u + 1) // RING)
                    if t:
                        i, u, uses = t
                        pe.wait_ge(s["aT_read"], i + 2)
                        pe.wait_ge(s["y_read"], 2 * i + 2)
                        for n in range(2):
                            for k in range(2):
                                mm = nc.tensor.matmul(py[:, n, :], aT[:, k, :], wd[:, u, k, n * 512:(n + 1) * 512], start=(k == 0), stop=(k == 1))
                            mm.then_inc(s["down_done"], 1)
                turn_rows(0, 0, 1)
                overlapped(pe, NT, step, RING)

            @block.scalar
            def _(act):
                def step(f, t):
                    if f:
                        i, u, uses = f
                        act.wait_ge(s["up_done"], i + 1)
                        nc.scalar.activation(sg[:], ph[:, u % 2, 0:FF], ACT.Sigmoid).then_inc(s["sig_done"], 1)
                    if t:
                        i, u, uses = t
                        act.wait_ge(s["down_done"], 2 * i + 1)
                        act.wait_ge(stored[u], 16 * uses)
                        nc.scalar.activation(ys[:, u, 0:512], py[:, 0, :], ACT.Copy).then_inc(s["y_read"], 1)
                        act.wait_ge(s["down_done"], 2 * i + 2)
                        nc.scalar.activation(ys[:, u, 512:D], py[:, 1, :], ACT.Copy).then_inc(s["y_read"], 1)
                        act.wait_ge(s["y_read"], 2 * i + 4)
                        act.dma_start(g.ys[bass.ds(i * P, P), :], ys[:, u, :]).then_inc(stored[u], 16)
                overlapped(act, NT, step, RING)
                for u in range(RING):
                    act.wait_ge(stored[u], 16 * (NT // RING + 1))

            @block.vector
            def _(v):
                v.sem_inc(s["w_free"], RING)
                v.sem_inc(s["xT_read"], 1)
                v.sem_inc(s["aT_read"], 1)
                v.sem_inc(s["y_read"], 2)
                for u in range(RING):
                    v.sem_inc(stored[u], 16)

                def evac_rows(i):
                    v.wait_ge(s["xT_done"], i + 1 + RING)
                    for k in range(KD):
                        last = nc.vector.tensor_scalar(xT[:, k, :], px[:, k // 4, (k % 4) * P:(k % 4 + 1) * P],
                                                       g.scale[:, 1, k:k + 1], g.shift[:, 1, k:k + 1], ALU.mult, ALU.add)
                    last.then_inc(s["xT_read"], 1)

                def step(f, t):
                    if t:
                        i, u, uses = t
                        v.wait_ge(s["aT_done"], i + 1)
                        nc.vector.tensor_copy(aT[:], pa[:, 0:2 * P].rearrange("p (k t) -> p k t", k=2)).then_inc(s["aT_read"], 1)
                    if f:
                        i, u, uses = f
                        v.wait_ge(s["sig_done"], i + 1)
                        nc.vector.tensor_tensor(ac[:], ph[:, u % 2, 0:FF], sg[:], ALU.mult)
                        v.drain()
                        nc.vector.tensor_tensor(ac[:], ph[:, u % 2, FF:], ac[:], ALU.mult).then_inc(s["act_ready"], 1)
                        if not isinstance(i, int) or i < NT - 1:
                            evac_rows(i + 1)
                    if t:
                        i, u, uses = t
                        v.wait_ge(s["down_done"], 2 * i + 2)
                        v.sem_inc(s["w_free"], 1)
                evac_rows(0)
                overlapped(v, NT, step, RING)



def stage_combine(nc, g):
    NW = BH * HD + 2 * HD + IH * ID + ID + IH
    CB = BH * HD + 2 * HD
    with ExitStack() as x:
        sb = lambda n, s, d=F32: x.enter_context(nc.sbuf_tensor(n, s, d))
        sem = x.enter_context(semaphores(nc, "combine"))
        w = sb("b_w", [P, KD, NW])
        ng = sb("b_gain", [P, KD])
        rt = sb("b_route", [P, 2, 4], I32)
        y1 = sb("b_y1", [P, 2, D])
        y2 = sb("b_y2", [P, 2, D])
        xb = sb("b_x", [P, 2, D])
        rope = sb("b_rope", [P, 2, ROPE])
        junk = sb("b_junk", [P, D])
        x2 = sb("b_x2", [P, 2, D])
        xn = sb("b_xn", [P, 2, D])
        xT = sb("b_xT", [P, 2, KD, P])
        nat = sb("b_nat", [P, 2, NW])
        rot = sb("b_rot", [P, 4, 9, 8])
        qT = sb("b_qT", [P, 2, 4, P])
        kT = sb("b_kT", [P, 2, 4, P])
        sm = sb("b_small", [P, 8])
        half = sb("b_half", [P, 1])
        px = x.enter_context(nc.psum_tensor("b_px", [P, 2, 512], F32))
        pp = x.enter_context(nc.psum_tensor("b_pp", [P, 2, 512], F32))
        pq = x.enter_context(nc.psum_tensor("b_pq", [P, 2, 512], F32))
        names = ("w_loaded half_ready route_ready gather_free y_ready ssy_ready msy_ready rsy_ready x2_ready ssx_ready msx_ready rsx_ready xn_ready "
                 "xT_done xT_ready proj_done nat_ready rotated heads_done heads_read").split()
        s = {n: sem(n) for n in names}
        loaded, gathered, stored_f, stored_t = ([sem(f"{n}_{u}") for u in range(2)] for n in ("block_loaded", "block_gathered", "front_stored", "tail_stored"))
        with nc.Block() as block:
            @block.sync
            def _(sp):
                sp.dma_start(ng[:], g.norm_gain_2[0, :].rearrange("(k p) -> p k", p=P), allow_slow_non_contiguous=True).then_inc(s["w_loaded"], 16)
                wi = g.w_in_2[0].rearrange("(k p) n -> p k n", p=P)
                sp.dma_start(w[:, :, 0:CB], wi[:, :, W2["qb"]:W2["qb"] + CB]).then_inc(s["w_loaded"], 16)
                sp.dma_start(w[:, :, CB:], wi[:, :, W2["iq"]:W2["iq"] + NW - CB]).then_inc(s["w_loaded"], 16)

                def load(i, u, uses, last):
                    sp.wait_ge(s["gather_free"], i + 1)
                    sp.dma_start(xb[:, u, :], g.x1[bass.ds(i * P, P), :]).then_inc(loaded[u], 16)
                    sp.dma_start(rope[:, u, :], g.c_rope[bass.ds(i * P, P), :]).then_inc(loaded[u], 16)
                pairs(sp, NB, load)

            @block.gpsimd
            def _(pool):
                nc.gpsimd.memset(half[:], -0.5).then_inc(s["half_ready"], 1)
                pool.wait_ge(s["half_ready"], 1)

                def gather(i, u):
                    pool.wait_ge(s["route_ready"], i + 1)
                    settle(g, pool)
                    for n, y in enumerate((y1, y2)):
                        pool.indirect_dma_start(out=y[:, u, :], out_offset=None, in_=g.ys[:, :],
                                                in_offset=bass.IndirectOffsetOnAxis(ap=rt[:, u, n:n + 1].bitcast(U32), axis=0)).then_inc(gathered[u], 16)

                def step(f, t):
                    if f:
                        i, u, uses = f
                        if not isinstance(i, int) or i < NB - 1:
                            gather(i + 1, 1 - u)
                        pool.wait_ge(s["msy_ready"], i + 1)
                        nc.gpsimd.tensor_tensor(sm[:, 1:2], sm[:, 0:1], half[:], ALU.pow).then_inc(s["rsy_ready"], 1)
                        pool.wait_ge(s["msx_ready"], i + 1)
                        nc.gpsimd.tensor_tensor(sm[:, 3:4], sm[:, 2:3], half[:], ALU.pow).then_inc(s["rsx_ready"], 1)
                gather(0, 0)
                overlapped(pool, NB, step)

            @block.tensor
            def _(pe):
                pe.wait_ge(s["w_loaded"], 48)

                def step(f, t):
                    if t:
                        i, u, uses = t
                        pe.wait_ge(s["xn_ready"], i + 1)
                        for k in range(KD):
                            mm = nc.tensor.transpose(px[:, k // 4, (k % 4) * P:(k % 4 + 1) * P], xn[:, u, k * P:(k + 1) * P], g.square[:, C_ID, :])
                        mm.then_inc(s["xT_done"], 1)
                        pe.wait_ge(s["xT_ready"], i + 1)
                        for n, (c0, c1) in enumerate(((0, 512), (512, NW))):
                            for k in range(KD):
                                mm = nc.tensor.matmul(pp[:, n, 0:c1 - c0], xT[:, u, k, :], w[:, k, c0:c1], start=(k == 0), stop=(k == KD - 1))
                            mm.then_inc(s["proj_done"], 1)
                        pe.wait_ge(s["rotated"], i + 1)
                        pe.wait_ge(s["heads_read"], i + 1)
                        for c in range(4):
                            nc.tensor.transpose(pq[:, 0, c * P:(c + 1) * P], nat[:, u, c * P:(c + 1) * P], g.square[:, C_ID, :])
                        nc.tensor.transpose(pq[0:HD, 1, 0:P], nat[:, u, BH * HD:BH * HD + HD], g.square[:, C_ID, :])
                        for c in range(2):
                            nc.tensor.transpose(pq[:, 1, (c + 1) * P:(c + 2) * P], nat[:, u, CB + c * P:CB + (c + 1) * P], g.square[:, C_ID, :])
                        nc.tensor.transpose(pq[0:ID, 1, 3 * P:4 * P], nat[:, u, CB + 2 * P:CB + 2 * P + ID], g.square[:, C_ID, :]).then_inc(s["heads_done"], 1)
                overlapped(pe, NB, step)

            @block.scalar
            def _(act):
                def step(f, t):
                    if f:
                        i, u, uses = f
                        act.wait_ge(s["y_ready"], i + 1)
                        nc.scalar.activation(junk[:], y1[:, u, :], ACT.Square, accum_out=sm[:, 0:1]).then_inc(s["ssy_ready"], 1)
                        act.wait_ge(s["x2_ready"], i + 1)
                        nc.scalar.activation(junk[:], x2[:, u, :], ACT.Square, accum_out=sm[:, 2:3]).then_inc(s["ssx_ready"], 1)
                        act.wait_ge(s["rsx_ready"], i + 1)
                        act.wait_ge(s["xT_done"], i + 1)
                        nc.scalar.activation(xn[:, u, :], x2[:, u, :], ACT.Copy, scale=sm[:, 3:4]).then_inc(s["xn_ready"], 1)
                        act.dma_start(g.x2[bass.ds(i * P, P), :], x2[:, u, :]).then_inc(stored_f[u], 16)
                    if t:
                        i, u, uses = t
                        act.wait_ge(stored_t[u], 112 * uses)
                        act.wait_ge(s["proj_done"], 2 * i + 1)
                        nc.scalar.activation(nat[:, u, 0:512], pp[:, 0, :], ACT.Copy)
                        act.wait_ge(s["proj_done"], 2 * i + 2)
                        nc.scalar.activation(nat[:, u, 512:NW - IH], pp[:, 1, 0:NW - 512 - IH], ACT.Copy)
                        nc.scalar.activation(nat[:, u, NW - IH:NW], pp[:, 1, NW - 512 - IH:NW - 512], ACT.Copy, scale=IH ** -0.5 * ID ** -0.5).then_inc(s["nat_ready"], 1)
                        act.wait_ge(s["heads_done"], i + 1)
                        nc.scalar.activation(qT[:, u, :, :], pq[:, 0, :].rearrange("p (c t) -> p c t", c=4), ACT.Copy, scale=HD ** -0.5)
                        nc.scalar.activation(kT[:, u, 1:3, :], pq[:, 1, P:3 * P].rearrange("p (c t) -> p c t", c=2), ACT.Copy)
                        nc.scalar.activation(kT[0:HD, u, 0, :], pq[0:HD, 1, 0:P], ACT.Copy)
                        nc.scalar.activation(kT[0:ID, u, 3, :], pq[0:ID, 1, 3 * P:4 * P], ACT.Copy).then_inc(s["heads_read"], 1)
                        act.wait_ge(s["heads_read"], i + 2)
                        cols = bass.ds(i * P, P)
                        for dst, src in ((g.xn3T.rearrange("(k p) t -> p k t", p=P)[:, :, cols], xT[:, u, :, :]),
                                         (g.qbT.rearrange("(k p) t -> p k t", p=P)[:, :, cols], qT[:, u, :, :]),
                                         (g.kbT[:, cols], kT[0:HD, u, 0, :]),
                                         (g.iqT.rearrange("(k p) t -> p k t", p=P)[:, :, cols], kT[:, u, 1:3, :]),
                                         (g.ikT[:, cols], kT[0:ID, u, 3, :]),
                                         (g.vb[cols, :], nat[:, u, BH * HD + HD:CB]),
                                         (g.iw[cols, :], nat[:, u, NW - IH:NW])):
                            act.dma_start(dst, src).then_inc(stored_t[u], 16)
                overlapped(act, NB, step)
                for u in range(2):
                    act.wait_ge(stored_f[u], 16 * (NB // 2 + 1))
                    act.wait_ge(stored_t[u], 16 * 7 * (NB // 2 + 1))

            @block.vector
            def _(v):
                V = nc.vector
                v.sem_inc(s["gather_free"], 2)
                v.sem_inc(s["heads_read"], 1)
                v.sem_inc(s["xT_done"], 2)
                for u in range(2):
                    v.sem_inc(stored_t[u], 112)
                    v.sem_inc(stored_f[u], 16)
                v.wait_ge(s["w_loaded"], 48)

                def fetch_route(i, u):
                    V.tensor_copy(rt[:, u, :], g.route[:, bass.ds(i, 1), :].rearrange("p o n -> p (o n)")).then_inc(s["route_ready"], 1)

                def step(f, t):
                    if t:
                        i, u, uses = t
                        v.wait_ge(s["xT_done"], i + 3)
                        v.wait_ge(stored_t[u], 112 * uses)
                        for k in range(KD):
                            last = V.tensor_scalar(xT[:, u, k, :], px[:, k // 4, (k % 4) * P:(k % 4 + 1) * P], ng[:, k:k + 1], None, ALU.mult)
                        last.then_inc(s["xT_ready"], 1)
                    if f:
                        i, u, uses = f
                        if not isinstance(i, int) or i < NB - 1:
                            fetch_route(i + 1, 1 - u)
                        v.wait_ge(gathered[u], 32 * uses)
                        V.tensor_scalar(y1[:, u, :], y1[:, u, :], rt[:, u, 2:3].bitcast(F32), None, ALU.mult)
                        v.drain()
                        V.scalar_tensor_tensor(out=y1[:, u, :], in0=y2[:, u, :], scalar=rt[:, u, 3:4].bitcast(F32), in1=y1[:, u, :],
                                               op0=ALU.mult, op1=ALU.add).then_inc(s["y_ready"], 1)
                        v.wait_ge(s["ssy_ready"], i + 1)
                        V.tensor_scalar(sm[:, 0:1], sm[:, 0:1], 1.0 / D, EPS, ALU.mult, ALU.add).then_inc(s["msy_ready"], 1)
                        v.wait_ge(s["rsy_ready"], i + 1)
                        v.wait_ge(stored_f[u], 16 * uses)
                        V.scalar_tensor_tensor(out=x2[:, u, :], in0=y1[:, u, :], scalar=sm[:, 1:2], in1=g.gate[:, 1, :], op0=ALU.mult, op1=ALU.mult)
                        v.drain()
                        v.wait_ge(loaded[u], 32 * uses)
                        V.tensor_tensor(x2[:, u, :], x2[:, u, :], xb[:, u, :], ALU.add).then_inc(s["x2_ready"], 1)
                        v.wait_ge(s["ssx_ready"], i + 1)
                        V.tensor_scalar(sm[:, 2:3], sm[:, 2:3], 1.0 / D, EPS, ALU.mult, ALU.add).then_inc(s["msx_ready"], 1)
                    if t:
                        i, u, uses = t
                        v.wait_ge(s["nat_ready"], i + 1)
                        for at, dh, r, c in ((0, HD, 8, 0), (CB, ID, 4, 16)):
                            q = nat[:, u, at:at + 9 * dh].rearrange("p (h d) -> p h d", d=dh)
                            lo, hi = q[:, :, 0:r], q[:, :, r:2 * r]
                            cos, sin = (rope[:, u, c + k * r:c + k * r + r].unsqueeze(1).to_broadcast([P, 9, r]) for k in range(2))
                            for n, (a_, b_) in enumerate(((lo, cos), (hi, sin), (hi, cos), (lo, sin))):
                                V.tensor_tensor(rot[:, n, :, 0:r], a_, b_, ALU.mult)
                            v.drain()
                            V.tensor_tensor(lo, rot[:, 0, :, 0:r], rot[:, 1, :, 0:r], ALU.subtract)
                            V.tensor_tensor(hi, rot[:, 2, :, 0:r], rot[:, 3, :, 0:r], ALU.add)
                            v.drain()
                        v.drain().then_inc(s["rotated"], 1)
                        v.sem_inc(s["gather_free"], 1)
                fetch_route(0, 0)
                overlapped(v, NB, step)


GROUPS = T // 512


def growing(eng, unit, body):
    for q in range(GROUPS):
        start = 4 * unit * (q * (q + 1) // 2)
        with eng.Fori(0, 2) as j:
            for u in range(2):
                body(4 * q + 2 * j + u, u, 2 * q + j + 1, start + (2 * j + u) * (unit * (q + 1)), q)


def stage_index_scores(nc, g):
    with ExitStack() as x:
        sb = lambda n, s, d=F32: x.enter_context(nc.sbuf_tensor(n, s, d))
        sem = x.enter_context(semaphores(nc, "index_scores"))
        ik = sb("i_k", [P, T])
        iq = sb("i_q", [P, 2, IH, P])
        qs = sb("i_q_parts", [P, 2, IH, P])
        ks = sb("i_k_parts", [P, T])
        iw = sb("i_w", [P, 2, IH])
        caus = sb("i_causal", [P, 2, 4 * P])
        rel = sb("i_relu", [P, 4, 512])
        sc = sb("i_score", [P, 2, T])
        pl = [x.enter_context(nc.psum_tensor(f"i_logits{n}", [P, 512], F32)) for n in range(8)]
        k_loaded, parts, dot, relu, acc, freed, sc_free = map(sem, "ik_loaded parts_ready dots_done relu_done accumulated loads_free score_free".split())
        loaded, stored = ([sem(f"{n}_{u}") for u in range(2)] for n in ("iq_loaded", "score_stored"))
        with nc.Block() as block:
            @block.sync
            def _(sp):
                wi = g.w_in_2[0].rearrange("(k p) n -> p k n", p=P)
                for n in range(4):
                    sp.dma_start(ik[n * ID:(n + 1) * ID, :], g.ikT[:, :]).then_inc(k_loaded, 16)

                def load(i, u, uses, at, q):
                    sp.wait_ge(freed, i + 1)
                    for n in range(4):
                        sp.dma_start(iq[n * ID:(n + 1) * ID, u, :, :], g.iqT.rearrange("(h d) t -> d h t", d=ID)[:, :, bass.ds(i * P, P)]).then_inc(loaded[u], 16)
                    sp.dma_start(iw[:, u, :], g.iw[bass.ds(i * P, P), :]).then_inc(loaded[u], 16)
                    sp.dma_start(caus[:, u, :], g.c_causal[bass.ds(i - 4 * q, 1), :, :].rearrange("o p n -> p (o n)")).then_inc(loaded[u], 16)
                growing(sp, IH, load)
                sp.dma_start(g.w_late[:, :, 0:2048], wi[:, :, 0:2048]).then_inc(g.w_late_loaded, 16)
                sp.dma_start(g.w_late[:, :, 2048:NA], wi[:, :, W2["gb"]:W2["gb"] + 512]).then_inc(g.w_late_loaded, 16)

            @block.tensor
            def _(pe):
                pe.wait_ge(parts, 1)

                def body(i, u, uses, at, q):
                    pe.wait_ge(parts, i + 2)
                    for h in range(IH):
                        for c in range(q + 1):
                            n = h * (q + 1) + c
                            pe.wait_ge(relu, at + n + 1)
                            one_pass(nc, pl[n % 8][:, :], qs[:, u, h, :], ks[:, c * 512:(c + 1) * 512], start=True, stop=True).then_inc(dot, 1)
                growing(pe, IH, body)

            @block.scalar
            def _(act):
                def body(i, u, uses, at, q):
                    for n in range(IH * (q + 1)):
                        act.wait_ge(dot, at + n + 1)
                        act.wait_ge(acc, at + n + 1)
                        nc.scalar.activation(rel[:, n % 4, :], pl[n % 8][:, :], ACT.Relu).then_inc(relu, 1)
                growing(act, IH, body)

            @block.vector
            def _(v):
                v.sem_inc(freed, 2)
                v.sem_inc(relu, 8)
                v.sem_inc(acc, 4)
                v.sem_inc(sc_free, 2)

                V = nc.vector
                v.wait_ge(k_loaded, 64)
                head(V, ks[:], ik[:])
                v.drain()
                for n in (1, 3):
                    rest(V, ks[n * ID:(n + 1) * ID, :], ik[n * ID:(n + 1) * ID, :], ks[n * ID:(n + 1) * ID, :])
                v.drain().then_inc(parts, 1)

                def body(i, u, uses, at, q):
                    v.wait_ge(loaded[u], 96 * uses)
                    head(V, qs[:, u, :, :], iq[:, u, :, :])
                    v.drain()
                    rest(V, qs[64:P, u, :, :], iq[64:P, u, :, :], qs[64:P, u, :, :])
                    v.drain().then_inc(parts, 1)
                    v.wait_ge(sc_free, i + 1)
                    for h in range(IH):
                        for c in range(q + 1):
                            cols = sc[:, u, c * 512:(c + 1) * 512]
                            n = h * (q + 1) + c
                            v.wait_ge(relu, at + n + 9)
                            if h:
                                nc.vector.scalar_tensor_tensor(out=cols, in0=rel[:, n % 4, :], scalar=iw[:, u, h:h + 1], in1=cols,
                                                               op0=ALU.mult, op1=ALU.add).then_inc(acc, 1)
                            else:
                                nc.vector.tensor_scalar(cols, rel[:, n % 4, :], iw[:, u, h:h + 1], None, ALU.mult).then_inc(acc, 1)
                        v.drain()
                    nc.vector.tensor_tensor(cols, cols, caus[:, u, :], ALU.add)
                    v.drain().then_inc(freed, 1)
                growing(v, IH, body)

            @block.gpsimd
            def _(pool):
                def body(i, u, uses, at, q):
                    pool.wait_ge(freed, i + 3)
                    settle(g, pool)
                    n = 512 * (q + 1)
                    pool.dma_start(g.score[bass.ds(i * P, P), 0:n], sc[:, u, 0:n]).then_inc(stored[u], 16)
                    pool.wait_ge(stored[u], 16 * uses)
                    pool.sem_inc(sc_free, 1)
                growing(pool, IH, body)



def stage_select(nc, g):
    with ExitStack() as x:
        sb = lambda n, s, d=F32: x.enter_context(nc.sbuf_tensor(n, s, d))
        sem = x.enter_context(semaphores(nc, "select"))
        w = g.w_late
        xT = sb("s_xT", [P, 2, KD, P])
        out = sb("s_out", [P, 2, NA])
        bm = sb("s_bmerge", [P, 2 * KD])
        score = [sb(f"s_score{u}", [P, 4, 512 * (GROUPS - 1 + u)]) for u in range(2)]
        work = sb("s_work", [P, 2, T])
        tie, rank = work[:, 0, :], work[:, 1, :]
        bit = sb("s_bit", [P, 4], I32)
        least = sb("s_least", [P, 4], I32)
        trial = sb("s_trial", [P, 4], I32)
        enough = sb("s_enough", [P, 4], I32)
        count = sb("s_count", [P, 4])
        floor = sb("s_floor", [P, 4])
        bank = [x.enter_context(nc.psum_tensor(f"s_bank{n}", [P, 512], F32)) for n in range(8)]
        w1_loaded, w2_loaded, done, read, pen_ready, pen_stored, zeroed, zero_stored = map(
            sem, "w1_loaded w2_loaded group_done group_read penalty_ready penalty_stored zeroed zero_stored".split())
        sc_loaded, xT_loaded, stored = ([sem(f"{n}_{u}") for u in range(2)] for n in ("score_loaded", "xT_loaded", "stored"))
        wi = g.w_in_2[0].rearrange("(k p) n -> p k n", p=P)
        with nc.Block() as block:
            @block.sync
            def _(sp):
                sp.dma_start(bm[:], g.b_merge_2[0].rearrange("a (k p) -> p (a k)", p=P), allow_slow_non_contiguous=True).then_inc(w1_loaded, 16)

                def load(before, groups):
                    def body(i, u, uses, last):
                        sp.wait_ge(done, 10 + before + groups * (i - 1))
                        sp.dma_start(xT[:, u, :, :], g.xn3T.rearrange("(k p) t -> p k t", p=P)[:, :, bass.ds(i * P, P)]).then_inc(xT_loaded[u], 16)
                    return body
                pairs(sp, NB, load(0, 5))
                sp.wait_ge(done, 10 + 5 * NB)
                sp.dma_start(w[:, :, 0:2048], wi[:, :, W2["za"]:IN2]).then_inc(w2_loaded, 16)
                pairs(sp, NB, load(5 * NB, 4))

            @block.tensor
            def _(pe):
                pe.sem_inc(done, 10)
                pe.sem_inc(read, 5)
                pe.wait_ge(g.w_late_loaded, 32)
                pe.wait_ge(w1_loaded, 16)

                def body(i, u, uses, last):
                    pe.wait_ge(xT_loaded[u], 16 * uses)
                    for q in range(5):
                        pe.wait_ge(read, 5 * i + q + 1)
                        b = bank[q]
                        for c in range(4) if q != 2 else (None,):
                            for k in range(KD):
                                if c is not None:
                                    at = q * 512 + c * P
                                    mm = nc.tensor.matmul(b[:, c * P:(c + 1) * P], w[:, k, at:at + P], xT[:, u, k, :], start=(k == 0), stop=(k == KD - 1))
                                else:
                                    mm = nc.tensor.matmul(b[:, :], xT[:, u, k, :], w[:, k, q * 512:(q + 1) * 512], start=(k == 0), stop=(k == KD - 1))
                        mm.then_inc(done, 1)
                pairs(pe, NB, body)
                pe.wait_ge(w2_loaded, 16)
                pe.wait_ge(read, 5 * NB + 5)

                def body2(i, u, uses, last):
                    pe.wait_ge(xT_loaded[u], 16 * uses + 16 * NB // 2)
                    for q in range(4):
                        pe.wait_ge(read, 5 * NB + 4 * i + q + 2)
                        for c in range(4):
                            for k in range(KD):
                                at = (q * 4 + c) * P
                                mm = nc.tensor.matmul(bank[q][:, c * P:(c + 1) * P], w[:, k, at:at + P], xT[:, u, k, :], start=(k == 0), stop=(k == KD - 1))
                        mm.then_inc(done, 1)
                pairs(pe, NB, body2)

            @block.scalar
            def _(act):
                zeros = out[:, 0, :]
                act.wait_ge(zeroed, 1)
                act.dma_start(g.ka2T.rearrange("(c p) t -> p c t", p=P)[:, :, 0:LEFT * CW], zeros[:, 0:2048].rearrange("p (c t) -> p c t", c=4)).then_inc(zero_stored, 16)
                act.dma_start(g.va2[0:LEFT * CW, :].rearrange("(c p) n -> p c n", p=P), zeros[:, 0:2048].rearrange("p (c t) -> p c t", c=4)).then_inc(zero_stored, 16)
                act.wait_ge(zero_stored, 32)
                for u in range(2):
                    act.sem_inc(stored[u], 80)

                def body(i, u, uses, last):
                    act.wait_ge(stored[u], 80 * uses)
                    for q, (f, scale) in enumerate(((ACT.Copy, HD ** -0.5), (ACT.Copy, 1.0), (ACT.Copy, 1.0), (ACT.Silu, 1.0), (ACT.Silu, 1.0))):
                        act.wait_ge(done, 10 + 5 * i + q + 1)
                        nc.scalar.activation(out[:, u, q * 512:(q + 1) * 512], bank[q][:, :], f, scale=scale).then_inc(read, 1)
                    act.wait_ge(read, 5 * i + 10)
                    cut = lambda q: out[:, u, q * 512:(q + 1) * 512].rearrange("p (c t) -> p c t", c=4)
                    act.dma_start(g.qa2T.rearrange("(c p) t -> p c t", p=P)[:, :, bass.ds(i * P, P)], cut(0)).then_inc(stored[u], 16)
                    act.dma_start(g.ka2T.rearrange("(c p) t -> p c t", p=P)[:, :, bass.ds(i * P + LEFT * CW, P)], cut(1)).then_inc(stored[u], 16)
                    act.dma_start(g.va2[bass.ds(i * P + LEFT * CW, P), :], out[:, u, 1024:1536]).then_inc(stored[u], 16)
                    act.dma_start(g.sgaT.rearrange("(c p) t -> p c t", p=P)[:, :, bass.ds(i * P, P)], cut(3)).then_inc(stored[u], 16)
                    act.dma_start(g.sgbT.rearrange("(c p) t -> p c t", p=P)[:, :, bass.ds(i * P, P)], cut(4)).then_inc(stored[u], 16)
                pairs(act, NB, body)

                def body2(i, u, uses, last):
                    act.wait_ge(stored[u], 80 * (NB // 2 + 1) + 16 * (uses - 1))
                    for q in range(4):
                        act.wait_ge(done, 10 + 5 * NB + 4 * i + q + 1)
                        for c in range(4):
                            n = 4 * q + c
                            mm = nc.scalar.activation(out[:, u, n * P:(n + 1) * P], bank[q][:, c * P:(c + 1) * P], ACT.Sigmoid, bias=bm[:, n:n + 1])
                        mm.then_inc(read, 1)
                    act.wait_ge(read, 5 * NB + 5 + 4 * i + 4)
                    act.dma_start(g.gzT.rearrange("(c p) t -> p c t", p=P)[:, :, bass.ds(i * P, P)], out[:, u, 0:2048].rearrange("p (c t) -> p c t", c=16)).then_inc(stored[u], 16)
                pairs(act, NB, body2)
                for u in range(2):
                    act.wait_ge(stored[u], 80 * (NB // 2 + 1) + 16 * (NB // 2))

            @block.gpsimd
            def _(pool):
                def load(q):
                    n = 512 * (q + 1)
                    pool.dma_start(score[q % 2][:, :, 0:n], g.score[q * 512:(q + 1) * 512, 0:n].rearrange("(b p) n -> p b n", p=P)).then_inc(sc_loaded[q % 2], 16)
                load(0)
                load(1)
                for q in range(GROUPS):
                    n = 512 * (q + 1)
                    for b in range(4):
                        pool.wait_ge(pen_ready, 4 * q + b + 1)
                        pool.dma_start(g.pen[(4 * q + b) * P:(4 * q + b + 1) * P, 0:n], score[q % 2][:, b, 0:n]).then_inc(pen_stored, 16)
                    pool.wait_ge(pen_stored, 64 * (q + 1))
                    if q + 2 < GROUPS:
                        load(q + 2)

            @block.vector
            def _(v):
                V = nc.vector
                V.memset(out[:, 0, :], 0.0).then_inc(zeroed, 1)

                for q in range(GROUPS):
                    n = 512 * (q + 1)
                    s = score[q % 2]
                    v.wait_ge(sc_loaded[q % 2], 16 * (q // 2 + 1))

                    def count_from(at_least, op=ALU.is_ge):
                        for b in range(4):
                            unread = work[:, b // 2, :].bitcast(mybir.dt.bfloat16)[:, b % 2 * T:b % 2 * T + n]
                            V.tensor_scalar(unread, s[:, b, 0:n], at_least(b), None, op, ALU.add, accum_out=count[:, b:b + 1])
                        v.drain()

                    V.memset(bit[:], 1 << 30)
                    count_from(lambda b: 0.0)
                    V.tensor_scalar(least[:], count[:], float(TOPK), -1.0, ALU.is_lt, ALU.mult)
                    v.drain()
                    with v.Fori(0, 31):
                        V.tensor_tensor(trial[:], least[:], bit[:], ALU.bitwise_xor)
                        v.drain()
                        V.tensor_scalar(bit[:], bit[:], 1, None, ALU.logical_shift_right)
                        count_from(lambda b: trial[:, b:b + 1].bitcast(F32))
                        V.tensor_scalar(enough[:], count[:], float(TOPK), None, ALU.is_ge)
                        v.drain()
                        V.copy_predicated(least[:], enough[:], trial[:])
                        v.drain()
                    V.tensor_scalar(floor[:], least[:].bitcast(F32), 0.9 * NEG, None, ALU.max)
                    count_from(lambda b: least[:, b:b + 1].bitcast(F32), ALU.is_gt)
                    for b in range(4):
                        row = s[:, b, 0:n]
                        V.tensor_scalar(tie[:, 0:n], row, least[:, b:b + 1].bitcast(F32), None, ALU.is_equal)
                        v.drain()
                        V.tensor_tensor_scan(rank[:, 0:n], tie[:, 0:n], tie[:, 0:n], count[:, b:b + 1], ALU.add, ALU.bypass)
                        v.drain()
                        V.scalar_tensor_tensor(out=rank[:, 0:n], in0=rank[:, 0:n], scalar=float(TOPK), in1=tie[:, 0:n], op0=ALU.is_gt, op1=ALU.mult)
                        v.drain()
                        V.scalar_tensor_tensor(out=row, in0=row, scalar=floor[:, b:b + 1], in1=rank[:, 0:n], op0=ALU.is_lt, op1=ALU.max)
                        v.drain()
                        V.tensor_scalar(row, row, NEG, None, ALU.mult).then_inc(pen_ready, 1)


def stage_attend(nc, g, banded):
    name = "banded" if banded else "sparse"
    NH = 8
    KW = BAND if banded else T
    KT = LEFT * CW + T if banded else T
    CUTS = 4 if banded else 2
    PIECE = KT // CUTS
    with ExitStack() as x:
        sb = lambda n, s, d=F32: x.enter_context(nc.sbuf_tensor(f"{name}_{n}", s, d))
        sem = x.enter_context(semaphores(nc, name))
        q = sb("q", [P, 2, NH, P])
        q_parts = [sb(f"q_{part}", [P, 2, NH, P]) for part in ("head", "rest")]
        raw = sb("k_raw", [P, CUTS, PIECE])
        kk = sb("k", [P, NH if banded else 1, KT])
        if banded:
            flags = sb("flags", [1, 2 * 512])
            minus = sb("minus", [1, P])
            flags_raw = sb("flags_raw", [1, 2 * 512])
            neg = sb("neg", [1, P])
            vv = sb("v", [P, 2, KW // P, NH * HD])
            bias = sb("bias", [P, NH, KW])
            band = sb("band", [P, KW])
            ext = sb("ext", [NH, BAND + P])
            rev = sb("rev", [NH, 2 * CLIP + 1])
        else:
            vv = sb("v", [P, T // P, HD])
            bias = sb("pen", [P, 2, T])
        gate = sb("gate", [P, 2, 4, P])
        S = sb("scores", [P, 2, KW])
        Pb = sb("probs", [P, 2, KW])
        PT = sb("probsT", [P, 2, 512])
        mx = sb("max", [P, 2, 8])
        L = sb("sums", [P, 2, NH])
        y = sb("gated", [P, 2, 4, P])
        bs = [x.enter_context(nc.psum_tensor(f"{name}_s{n}", [P, 512], F32)) for n in range(4)]
        bt = [x.enter_context(nc.psum_tensor(f"{name}_t{n}", [P, 512], F32)) for n in range(2)]
        bo = x.enter_context(nc.psum_tensor(f"{name}_o", [P, 512], F32))
        const, qk, s_read, m_ready, p_ready, tp, pt_read, pv, scaled, y_ready, freed, bias_ready, ext_stored, rows_stored, flag = map(
            sem, "consts_loaded qk_done scores_read max_ready probs_ready probsT_done probsT_read pv_done probs_scaled gated loads_free bias_ready table_stored rows_stored flag_ready".split())
        loaded, stored = ([sem(f"{n}_{u}") for u in range(2)] for n in ("loaded", "stored"))
        q_loaded = [sem(f"q_loaded_{u}") for u in range(2)]
        raw_loaded = [sem(f"raw_loaded_{u}") for u in range(CUTS)]
        q_ready, k_head, k_ready, raw_free = map(sem, "q_parts_ready k_heads_ready k_parts_ready raw_free".split())
        LOADS = 3 if banded else 2
        PIECES = CUTS * (NH if banded else 1)
        yT = g.yaT if banded else g.ybT

        def bank(h, c):
            return 2 * (h % 2) + c if banded else c

        def blocks(eng, body):
            if banded:
                for first, end, early in ((0, 2, True), (2, NB // 2, False)):
                    with eng.Fori(first, end) as j:
                        for u in range(2):
                            body(2 * j + u, u, j + 1, (2 * j + u) * NH * 2, [512, P], early)
            else:
                growing(eng, NH, lambda i, u, uses, at, grp: body(i, u, uses, at, [512] * (grp + 1), False))

        with nc.Block() as block:
            @block.sync
            def _(sp):
                src = g.ka2T if banded else g.kbT
                if not banded:
                    sp.dma_start(vv[:], g.vb.rearrange("(c p) n -> p c n", p=P)).then_inc(const, 16)

                for n in range(PIECES):
                    sp.wait_ge(raw_free, n + 1)
                    for part in range(2):
                        sp.dma_start(raw[part * HD:(part + 1) * HD, n % CUTS, :],
                                     src[(n // CUTS) * HD:(n // CUTS + 1) * HD, (n % CUTS) * PIECE:(n % CUTS + 1) * PIECE]).then_inc(raw_loaded[n % CUTS], 16)

                def load(i, u, uses, at, widths, early):
                    sp.wait_ge(freed, i + 1)
                    n = sum(widths)
                    src = g.qa2T if banded else g.qbT
                    for part in range(2):
                        sp.dma_start(q[part * HD:(part + 1) * HD, u, :, :], src.rearrange("(h d) t -> d h t", d=HD)[:, :, bass.ds(i * P, P)]).then_inc(q_loaded[u], 16)
                    sp.dma_start(gate[:, u, :, :], (g.sgaT if banded else g.sgbT).rearrange("(c p) t -> p c t", p=P)[:, :, bass.ds(i * P, P)]).then_inc(loaded[u], 16)
                    if banded:
                        for c in range(2):
                            sp.dma_start(vv[:, u, 0:4, :] if c == 0 else vv[:, u, 4:5, :],
                                         g.va2[bass.ds(i * P + 512 * c, 512 if c == 0 else P), :].rearrange("(c p) n -> p c n", p=P)).then_inc(loaded[u], 16)
                    else:
                        sp.dma_start(bias[:, u, 0:n], g.pen[bass.ds(i * P, P), 0:n]).then_inc(loaded[u], 16)
                blocks(sp, load)
                if not banded:
                    for n, w in enumerate((g.w_branch_a_2, g.w_branch_b_2)):
                        sp.dma_start(g.w_branches[:, n, :, :], w[0].rearrange("(k p) n -> p k n", p=P)).then_inc(g.w_out_loaded, 16)
                    sp.dma_start(g.w_last[:], g.w_out_2[0].rearrange("(k p) n -> p k n", p=P)).then_inc(g.w_out_loaded, 16)

            @block.gpsimd
            def _(pool):
                if banded:
                    nc.gpsimd.memset(neg[:], NEG)
                    pool.wait_ge(const, 48)
                    pool.drain()
                    head(nc.gpsimd, minus[:], neg[:])
                    head(nc.gpsimd, flags[:], flags_raw[:]).then_inc(flag, 1)

                def split(i, u, uses, at, widths, early):
                    pool.wait_ge(q_loaded[u], 32 * uses)
                    pool.wait_ge(freed, i + 1)
                    settle(g, pool)
                    head(nc.gpsimd, q_parts[0][:, u, :, :], q[:, u, :, :])
                    pool.drain()
                    rest(nc.gpsimd, q_parts[1][:, u, :, :], q[:, u, :, :], q_parts[0][:, u, :, :]).then_inc(q_ready, 1)
                blocks(pool, split)

            @block.tensor
            def _(pe):
                pe.wait_ge(const, 64 if banded else 16)
                pe.wait_ge(k_ready, 1)
                if banded:
                    pe.wait_ge(flag, 1)

                def body(i, u, uses, at, widths, early):
                    nch = len(widths)
                    pe.wait_ge(loaded[u], 16 * LOADS * uses)
                    pe.wait_ge(q_ready, i + 1)

                    def scores(h):
                        for c, w in enumerate(widths):
                            pe.wait_ge(s_read, at + (h - 1 if banded else h) * nch + 4)
                            keys = kk[:, h, bass.ds(i * P + c * 512, w)] if banded else kk[:, 0, c * 512:c * 512 + w]
                            flagged = early and c == 0
                            one_pass(nc, bs[bank(h, c)][:, 0:w], q_parts[0][:, u, h, :], keys, start=True, stop=False)
                            mm = one_pass(nc, bs[bank(h, c)][:, 0:w], q_parts[1][:, u, h, :], keys, start=False, stop=not flagged)
                            if flagged:
                                mm = one_pass(nc, bs[bank(h, c)][:, 0:w], minus[:, :], flags[:, bass.ds(i * P, w)], start=False, stop=True)
                            mm.then_inc(qk, 1)

                    def turn(h, c):
                        n = h * nch + c
                        if c == 0:
                            pe.wait_ge(scaled, NH * i + h + 1)
                        pe.wait_ge(pt_read, at + n + 1)
                        for k in range(widths[c] // P):
                            mm = nc.tensor.transpose(bt[n % 2][:, k * P:(k + 1) * P], Pb[:, h % 2, c * 512 + k * P:c * 512 + (k + 1) * P], g.square[:, C_ID, :])
                        mm.then_inc(tp, 1)

                    def values(h, c):
                        n = h * nch + c
                        pe.wait_ge(pt_read, at + n + 3)
                        if h == 0 and c == 0:
                            pe.wait_ge(y_ready, i + 1)
                        for k in range(widths[c] // P):
                            val = vv[:, u, 4 * c + k, h * HD:(h + 1) * HD] if banded else vv[:, 4 * c + k, :]
                            mm = nc.tensor.matmul(bo[h % 2 * HD:(h % 2 + 1) * HD, h // 2 * P:(h // 2 + 1) * P], val, PT[:, n % 2, k * P:(k + 1) * P],
                                                  start=(c == 0 and k == 0), stop=(c == nch - 1 and k == widths[c] // P - 1), tile_position=(0, h % 2 * HD))
                        mm.then_inc(pv, 1)
                    scores(0)
                    scores(1)
                    for h in range(NH):
                        if h + 2 < NH:
                            scores(h + 2)
                        turn(h, 0)
                        for c in range(1, nch):
                            turn(h, c)
                            values(h, c - 1)
                        values(h, nch - 1)
                blocks(pe, body)

            @block.scalar
            def _(act):
                if banded:
                    act.dma_start(rev[:], g.rel_rev[0]).then_inc(const, 16)
                    act.dma_start(flags_raw[:], g.c_padflag[:, 0:1024]).then_inc(const, 16)
                    act.dma_start(band[:], g.c_band[:, :]).then_inc(const, 16)
                    act.wait_ge(bias_ready, 1)
                    act.dma_start(g.rel_ext[:, :], ext[:]).then_inc(ext_stored, 16)
                    act.wait_ge(ext_stored, 16)
                    every_query = bass.AP(tensor=g.rel_ext.tensor, offset=0, ap=[[0, P], [BAND + P, NH], [1, BAND + P]])
                    act.dma_start(g.rel_rows[:, :, :], every_query).then_inc(rows_stored, 16)
                    act.wait_ge(rows_stored, 16)
                    toeplitz = bass.AP(tensor=g.rel_rows.tensor, offset=P - 1, ap=[[NH * (BAND + P) - 1, P], [BAND + P, NH], [1, BAND]])
                    act.dma_start(bias[:], toeplitz).then_inc(const, 16)
                for n in range(PIECES):
                    act.wait_ge(raw_loaded[n % CUTS], 32 * (n // CUTS + 1))
                    nc.scalar.activation(kk[:, n // CUTS, (n % CUTS) * PIECE:(n % CUTS + 1) * PIECE].bitcast(F32R), raw[:, n % CUTS, :], ACT.Copy).then_inc(k_head, 1)
                act.sem_inc(pt_read, 2)
                act.sem_inc(p_ready, 2)
                act.sem_inc(s_read, 4)
                for u in range(2):
                    act.sem_inc(stored[u], 16)

                def body(i, u, uses, at, widths, early):
                    nch, n_keys = len(widths), sum(widths)

                    def probs(h):
                        act.wait_ge(m_ready, NH * i + h + 1)
                        act.wait_ge(tp, at + (h - 1) * nch + 8)
                        nc.scalar.activation(Pb[:, h % 2, 0:n_keys], S[:, h % 2, 0:n_keys], ACT.Exp, bias=mx[:, h % 2, 7:8],
                                             accum_out=L[:, u, h:h + 1]).then_inc(p_ready, 1)
                    probs(0)
                    for h in range(NH):
                        if h + 1 < NH:
                            probs(h + 1)
                        for c, w in enumerate(widths):
                            n = h * nch + c
                            act.wait_ge(tp, at + n + 9)
                            act.wait_ge(pv, at + n + 1)
                            nc.scalar.activation(PT[:, n % 2, 0:w], bt[n % 2][:, 0:w], ACT.Copy).then_inc(pt_read, 1)
                    act.wait_ge(y_ready, i + 2)
                    act.dma_start(yT.rearrange("(c p) t -> p c t", p=P)[:, :, bass.ds(i * P, P)], y[:, u, :, :]).then_inc(stored[u], 16)
                blocks(act, body)
                for u in range(2):
                    act.wait_ge(stored[u], 16 * (NB // 2 + 1))

            @block.vector
            def _(v):
                V = nc.vector
                v.sem_inc(freed, 2)
                v.sem_inc(y_ready, 1)
                v.sem_inc(tp, 8)
                v.sem_inc(pv, 2)
                v.sem_inc(raw_free, CUTS)
                if banded:
                    v.wait_ge(const, 48)
                    V.tensor_copy(ext[:, 0:BAND - CLIP], rev[:, 0:1].to_broadcast([NH, BAND - CLIP]))
                    V.tensor_copy(ext[:, BAND - CLIP:BAND - CLIP + CLIP + P - 1 + 1], rev[:, 1:CLIP + P + 1]).then_inc(bias_ready, 1)
                for n in range(PIECES):
                    piece = kk[:, n // CUTS, (n % CUTS) * PIECE:(n % CUTS + 1) * PIECE]
                    v.wait_ge(k_head, n + 1)
                    rest(V, piece[HD:P, :], raw[HD:P, n % CUTS, :], piece[HD:P, :]).then_inc(raw_free, 1)
                v.drain().then_inc(k_ready, 1)
                if banded:
                    v.wait_ge(const, 64)
                    V.tensor_tensor(bias[:], bias[:], band[:].unsqueeze(1).to_broadcast([P, NH, KW]), ALU.add)
                    v.drain()

                def body(i, u, uses, at, widths, early):
                    nch = len(widths)
                    v.wait_ge(loaded[u], 16 * LOADS * uses)
                    n_keys = sum(widths)

                    def rowmax(h):
                        v.wait_ge(p_ready, NH * i + h + 1)
                        for c, w in enumerate(widths):
                            v.wait_ge(qk, at + h * nch + c + 1)
                            settle(g, v)
                            add = bias[:, h, c * 512:c * 512 + w] if banded else bias[:, u, c * 512:c * 512 + w]
                            V.tensor_tensor_reduce(S[:, h % 2, c * 512:c * 512 + w], bs[bank(h, c)][:, 0:w], add, 1.0, GONE, ALU.add, ALU.max,
                                                   mx[:, h % 2, c:c + 1]).then_inc(s_read, 1)
                        v.drain()
                        V.tensor_reduce(mx[:, h % 2, 7:8], mx[:, h % 2, 0:nch], AX.X, ALU.max, negate=True).then_inc(m_ready, 1)

                    def scale(h):
                        v.wait_ge(p_ready, NH * i + h + 3)
                        V.reciprocal(L[:, u, h:h + 1], L[:, u, h:h + 1])
                        v.drain()
                        V.tensor_scalar(Pb[:, h % 2, 0:n_keys], Pb[:, h % 2, 0:n_keys], L[:, u, h:h + 1], None, ALU.mult).then_inc(scaled, 1)
                    rowmax(0)
                    for h in range(1, NH):
                        rowmax(h)
                        scale(h - 1)
                    scale(NH - 1)
                    v.wait_ge(stored[u], 16 * uses)
                    v.wait_ge(pv, at + NH * nch + 2)
                    V.tensor_tensor(y[:, u, :, :], bo[:, :].rearrange("p (c t) -> p c t", c=4), gate[:, u, :, :], ALU.mult).then_inc(y_ready, 1)
                    v.drain().then_inc(freed, 1)
                blocks(v, body)


def stage_output(nc, g):
    with ExitStack() as x:
        sb = lambda n, s, d=F32: x.enter_context(nc.sbuf_tensor(n, s, d))
        sem = x.enter_context(semaphores(nc, "output"))
        wab, wo = g.w_branches, g.w_last
        fg = sb("o_gain", [P, D])
        y = sb("o_y", [P, 2, 2, 4, P])
        gz = sb("o_gates", [P, 2, 2 * KD, P])
        xb = sb("o_x", [P, 2, D])
        mer = sb("o_merged", [P, 2, 2, KD, P])
        r = sb("o_res", [P, 2, D])
        junk = sb("o_junk", [P, D])
        sm = sb("o_small", [P, 4])
        half = sb("o_half", [P, 1])
        pb = [x.enter_context(nc.psum_tensor(f"o_branch{n}", [P, 512], F32)) for n in range(4)]
        po = [x.enter_context(nc.psum_tensor(f"o_out{n}", [P, 512], F32)) for n in range(2)]
        w_loaded, half_ready, br, br_read, merged, out_done, out_read, res, ssq, msq, rs, freed, front_free = map(
            sem, "w_loaded half_ready branch_done branch_read merged out_done out_read residual sum_squares mean_square rs_ready loads_free front_free".split())
        loaded, x_loaded, stored = ([sem(f"{n}_{u}") for u in range(2)] for n in ("loaded", "x_loaded", "stored"))
        with nc.Block() as block:
            @block.sync
            def _(sp):
                sp.dma_start(fg[:], g.final_norm_gain_2.rearrange("(o n) -> o n", o=1).to_broadcast([P, D])).then_inc(w_loaded, 16)

                def load(i, u, uses, last):
                    sp.wait_ge(front_free, i + 1)
                    cols = bass.ds(i * P, P)
                    for n, src in enumerate((g.yaT, g.ybT)):
                        sp.dma_start(y[:, u, n, :, :], src.rearrange("(k p) t -> p k t", p=P)[:, :, cols]).then_inc(loaded[u], 16)
                    sp.dma_start(gz[:, u, :, :], g.gzT.rearrange("(k p) t -> p k t", p=P)[:, :, cols]).then_inc(loaded[u], 16)
                    sp.wait_ge(freed, i + 1)
                    sp.dma_start(xb[:, u, :], g.x2[cols, :]).then_inc(x_loaded[u], 16)
                pairs(sp, NB, load)

            @block.gpsimd
            def _(pool):
                nc.gpsimd.memset(half[:], -0.5).then_inc(half_ready, 1)
                pool.wait_ge(half_ready, 1)

                def step(f, t):
                    if t:
                        i, u, uses = t
                        pool.wait_ge(msq, i + 1)
                        nc.gpsimd.tensor_tensor(sm[:, 2:3], sm[:, 1:2], half[:], ALU.pow).then_inc(rs, 1)
                    if f:
                        i, u, uses = f
                        pool.wait_ge(br_read, 4 * i + 8)
                        nc.gpsimd.tensor_tensor(mer[:, u, 0, :, :], mer[:, u, 0, :, :], mer[:, u, 1, :, :], ALU.add).then_inc(merged, 1)
                overlapped(pool, NB, step)

            @block.tensor
            def _(pe):
                pe.sem_inc(br_read, 4)
                pe.sem_inc(out_read, 2)
                pe.wait_ge(g.w_out_loaded, 48)

                def branches(i, u, uses):
                    pe.wait_ge(loaded[u], 48 * uses)
                    for n in range(2):
                        for m in range(2):
                            pe.wait_ge(br_read, 4 * i + 2 * n + m + 1)
                            for c in range(4):
                                for k in range(4):
                                    at = (4 * m + c) * P
                                    mm = nc.tensor.matmul(pb[2 * n + m][:, c * P:(c + 1) * P], wab[:, n, k, at:at + P], y[:, u, n, k, :], start=(k == 0), stop=(k == 3))
                            mm.then_inc(br, 1)

                def step(f, t):
                    if f:
                        branches(*f)
                    if t:
                        i, u, uses = t
                        pe.wait_ge(merged, i + 1)
                        for n in range(2):
                            pe.wait_ge(out_read, 2 * i + n + 1)
                            for k in range(KD):
                                mm = nc.tensor.matmul(po[n][:, :], mer[:, u, 0, k, :], wo[:, k, n * 512:(n + 1) * 512], start=(k == 0), stop=(k == KD - 1))
                            mm.then_inc(out_done, 1)
                overlapped(pe, NB, step)

            @block.scalar
            def _(act):
                for u in range(2):
                    act.sem_inc(stored[u], 16)

                def step(f, t):
                    if t:
                        i, u, uses = t
                        act.wait_ge(res, 3 * i + 2)
                        nc.scalar.activation(junk[:], r[:, u, :], ACT.Square, accum_out=sm[:, 0:1]).then_inc(ssq, 1)
                        act.wait_ge(res, 3 * i + 3)
                        act.dma_start(g.out[0, bass.ds(i * P, P), :], r[:, u, :]).then_inc(stored[u], 16)
                overlapped(act, NB, step)
                for u in range(2):
                    act.wait_ge(stored[u], 16 * (NB // 2 + 1))

            @block.vector
            def _(v):
                V = nc.vector
                v.sem_inc(freed, 2)
                v.sem_inc(front_free, 2)
                v.wait_ge(w_loaded, 16)

                def step(f, t):
                    if f:
                        i, u, uses = f
                        for n in range(2):
                            for m in range(2):
                                v.wait_ge(br, 4 * i + 2 * n + m + 1)
                                ks = slice(4 * m, 4 * m + 4)
                                V.tensor_tensor(mer[:, u, n, ks, :], pb[2 * n + m][:, :].rearrange("p (k t) -> p k t", k=4),
                                                gz[:, u, KD * n + 4 * m:KD * n + 4 * m + 4, :], ALU.mult).then_inc(br_read, 1)
                        v.drain().then_inc(front_free, 1)
                    if t:
                        i, u, uses = t
                        v.wait_ge(stored[u], 16 * uses)
                        v.wait_ge(x_loaded[u], 16 * uses)
                        for n in range(2):
                            v.wait_ge(out_done, 2 * i + n + 1)
                            V.tensor_tensor(r[:, u, n * 512:(n + 1) * 512], po[n][:, :], xb[:, u, n * 512:(n + 1) * 512], ALU.add).then_inc(out_read, 1)
                        v.drain().then_inc(freed, 1)
                        v.sem_inc(res, 2)
                        v.wait_ge(ssq, i + 1)
                        V.tensor_scalar(sm[:, 1:2], sm[:, 0:1], 1.0 / D, EPS, ALU.mult, ALU.add).then_inc(msq, 1)
                        v.wait_ge(rs, i + 1)
                        V.scalar_tensor_tensor(out=r[:, u, :], in0=r[:, u, :], scalar=sm[:, 2:3], in1=fg[:], op0=ALU.mult, op1=ALU.mult).then_inc(res, 1)
                overlapped(v, NB, step)




_INS = ["x", "c", "ln1_pre", "ln1_post", "ln2_pre", "ln2_post", "w_ada", "b_ada", "w_in", "attn_sinks", "attn_out_norm",
        "hgrn_lb", "hgrn_out_norm", "w_out", "w_router_group", "b_router_group", "w_router_expert", "b_router_expert",
        "w_exp_gate", "w_exp_up", "w_exp_down", "norm_gain_2", "w_in_2", "b_merge_2", "rel_bias_2", "w_branch_a_2",
        "w_branch_b_2", "w_out_2", "final_norm_gain_2"]
_SCRATCH = dict(qaT=(AW, T), kaT=(KVW, P + T), va=(P + T, KVW), hg5=(T, 5, HW_), x1=(T, D), xn2=(T, D), ids=((NT * P, 1), I32), ys=(NT * P, D), x2=(T, D), xn3T=(D, T), qbT=(BH * HD, T), kbT=(HD, T),
                iqT=(IH * ID, T), ikT=(ID, T), vb=(T, HD), iw=(T, IH), score=(T, T), pen=(T, T),
                qa2T=(512, T), ka2T=(512, LEFT * CW + T), va2=(LEFT * CW + T, 512), sgaT=(512, T), sgbT=(512, T), gzT=(2 * D, T), rel_ext=(8, BAND + P), rel_rows=(P, 8, BAND + P), yaT=(512, T), ybT=(512, T))



def build(nc, g):
    with ExitStack() as x:
        sb = lambda n, s, d=F32: x.enter_context(nc.sbuf_tensor(n, s, d))
        g.square = sb("square", [P, 6, P])
        g.scale = sb("norm_scale", [P, 2, KD])
        g.shift = sb("norm_shift", [P, 2, KD])
        g.gate = sb("gate_rows", [P, 2, D])
        g.tick = x.enter_context(nc.semaphore("tick"))
        g.win1_loaded = x.enter_context(nc.semaphore("win1_loaded"))
        with nc.sbuf_tensor("win1", [P, KD, IN1], F32) as g.win1:
            stage_modulation(nc, g)
            stage_project1(nc, g)
        g.logits = sb("logits", [P, NB, NG + NE])
        g.route = sb("route", [P, NB, 4], I32)
        g.tile_expert = sb("tile_expert", [P, NT], I32)
        stage_mix(nc, g)
        stage_route(nc, g)
        stage_experts(nc, g)
        stage_combine(nc, g)
        g.w_late_loaded = x.enter_context(nc.semaphore("w_late_loaded"))
        with nc.sbuf_tensor("w_late", [P, KD, NA], F32) as g.w_late:
            stage_index_scores(nc, g)
            stage_select(nc, g)
        stage_attend(nc, g, True)
        g.w_out_loaded = x.enter_context(nc.semaphore("w_out_loaded"))
        g.w_branches = sb("w_branches", [P, 2, 4, D])
        g.w_last = sb("w_last", [P, KD, D])
        stage_attend(nc, g, False)
        stage_output(nc, g)


def kernel(**inputs):
    import concourse.bacc as _bacc
    from concourse.bass_utils import run_bass_kernel_spmd as _run

    nc = _bacc.Bacc("TRN2", target_bir_lowering=False, num_devices=1)
    g = Net()
    arrays = {}
    given = {name: inputs[name] for name in _INS if name != "rel_bias_2"}
    given["rel_rev"] = np.asarray(inputs["rel_bias_2"])[:, :, ::-1]
    given.update(shape_constants())
    for name, a in given.items():
        a = np.ascontiguousarray(a)
        arrays[f"in_{name}"] = a
        g.__dict__[name] = nc.dram_tensor(f"in_{name}", a.shape, mybir.dt.from_np(a.dtype), kind="ExternalInput").ap()
    for name, shape in _SCRATCH.items():
        shape, dtype = shape if isinstance(shape[0], tuple) else (shape, F32)
        g.__dict__[name] = nc.dram_tensor(f"mid_{name}", shape, dtype, kind="Internal").ap()
    g.out = nc.dram_tensor("out_0_dram", (1, T, D), F32, kind="ExternalOutput").ap()
    build(nc, g)
    r = _run(nc, [arrays], core_ids=[0])
    return r.results[0]["out_0_dram"]
```
